# Optimizing a Trainium2 kernel written in Bass

```python
import numpy as np
import jax, jax.numpy as jnp
from jax import lax
import math

D_MODEL = 1024
BATCH = 1
SEQ = 512
DEPTH = 2

N_A_LAYERS = DEPTH // 2
N_B_LAYERS = DEPTH - N_A_LAYERS
EPS = 1e-6
NEG_INF = -1e30
ROPE_THETA = 10000.0

GLA_HEADS = 4
GLA_DK = D_MODEL // (2 * GLA_HEADS)
GLA_DV = D_MODEL // GLA_HEADS
GLA_GATE_RANK = 16
GLA_TAU = 16.0
GLA_CHUNK = 64
GLA_IN = 2 * GLA_HEADS * GLA_DK + 2 * GLA_HEADS * GLA_DV + GLA_GATE_RANK

NSA_HEADS = 16
NSA_KV_HEADS = 4
NSA_GROUP = NSA_HEADS // NSA_KV_HEADS
NSA_HEAD_DIM = D_MODEL // NSA_HEADS
CMP_BLOCK = 32
CMP_STRIDE = 16
CMP_HIDDEN = 4 * NSA_HEAD_DIM
SEL_BLOCK = 64
SEL_TOPK = 16
WINDOW = 512
NSA_QCHUNK = 32
NSA_IN = NSA_HEADS * NSA_HEAD_DIM + 3 * NSA_HEADS
NSA_KV_OUT = 6 * NSA_KV_HEADS * NSA_HEAD_DIM
FORCE_SCORE = 1e4

FFN_DIM = 2816
CONV_WIDTH = 3


def rmsnorm(x, g):
    x32 = x.astype(jnp.float32)
    y = x32 * lax.rsqrt(jnp.mean(x32 * x32, axis=-1, keepdims=True) + EPS)
    return (y * g).astype(x.dtype)

def rope(x, pos):
    half = x.shape[-1] // 2
    inv = ROPE_THETA ** (-jnp.arange(half, dtype=jnp.float32) / half)
    ang = pos.astype(jnp.float32)[:, None] * inv[None, :]
    cos, sin = jnp.cos(ang), jnp.sin(ang)
    x1 = x[..., :half].astype(jnp.float32)
    x2 = x[..., half:].astype(jnp.float32)
    return jnp.concatenate([x1 * cos - x2 * sin, x1 * sin + x2 * cos], axis=-1).astype(x.dtype)

def masked_softmax(s, mask):
    s = jnp.where(mask, s.astype(jnp.float32), NEG_INF)
    return jnp.where(mask, jax.nn.softmax(s, axis=-1), 0.0)

def conv_ffn(h, w_up, conv_w, conv_b, w_down):
    S = h.shape[1]
    u = h @ w_up
    up = jnp.pad(u, ((0, 0), (CONV_WIDTH - 1, 0), (0, 0)))
    u = conv_b + up[:, 0:S] * conv_w[0]
    for j in range(1, CONV_WIDTH):
        u = u + up[:, j:j + S] * conv_w[j]
    gate, val = jnp.split(u, 2, axis=-1)
    return (jax.nn.silu(gate) * val) @ w_down

def gla_mixer(h, w_in, w_alpha_up, b_alpha, g_out, w_o):
    Bsz, S, _ = h.shape
    H, DK, DV, C = GLA_HEADS, GLA_DK, GLA_DV, GLA_CHUNK
    NC = S // C
    proj = h @ w_in
    splits = [H * DK, 2 * H * DK, 2 * H * DK + H * DV, 2 * H * DK + 2 * H * DV]
    q, k, v, r, a_low = jnp.split(proj, splits, axis=-1)
    log_a = jax.nn.log_sigmoid((a_low @ w_alpha_up + b_alpha).astype(jnp.float32)) / GLA_TAU

    def to_chunks(t, d):
        return t.astype(jnp.float32).reshape(Bsz, NC, C, H, d).transpose(1, 0, 3, 2, 4)

    qc = to_chunks(q, DK) * DK ** -0.5
    kc = to_chunks(k, DK)
    vc = to_chunks(v, DV)
    gc = to_chunks(log_a, DK)
    causal = jnp.tril(jnp.ones((C, C), dtype=bool))[:, :, None]

    def step(state, inp):
        q_, k_, v_, g_ = inp
        b = jnp.cumsum(g_, axis=2)
        o_inter = jnp.einsum('bhtk,bhkv->bhtv', q_ * jnp.exp(b), state)
        diff = b[:, :, :, None, :] - b[:, :, None, :, :]
        decay = jnp.where(causal, jnp.exp(jnp.minimum(diff, 0.0)), 0.0)
        att = jnp.einsum('bhtk,bhsk,bhtsk->bhts', q_, k_, decay)
        o_intra = jnp.einsum('bhts,bhsv->bhtv', att, v_)
        b_last = b[:, :, -1:, :]
        new_state = state * jnp.exp(b_last[:, :, 0, :, None]) + jnp.einsum(
            'bhsk,bhsv->bhkv', k_ * jnp.exp(b_last - b), v_)
        return new_state, o_inter + o_intra

    state0 = jnp.zeros((Bsz, H, DK, DV), jnp.float32)
    _, o = lax.scan(step, state0, (qc, kc, vc, gc))
    o = o.transpose(1, 0, 3, 2, 4).reshape(Bsz, S, H, DV)
    o = o * lax.rsqrt(jnp.mean(o * o, axis=-1, keepdims=True) + EPS) * g_out
    o = o.reshape(Bsz, S, H * DV).astype(h.dtype) * jax.nn.silu(r)
    return o @ w_o

def compress_blocks(t_raw, pe, w1, w2):
    Bsz, Hk, S, Dh = t_raw.shape
    n_cmp = (S - CMP_BLOCK) // CMP_STRIDE + 1
    idx = np.arange(n_cmp)[:, None] * CMP_STRIDE + np.arange(CMP_BLOCK)[None, :]
    blocks = (t_raw[:, :, idx, :] + pe).reshape(Bsz, Hk, n_cmp, CMP_BLOCK * Dh)
    return jax.nn.gelu(blocks @ w1) @ w2

def cmp_to_sel_weights(S):
    n_cmp = (S - CMP_BLOCK) // CMP_STRIDE + 1
    n_sel = S // SEL_BLOCK
    c0 = np.arange(n_cmp)[:, None] * CMP_STRIDE
    s0 = np.arange(n_sel)[None, :] * SEL_BLOCK
    ov = np.clip(np.minimum(c0 + CMP_BLOCK, s0 + SEL_BLOCK) - np.maximum(c0, s0), 0, None)
    return (ov / CMP_BLOCK).astype(np.float32)

def nsa_shared_kv(x, g_kv, w_kv, pe_k, pe_v, wk1, wk2, wv1, wv2):
    Bsz, S, _ = x.shape
    hn = rmsnorm(x, g_kv)
    kv = (hn @ w_kv).reshape(Bsz, S, 6, NSA_KV_HEADS, NSA_HEAD_DIM).transpose(2, 0, 3, 1, 4)
    pos = jnp.arange(S)
    k_cmp = compress_blocks(kv[0], pe_k, wk1, wk2)
    v_cmp = compress_blocks(kv[1], pe_v, wv1, wv2)
    k_sel = rope(kv[2], pos)
    k_win = rope(kv[4], pos)
    return k_cmp, v_cmp, k_sel, kv[3], k_win, kv[5]

gather_blocks = jax.vmap(jax.vmap(lambda blocks, ix: blocks[ix]))

def nsa_mixer(h, w_in, w_o, k_cmp, v_cmp, k_sel, v_sel, k_win, v_win):
    Bsz, S, _ = h.shape
    Hk, G, Dh, SB, QC = NSA_KV_HEADS, NSA_GROUP, NSA_HEAD_DIM, SEL_BLOCK, NSA_QCHUNK
    n_cmp = k_cmp.shape[2]
    n_sel = S // SB
    top = min(SEL_TOPK, n_sel)
    scale = Dh ** -0.5
    pos = jnp.arange(S)
    proj = h @ w_in
    q = proj[..., :NSA_HEADS * Dh].reshape(Bsz, S, Hk, G, Dh).transpose(0, 2, 3, 1, 4)
    gates = jax.nn.sigmoid(proj[..., NSA_HEADS * Dh:].astype(jnp.float32))
    gates = gates.reshape(Bsz, S, 3, Hk, G).transpose(2, 0, 3, 4, 1)[..., None]

    cmp_end = jnp.arange(n_cmp) * CMP_STRIDE + CMP_BLOCK - 1
    p_cmp = masked_softmax(jnp.einsum('bkgsd,bknd->bkgsn', q, k_cmp) * scale,
                           cmp_end[None, :] <= pos[:, None])
    o_cmp = jnp.einsum('bkgsn,bknd->bkgsd', p_cmp, v_cmp)

    imp = jnp.einsum('bkgsn,nj->bksj', p_cmp, jnp.asarray(cmp_to_sel_weights(S)))
    blk = jnp.arange(n_sel)[None, :]
    cur = (pos // SB)[:, None]
    forced = (blk == 0) | (blk == cur) | (blk == cur - 1)
    imp = jnp.where(blk > cur, -1.0, jnp.where(forced, FORCE_SCORE, imp))
    _, sel_idx = lax.top_k(imp, top)

    q_rot = rope(q, pos)
    k_blocks = k_sel.reshape(Bsz, Hk, n_sel, SB, Dh)
    v_blocks = v_sel.reshape(Bsz, Hk, n_sel, SB, Dh)
    pad = ((0, 0), (0, 0), (WINDOW, 0), (0, 0))
    k_win_pad = jnp.pad(k_win, pad)
    v_win_pad = jnp.pad(v_win, pad)

    def chunk(c):
        t0 = c * QC
        qc = lax.dynamic_slice_in_dim(q_rot, t0, QC, axis=3)
        qpos = t0 + jnp.arange(QC)
        idx = lax.dynamic_slice_in_dim(sel_idx, t0, QC, axis=2)
        ks = gather_blocks(k_blocks, idx).reshape(Bsz, Hk, QC, top * SB, Dh)
        vs = gather_blocks(v_blocks, idx).reshape(Bsz, Hk, QC, top * SB, Dh)
        kpos = (idx[..., None] * SB + jnp.arange(SB)).reshape(Bsz, Hk, 1, QC, top * SB)
        p_sel = masked_softmax(jnp.einsum('bkgqd,bkqmd->bkgqm', qc, ks) * scale,
                               kpos <= qpos[:, None])
        o_sel = jnp.einsum('bkgqm,bkqmd->bkgqd', p_sel, vs)
        kw = lax.dynamic_slice_in_dim(k_win_pad, t0, WINDOW + QC, axis=2)
        vw = lax.dynamic_slice_in_dim(v_win_pad, t0, WINDOW + QC, axis=2)
        kwpos = t0 - WINDOW + jnp.arange(WINDOW + QC)
        dist = qpos[:, None] - kwpos[None, :]
        win_mask = (kwpos[None, :] >= 0) & (dist >= 0) & (dist < WINDOW)
        p_win = masked_softmax(jnp.einsum('bkgqd,bknd->bkgqn', qc, kw) * scale, win_mask)
        o_win = jnp.einsum('bkgqn,bknd->bkgqd', p_win, vw)
        return o_sel, o_win

    o_sel, o_win = lax.map(chunk, jnp.arange(S // QC))
    o_sel = jnp.moveaxis(o_sel, 0, 3).reshape(Bsz, Hk, G, S, Dh)
    o_win = jnp.moveaxis(o_win, 0, 3).reshape(Bsz, Hk, G, S, Dh)
    o = gates[0] * o_cmp + gates[1] * o_sel + gates[2] * o_win
    o = o.transpose(0, 3, 1, 2, 4).reshape(Bsz, S, NSA_HEADS * Dh).astype(h.dtype)
    return o @ w_o

def first_inputs(seed: int = 0) -> dict:
    key = jax.random.key(seed)
    ks = jax.random.split(key, 32)
    f32 = jnp.float32

    def nrm(k, shape, fan_in):
        return jax.random.normal(k, shape, f32) * fan_in ** -0.5

    def gain(k, shape):
        return 1.0 + 0.02 * jax.random.normal(k, shape, f32)

    two_f = 2 * FFN_DIM
    return {
        'x': jax.random.normal(ks[0], (BATCH, SEQ, D_MODEL), f32),
        'norm_mix': gain(ks[1], (DEPTH, D_MODEL)),
        'norm_ffn': gain(ks[2], (DEPTH, D_MODEL)),
        'gla_w_in': nrm(ks[3], (N_A_LAYERS, D_MODEL, GLA_IN), D_MODEL),
        'gla_w_alpha_up': nrm(ks[4], (N_A_LAYERS, GLA_GATE_RANK, GLA_HEADS * GLA_DK), GLA_GATE_RANK),
        'gla_b_alpha': 0.1 * jax.random.normal(ks[5], (N_A_LAYERS, GLA_HEADS * GLA_DK), f32),
        'gla_norm': gain(ks[6], (N_A_LAYERS, GLA_HEADS, GLA_DV)),
        'gla_w_o': nrm(ks[7], (N_A_LAYERS, GLA_HEADS * GLA_DV, D_MODEL), GLA_HEADS * GLA_DV),
        'kv_norm': gain(ks[8], (D_MODEL,)),
        'nsa_w_kv': nrm(ks[9], (D_MODEL, NSA_KV_OUT), D_MODEL),
        'cmp_pe_k': 0.02 * jax.random.normal(ks[10], (CMP_BLOCK, NSA_HEAD_DIM), f32),
        'cmp_pe_v': 0.02 * jax.random.normal(ks[11], (CMP_BLOCK, NSA_HEAD_DIM), f32),
        'cmp_k_w1': nrm(ks[12], (CMP_BLOCK * NSA_HEAD_DIM, CMP_HIDDEN), CMP_BLOCK * NSA_HEAD_DIM),
        'cmp_k_w2': nrm(ks[13], (CMP_HIDDEN, NSA_HEAD_DIM), CMP_HIDDEN),
        'cmp_v_w1': nrm(ks[14], (CMP_BLOCK * NSA_HEAD_DIM, CMP_HIDDEN), CMP_BLOCK * NSA_HEAD_DIM),
        'cmp_v_w2': nrm(ks[15], (CMP_HIDDEN, NSA_HEAD_DIM), CMP_HIDDEN),
        'nsa_w_in': nrm(ks[16], (N_B_LAYERS, D_MODEL, NSA_IN), D_MODEL),
        'nsa_w_o': nrm(ks[17], (N_B_LAYERS, NSA_HEADS * NSA_HEAD_DIM, D_MODEL), NSA_HEADS * NSA_HEAD_DIM),
        'ffn_w_up': nrm(ks[18], (DEPTH, D_MODEL, two_f), D_MODEL),
        'ffn_conv_w': nrm(ks[19], (DEPTH, CONV_WIDTH, two_f), CONV_WIDTH),
        'ffn_conv_b': 0.02 * jax.random.normal(ks[20], (DEPTH, two_f), f32),
        'ffn_w_down': nrm(ks[21], (DEPTH, FFN_DIM, D_MODEL), FFN_DIM),
        'norm_final': gain(ks[22], (D_MODEL,)),
    }

def first_block(x, norm_mix, norm_ffn, gla_w_in, gla_w_alpha_up, gla_b_alpha, gla_norm, gla_w_o,
              kv_norm, nsa_w_kv, cmp_pe_k, cmp_pe_v, cmp_k_w1, cmp_k_w2, cmp_v_w1, cmp_v_w2,
              nsa_w_in, nsa_w_o, ffn_w_up, ffn_conv_w, ffn_conv_b, ffn_w_down, norm_final):
    shared = None
    for layer in range(DEPTH):
        if layer < N_A_LAYERS:
            hn = rmsnorm(x, norm_mix[layer])
            x = x + gla_mixer(hn, gla_w_in[layer], gla_w_alpha_up[layer], gla_b_alpha[layer],
                              gla_norm[layer], gla_w_o[layer])
        else:
            if layer == N_A_LAYERS:
                shared = nsa_shared_kv(x, kv_norm, nsa_w_kv, cmp_pe_k, cmp_pe_v,
                                       cmp_k_w1, cmp_k_w2, cmp_v_w1, cmp_v_w2)
            b = layer - N_A_LAYERS
            hn = rmsnorm(x, norm_mix[layer])
            x = x + nsa_mixer(hn, nsa_w_in[b], nsa_w_o[b], *shared)
        hn = rmsnorm(x, norm_ffn[layer])
        x = x + conv_ffn(hn, ffn_w_up[layer], ffn_conv_w[layer], ffn_conv_b[layer], ffn_w_down[layer])
    return rmsnorm(x, norm_final)


DIFF_HEADS = 4
DIFF_HEAD_DIM = 64
DIFF_WIDTH = DIFF_HEADS * 2 * DIFF_HEAD_DIM
SB_HEADS = 8
SB_HEAD_DIM = 64
SB_WIDTH = SB_HEADS * SB_HEAD_DIM
IN_COLS = 3 * DIFF_WIDTH + 3 * SB_WIDTH + 2 * D_MODEL
FFN_HIDDEN = -(-(8 * D_MODEL) // (3 * 256)) * 256
Q_BLOCK = 128
NORM_EPS = 1e-6


def rms_norm(x, g):
    xf = x.astype(jnp.float32)
    y = xf * lax.rsqrt(jnp.mean(xf * xf, axis=-1, keepdims=True) + NORM_EPS)
    return (y * g.astype(jnp.float32)).astype(x.dtype)

def rope_tables(seq, dim):
    pos = jnp.arange(seq, dtype=jnp.float32)
    inv = ROPE_THETA ** (-jnp.arange(0, dim, 2, dtype=jnp.float32) / dim)
    ang = pos[:, None] * inv[None, :]
    return jnp.cos(ang), jnp.sin(ang)

def apply_rope(t, cos, sin):
    c = cos[None, :, None, :].astype(t.dtype)
    s = sin[None, :, None, :].astype(t.dtype)
    t1, t2 = jnp.split(t, 2, axis=-1)
    return jnp.concatenate([t1 * c - t2 * s, t2 * c + t1 * s], axis=-1)

def to_blocks(t):
    b, h, s, d = t.shape
    return t.reshape(b, h, s // Q_BLOCK, Q_BLOCK, d).transpose(2, 0, 1, 3, 4)

def from_blocks(o):
    nb, b, h, q, dv = o.shape
    return o.transpose(1, 0, 3, 2, 4).reshape(b, nb * q, h, dv)

def diff_attention(q1, q2, k1, k2, v, lam):
    s_len = k1.shape[2]
    kpos = jnp.arange(s_len)
    qpos_blocks = kpos.reshape(-1, Q_BLOCK)
    scale = DIFF_HEAD_DIM ** -0.5

    def block(args):
        qb1, qb2, qpos = args
        mask = kpos[None, :] <= qpos[:, None]

        def probs(qb, k):
            sc = jnp.einsum('bhqd,bhkd->bhqk', qb, k).astype(jnp.float32) * scale
            sc = jnp.where(mask, sc, -jnp.inf)
            return jax.nn.softmax(sc, axis=-1)

        w = probs(qb1, k1) - lam * probs(qb2, k2)
        return jnp.einsum('bhqk,bhkd->bhqd', w.astype(v.dtype), v)

    o = lax.map(block, (to_blocks(q1), to_blocks(q2), qpos_blocks))
    return from_blocks(o)

def stick_breaking_attention(q, k, v):
    s_len = k.shape[2]
    kpos = jnp.arange(s_len)
    qpos_blocks = kpos.reshape(-1, Q_BLOCK)
    scale = SB_HEAD_DIM ** -0.5

    def block(args):
        qb, qpos = args
        mask = kpos[None, :] < qpos[:, None]
        z = jnp.einsum('bhqd,bhkd->bhqk', qb, k).astype(jnp.float32) * scale
        log_beta = jax.nn.log_sigmoid(z)
        log_rem = jnp.where(mask, jax.nn.log_sigmoid(-z), 0.0)
        key_axis = log_rem.ndim - 1
        after = lax.cumsum(log_rem, axis=key_axis, reverse=True) - log_rem
        a = jnp.where(mask, jnp.exp(log_beta + after), 0.0)
        return jnp.einsum('bhqk,bhkd->bhqd', a.astype(v.dtype), v)

    o = lax.map(block, (to_blocks(q), qpos_blocks))
    return from_blocks(o)

def hybrid_layer(x, cos, sin, layer, g_attn, w_in, b_gate, lam_p, subln, w_o_diff, w_o_sb,
                 w_out, g_ffn, w_ffn_in, w_ffn_out):
    b, s, _ = x.shape
    h = rms_norm(x, g_attn)
    proj = h @ w_in
    offs = np.cumsum([DIFF_WIDTH, DIFF_WIDTH, DIFF_WIDTH, SB_WIDTH, SB_WIDTH, SB_WIDTH]).tolist()
    dq, dk, dv, sq, sk, sv, gates = jnp.split(proj, offs, axis=-1)

    dq = apply_rope(dq.reshape(b, s, 2 * DIFF_HEADS, DIFF_HEAD_DIM), cos, sin)
    dk = apply_rope(dk.reshape(b, s, 2 * DIFF_HEADS, DIFF_HEAD_DIM), cos, sin)
    dq = dq.reshape(b, s, DIFF_HEADS, 2, DIFF_HEAD_DIM).transpose(3, 0, 2, 1, 4)
    dk = dk.reshape(b, s, DIFF_HEADS, 2, DIFF_HEAD_DIM).transpose(3, 0, 2, 1, 4)
    dv = dv.reshape(b, s, DIFF_HEADS, 2 * DIFF_HEAD_DIM).transpose(0, 2, 1, 3)
    lam_init = 0.8 - 0.6 * math.exp(-0.3 * layer)
    lp = lam_p.astype(jnp.float32)
    lam = jnp.exp(jnp.sum(lp[0] * lp[1])) - jnp.exp(jnp.sum(lp[2] * lp[3])) + lam_init
    o_diff = diff_attention(dq[0], dq[1], dk[0], dk[1], dv, lam)
    o_diff = (rms_norm(o_diff, subln) * (1.0 - lam_init)).reshape(b, s, DIFF_WIDTH)

    sq = sq.reshape(b, s, SB_HEADS, SB_HEAD_DIM).transpose(0, 2, 1, 3)
    sk = sk.reshape(b, s, SB_HEADS, SB_HEAD_DIM).transpose(0, 2, 1, 3)
    sv = sv.reshape(b, s, SB_HEADS, SB_HEAD_DIM).transpose(0, 2, 1, 3)
    o_sb = stick_breaking_attention(sq, sk, sv).reshape(b, s, SB_WIDTH)

    g_diff, g_sb = jnp.split(jax.nn.sigmoid(gates + b_gate), 2, axis=-1)
    merged = g_diff * (o_diff @ w_o_diff) + g_sb * (o_sb @ w_o_sb)
    x = x + merged @ w_out

    h2 = rms_norm(x, g_ffn)
    gate, up = jnp.split(h2 @ w_ffn_in, 2, axis=-1)
    return x + (jax.nn.silu(gate) * up) @ w_ffn_out

def second_inputs(seed: int = 0) -> dict:
    key = jax.random.key(seed)
    ks = jax.random.split(key, 14)
    f32 = jnp.float32
    nrm = lambda k, shape, scale: jax.random.normal(k, shape, f32) * scale
    return {
        "x": nrm(ks[0], (BATCH, SEQ, D_MODEL), 1.0),
        "norm_attn": 1.0 + nrm(ks[1], (DEPTH, D_MODEL), 0.02),
        "w_in": nrm(ks[2], (DEPTH, D_MODEL, IN_COLS), D_MODEL ** -0.5),
        "b_gate": nrm(ks[3], (DEPTH, 2 * D_MODEL), 0.02),
        "diff_lambda": nrm(ks[4], (DEPTH, 4, DIFF_HEAD_DIM), 0.1),
        "diff_subln": 1.0 + nrm(ks[5], (DEPTH, 2 * DIFF_HEAD_DIM), 0.02),
        "w_o_diff": nrm(ks[6], (DEPTH, DIFF_WIDTH, D_MODEL), DIFF_WIDTH ** -0.5),
        "w_o_sb": nrm(ks[7], (DEPTH, SB_WIDTH, D_MODEL), SB_WIDTH ** -0.5),
        "w_out": nrm(ks[8], (DEPTH, D_MODEL, D_MODEL), D_MODEL ** -0.5),
        "norm_ffn": 1.0 + nrm(ks[9], (DEPTH, D_MODEL), 0.02),
        "w_ffn_in": nrm(ks[10], (DEPTH, D_MODEL, 2 * FFN_HIDDEN), D_MODEL ** -0.5),
        "w_ffn_out": nrm(ks[11], (DEPTH, FFN_HIDDEN, D_MODEL), FFN_HIDDEN ** -0.5),
        "norm_final": 1.0 + nrm(ks[12], (D_MODEL,), 0.02),
    }

def second_block(x, norm_attn, w_in, b_gate, diff_lambda, diff_subln, w_o_diff, w_o_sb, w_out,
              norm_ffn, w_ffn_in, w_ffn_out, norm_final):
    cos, sin = rope_tables(x.shape[1], DIFF_HEAD_DIM)
    for layer in range(DEPTH):
        x = hybrid_layer(x, cos, sin, layer, norm_attn[layer], w_in[layer], b_gate[layer],
                         diff_lambda[layer], diff_subln[layer], w_o_diff[layer], w_o_sb[layer],
                         w_out[layer], norm_ffn[layer], w_ffn_in[layer], w_ffn_out[layer])
    return rms_norm(x, norm_final)


def setup_inputs(seed=0):
    out = dict(first_inputs(seed))
    for name, value in second_inputs(seed + 1).items():
        if name != "x":
            out[name + "_2"] = value
    return out


def reference(
    x, norm_mix, norm_ffn, gla_w_in, gla_w_alpha_up, gla_b_alpha, gla_norm, gla_w_o, kv_norm,
    nsa_w_kv, cmp_pe_k, cmp_pe_v, cmp_k_w1, cmp_k_w2, cmp_v_w1, cmp_v_w2, nsa_w_in, nsa_w_o,
    ffn_w_up, ffn_conv_w, ffn_conv_b, ffn_w_down, norm_final, norm_attn_2, w_in_2, b_gate_2,
    diff_lambda_2, diff_subln_2, w_o_diff_2, w_o_sb_2, w_out_2, norm_ffn_2, w_ffn_in_2,
    w_ffn_out_2, norm_final_2,
):
    x = first_block(
        x, norm_mix, norm_ffn, gla_w_in, gla_w_alpha_up, gla_b_alpha, gla_norm, gla_w_o,
        kv_norm, nsa_w_kv, cmp_pe_k, cmp_pe_v, cmp_k_w1, cmp_k_w2, cmp_v_w1, cmp_v_w2, nsa_w_in,
        nsa_w_o, ffn_w_up, ffn_conv_w, ffn_conv_b, ffn_w_down, norm_final,
    )
    return second_block(
        x, norm_attn_2, w_in_2, b_gate_2, diff_lambda_2, diff_subln_2, w_o_diff_2, w_o_sb_2,
        w_out_2, norm_ffn_2, w_ffn_in_2, w_ffn_out_2, norm_final_2,
    )


_drawn_inputs = setup_inputs


def setup_inputs(seed=0):
    import zlib

    import numpy as np

    out = dict(_drawn_inputs(seed))
    spreads = {}
    factors = {'gla_norm': 3.294,
     'kv_norm': 7.964,
     'cmp_pe_k': 8.0,
     'cmp_pe_v': 4.544,
     'norm_attn_2': 2.814,
     'b_gate_2': 8.0,
     'diff_subln_2': 4.931,
     'norm_ffn_2': 3.137,
     'norm_final_2': 2.828}
    for name, (base, spread) in spreads.items():
        noise = np.random.default_rng([zlib.crc32(name.encode()), seed]).standard_normal(out[name].shape)
        drawn = base * np.exp(spread * noise) if base else spread * noise
        out[name] = __import__('jax').numpy.asarray(drawn.astype(out[name].dtype))
    for name, factor in factors.items():
        out[name] = (out[name] * factor).astype(out[name].dtype)
    return out
```

```python
from contextlib import ExitStack

import numpy as np

import concourse.bass as bass
from concourse import mybir

ALU = mybir.AluOpType
ACT = mybir.ActivationFunctionType
F32 = mybir.dt.float32
F32R = mybir.dt.float32r
BF16 = mybir.dt.bfloat16
U16 = mybir.dt.uint16
AX_X = mybir.AxisListType.X

P = 128
T = 512
D = 1024
KT = D // P
TT = T // P
FFN = 2816
FT = FFN // P
EPS = 1e-6
NEG = -1e30

GLA_HEADS, GLA_DK, GLA_DV, GLA_TAU, GLA_RANK = 4, 128, 256, 16.0, 16
LEVELS = 7
NSA_HEADS, NSA_KV, DH = 16, 4, 64
CMP_BLOCK, CMP_STRIDE, CMP_HIDDEN = 32, 16, 256
N_CMP = (T - CMP_BLOCK) // CMP_STRIDE + 1
NC_PAD = 32
YW = NSA_KV * T + CMP_STRIDE
DIFF_HEADS, SB_HEADS = 4, 8
QSCALE = DH ** -0.5

SBUF_WORDS = 53200
RING = 4
UNIT = KT * P

U_GLA = 1 + 4 + 4 + 8 + 8
U_FFN = 2 * FT + FT
U_NSA_KV = 12
U_CMP = 8
U_NSA_Q = 1 + 8
U_HYB = 40
U_MERGE = 8
U_RES = 8

START = {}
_u = 0
for _name, _n in (("gla", U_GLA), ("gla_o", U_RES), ("ffn0", U_FFN), ("kv", U_NSA_KV), ("cmp", U_CMP),
                  ("nsa_q", U_NSA_Q), ("nsa_o", U_RES), ("ffn1", U_FFN),
                  ("hyb0", U_HYB), ("merge0", U_MERGE), ("out0", U_RES), ("ffn2", U_FFN),
                  ("hyb1", U_HYB), ("merge1", U_MERGE), ("out1", U_RES), ("ffn3", U_FFN)):
    START[_name] = _u
    _u += _n
UNITS = _u

COLS = {}
_c = 0
for _name, _n in (("gain", 11 * KT), ("conv_w", 2 * 3 * 2 * FT), ("conv_b", 2 * 2 * FT), ("b_gate", 2 * 16),
                  ("subln", 2), ("gla_norm", 8), ("w_alpha", 512), ("pe", 2 * 16), ("w2k", 256),
                  ("w2v", 128), ("lam", 2 * 4)):
    COLS[_name] = (_c, _c + _n)
    _c += _n
N_COLS = _c

CONST = {}
_c = 0
for _name, _n in (("ident", P), ("ones", P), ("cum", P), ("negtri", P), ("negones", P), ("rot", P),
                  ("cos", T), ("sin", T), ("sb_keep", P),
                  ("cmp_mask", TT * NC_PAD), ("cmp_valid", TT), ("eps", 1), ("one", 1)):
    CONST[_name] = (_c, _c + _n)
    _c += _n
N_CONST = _c
MASKS = 10


def constants():
    out = np.zeros((P, N_CONST), np.float32)

    def put(name, a):
        lo, hi = CONST[name]
        out[:, lo:hi] = np.asarray(a, np.float32).reshape(P, hi - lo)

    a, b = np.arange(P)[:, None], np.arange(P)[None, :]
    put("ident", a == b)
    put("ones", np.ones((P, P)))
    put("cum", (a <= b) / GLA_TAU)
    put("negtri", -1.0 * (a >= b))
    put("negones", -np.ones((P, P)))
    half = DH // 2
    rot = np.zeros((P, P))
    for m in range(P):
        if m % DH < half:
            rot[m + half, m] = -1.0
        else:
            rot[m - half, m] = 1.0
    put("rot", rot)
    inv = np.float32(10000.0) ** (-np.arange(half, dtype=np.float32) / np.float32(half))
    ang = (np.arange(T, dtype=np.float32)[:, None] * inv[None, :]).astype(np.float32)
    put("cos", np.cos(ang).T[np.arange(P) % half])
    put("sin", np.sin(ang).T[np.arange(P) % half])
    lv = np.zeros((P, 8, P))
    for n in range(LEVELS):
        h = P >> (n + 1)
        lv[:, n] = (a // (2 * h) == b // (2 * h)) & ((a // h) % 2 == 0) & ((b // h) % 2 == 1)
    lv[:, 7] = a == b
    masks = np.concatenate([lv, np.where(b <= a, 0.0, NEG)[:, None], np.where(a < b, 0.0, NEG)[:, None]], axis=1)
    put("sb_keep", a < b)
    n = np.arange(NC_PAD)
    pos = np.arange(TT)[None, :, None] * P + np.arange(P)[:, None, None]
    seen = (n * CMP_STRIDE + CMP_BLOCK - 1 <= pos) & (n < N_CMP)
    put("cmp_mask", np.where(seen, 0.0, NEG))
    put("cmp_valid", seen.any(-1))
    put("eps", np.full((P, 1), EPS))
    put("one", np.ones((P, 1)))
    return out, masks.astype(np.float32)


def build(nc, x_in, weights, params, consts, masks, out):
    ctx = ExitStack()
    with ctx:
        def sem(name):
            return ctx.enter_context(nc.semaphore(name))

        top = [0]

        def at(name, shape, dt, offset):
            return nc.alloc_sbuf_tensor_at(name, shape, dt, offset=first_byte + 4 * offset)

        def words(n):
            lo = top[0]
            top[0] += -(-n // 8) * 8
            return lo

        first_byte = -(-nc.sbuf_base // 32) * 32
        ctx.enter_context(nc.sbuf_tensor("all_of_sbuf", [P, SBUF_WORDS], F32))
        o_X = words(KT * T)
        o_XH = words(KT * T)
        o_XL = words(KT * T)
        o_ring = words(RING * 2 * UNIT)
        o_const = words(N_CONST)
        o_par = words(N_COLS)
        o_rstd = words(T)
        o_ss = words(T)
        o_sq = words(2 * T)
        o_small = words(800)
        o_masks = words(MASKS * P // 2)
        o_A = words(0)
        HID = FT * T
        assert o_A + 25690 <= SBUF_WORDS, o_A

        X = at("X", [P, KT, T], F32, o_X)
        XH = at("XH", [P, KT, T], F32R, o_XH)
        XL = at("XL", [P, KT, T], F32R, o_XL)
        w_raw = [at(f"w_raw{s}", [P, KT, P], F32, o_ring + 2 * s * UNIT) for s in range(RING)]
        w_lo = [at(f"w_lo{s}", [P, KT, P], F32R, o_ring + 2 * s * UNIT) for s in range(RING)]
        w_hi = [at(f"w_hi{s}", [P, KT, P], F32R, o_ring + (2 * s + 1) * UNIT) for s in range(RING)]
        const_sb = at("const_sb", [P, N_CONST], F32, o_const)
        par_sb = at("par_sb", [P, N_COLS], F32, o_par)
        rstd = at("rstd", [P, T], F32, o_rstd)
        ss = at("ss", [P, T], F32, o_ss)
        sq = at("sq", [P, 2, T], F32, o_sq)
        o_s = [o_small]

        def small(name, shape, dt=F32):
            n = int(np.prod(shape[1:])) * (2 if dt == BF16 else 4) // 4
            t = at(name, shape, dt, o_s[0])
            o_s[0] += (n + 7) // 8 * 8
            assert o_s[0] <= o_small + 800
            return t

        masks_bf = at("masks_bf", [P, MASKS, P], BF16, o_masks)
        causal_bf, sb_neg_bf = masks_bf[:, 8, :], masks_bf[:, 9, :]
        ident_bf = small("ident_bf", [P, P], BF16)

        def C(name):
            lo, hi = CONST[name]
            return const_sb[:, lo:hi]

        def PAR(name):
            lo, hi = COLS[name]
            return par_sb[:, lo:hi]

        ident, ones_m, rot_m, cos_t, sin_t = C("ident"), C("ones"), C("rot"), C("cos"), C("sin")
        negtri, negones = C("negtri"), C("negones")

        def gain(n, k):
            lo = COLS["gain"][0] + n * KT + k
            return par_sb[:, lo:lo + 1]

        eps_col, one_col = C("eps"), C("one")

        hid_h = at("hid_h", [P, FT * T], F32R, o_A)
        hid_l = at("hid_l", [P, FT * T], F32R, o_A + HID)
        o_T = o_A + 2 * HID
        f_u = [at(f"f_u{s}", [P, T + 2], F32, o_T + s * 520) for s in range(2)]
        f_c = [at(f"f_c{s}", [P, T], F32, o_T + 1040 + s * T) for s in range(2)]
        f_s = at("f_s", [P, T], F32, o_T + 1040 + 2 * T)
        f_h = at("f_h", [P, T], F32, o_T + 1040 + 3 * T)

        x_tok = at("x_tok", [P, TT, D], F32, o_A)
        masks_in = at("masks_in", [P, MASKS, P], F32, o_A + 8192)
        y_tok = at("y_tok", [P, TT, D], F32, o_A + 8192)
        y_fm = at("y_fm", [P, KT, T], F32, o_A)

        H4 = GLA_HEADS
        g_q = at("g_q", [P, H4, T], F32, o_A)
        g_k = at("g_k", [P, H4, T], F32, o_A + 2048)
        g_b = at("g_b", [P, H4, T], F32, o_A + 4096)
        g_z = [at(f"g_z{s}", [P, H4, T], F32, o_A + 6144 + 2048 * s) for s in range(2)]
        g_v = at("g_v", [P, TT, D], F32, o_A + 10240)
        g_a = at("g_a", [P, T], F32, o_A + 10240)
        g_r = at("g_r", [P, 8, T], F32, o_A + 14336)
        g_vt = at("g_vt", [P, 2, T], F32, o_A + 14336 + 6 * T)
        g_g = at("g_g", [P, TT, T], F32, o_A + 18432)
        g_att = at("g_att", [P, TT, H4, P], F32, o_A + 18432)
        g_state = at("g_state", [P, H4, GLA_DV], F32, o_A + 20480)
        g_kdT = at("g_kdT", [P, TT - 1, H4, P], F32, o_A + 21504)
        g_qd = at("g_qd", [P, H4, T], F32, o_A + 23040)
        g_elast = small("g_elast", [P, H4, TT])
        g_o = at("g_o", [P, 8, T], F32, o_A)
        g_oh = at("g_oh", [P, 8, T], F32R, o_A + 4096)
        g_ol = at("g_ol", [P, 8, T], F32R, o_A + 8192)
        g_osq = at("g_osq", [P, 2, T], F32, o_A + 18432)
        g_ors = at("g_ors", [P, T], F32, o_A + 18432 + 2 * T)

        XH2 = at("XH2", [P, KT, T], F32R, o_A + 14592)
        XL2 = at("XL2", [P, KT, T], F32R, o_A + 14592 + 4096)
        n_yh = [at(f"n_yh{s}", [P, YW], F32R, o_A + s * YW) for s in range(2)]
        n_yl = [at(f"n_yl{s}", [P, YW], F32R, o_A + (2 + s) * YW) for s in range(2)]
        n_k = [at(f"n_k{s}", [P, NSA_KV, T], F32, o_A + 8448 + 2048 * s) for s in range(2)]
        n_v = [at(f"n_v{s}", [P, TT, NSA_KV * DH], F32, o_A + 12544 + 1024 * s) for s in range(2)]
        o_N = o_A + 22784
        n_raw = at("n_raw", [P, 2, T], F32, o_N)
        n_t1 = at("n_t1", [P, T], F32, o_sq)
        n_t2 = at("n_t2", [P, T], F32, o_sq + T)
        n_yt_h = at("n_yt_h", [P, T], F32R, o_sq)
        n_yt_l = at("n_yt_l", [P, T], F32R, o_sq + T)
        n_qp = at("n_qp", [P, NSA_HEADS, T], F32, o_XH)
        n_hT = at("n_hT", [P, 2, CMP_HIDDEN], F32, o_N + 1024)
        n_hid = at("n_hid", [P, 2, 2, P], F32, o_N + 2048)
        n_kc = small("n_kc", [P, NSA_KV, 2, NC_PAD])
        n_bd = at("n_bd", [P, NSA_KV, 2, P], F32, o_N + 1024)
        n_peh = at("n_peh", [P, 2, 16], F32R, o_N + 2560)
        n_pel = at("n_pel", [P, 2, 16], F32R, o_N + 2592)
        n_gate = at("n_gate", [P, TT, 48], F32, o_N + 2624)
        n_st = at("n_st", [P, 2, P], F32, o_N + 2048)
        n_PT = at("n_PT", [P, 2, 4, TT, P], F32, o_A)
        n_P = at("n_P", [P, 4, T], F32, o_A + 4096)
        n_sc = [at(f"n_sc{s}", [P, T], F32, o_A + 2048 + s * T) for s in range(2)]
        n_pcT = at("n_pcT", [P, 4, T], F32, o_A + 6144)
        n_cst = small("n_cst", [P, 3, 16])
        n_oh = at("n_oh", [P, 8, T], F32R, o_A + 14592)
        n_ol = at("n_ol", [P, 8, T], F32R, o_A + 14592 + 4096)

        h_dq = at("h_dq", [P, 4, T], F32, o_A)
        h_dk = at("h_dk", [P, 4, 2, T], F32, o_A + 2048)
        h_dv = at("h_dv", [P, TT, T], F32, o_A + 6144)
        h_gate = at("h_gate", [P, 16, T], F32, o_A)
        h_sq = at("h_sq", [P, 4, T], F32, o_A + 8192)
        h_sk = at("h_sk", [P, SB_HEADS, T], F32, o_A + 10240)
        h_sv = at("h_sv", [P, TT, T], F32, o_A + 14336)
        h_od = at("h_od", [P, 4, T], F32, o_A + 16384)
        h_os = at("h_os", [P, 4, T], F32, o_A + 18432)
        o_H = o_A + 20480
        h_raw = at("h_raw", [P, 2, T], F32, o_H)
        h_P = at("h_P", [P, 2, T], F32, o_H + 1024)
        h_W = at("h_W", [P, 2, T], F32, o_H + 2048)
        h_WT = at("h_WT", [P, TT, T], F32, o_H + 3072)
        h_sp = at("h_sp", [P, 2, 1280], F32, o_H)
        h_a = at("h_a", [P, 2, 1280], F32, o_H + 2560)
        h_t1 = at("h_t1", [P, T], F32, o_sq)
        h_t2 = at("h_t2", [P, T], F32, o_sq + T)
        h_osq = at("h_osq", [P, T], F32, o_sq)
        h_ors = at("h_ors", [P, T], F32, o_sq + T)
        h_m = at("h_m", [P, 2, T], F32, o_sq)
        h_st = small("h_st", [P, 4, 32])
        h_lam = small("h_lam", [P, 8])
        h_sub = small("h_sub", [P, 2])
        h_odh = at("h_odh", [P, 4, T], F32R, o_XH)
        h_odl = at("h_odl", [P, 4, T], F32R, o_XH + 2048)
        h_osh = at("h_osh", [P, 4, T], F32R, o_XL)
        h_osl = at("h_osl", [P, 4, T], F32R, o_XL + 2048)
        h_mt = at("h_mt", [P, 8, T], F32, o_H)
        h_m2 = at("h_m2", [P, T], F32, o_H + 4096)
        h_mh = at("h_mh", [P, 8, T], F32R, o_A + 8192)
        h_ml = at("h_ml", [P, 8, T], F32R, o_A + 12288)

        bank = [ctx.enter_context(nc.psum_tensor(f"bank{b}", [P, T], F32)) for b in range(8)]

        s_const = sem("const_in")
        s_xin = sem("x_in")
        s_bf = sem("masks_bf16_ready")
        s_raw = [sem(f"unit_in{s}") for s in range(RING)]
        s_hi = sem("w_hi_ready")
        s_w = sem("unit_split")
        s_used = sem("unit_used")
        s_xt = sem("xT_ready")
        s_x = sem("x_written")
        s_sq = sem("sq_ready")
        s_xh = sem("xh_ready")
        s_xl = sem("xl_ready")
        s_ss = sem("sumsq_step")
        s_stat = sem("sumsq_ready")
        s_rln = sem("rstd_ln_ready")
        s_rstd = sem("rstd_ready")
        s_res = sem("down_tile_ready")
        s_dve = sem("dve_step")
        s_act = sem("act_step")
        s_u, s_c0, s_c1, s_c2, s_silu, s_h, s_hh, s_hl = (sem("ffn_" + n) for n in (
            "u_ready", "tap2_ready", "tap1_ready", "conv_ready", "silu_ready", "h_ready", "hid_hi_ready", "hid_ready"))
        s_y, s_yt, s_yc, s_out = (sem("out_" + n) for n in ("y_ready", "yT_ready", "y_copied", "stored"))
        gs = {n: sem("gla_" + n) for n in (
            "evac", "vT", "vc", "silu", "apre", "soft", "g", "cum", "b", "D", "E", "Z", "mm", "ev", "qd", "kd", "kdT",
            "kdc", "o", "oc", "st", "state", "osq", "on", "ors", "ot", "oh", "ol")}
        ns = {n: sem("nsa_" + n) for n in (
            "xh2", "xl2", "evac", "yh", "yl", "rot", "rope", "vT", "vc", "hid", "hT", "hTc", "kvc", "kvcc", "gT",
            "gate", "p0", "cs", "csub", "cmax", "ce", "p", "s", "mx", "exp", "w", "t", "tc", "pT", "pTc", "pv", "oh", "o")}
        hs = {n: sem("hyb_" + n) for n in (
            "evac", "rot", "rope", "vT", "vc", "gate", "lp", "lsum", "le", "lam", "s", "mx", "exp", "w", "t", "tc", "pv",
            "osq", "on", "ors", "od", "odh", "odl", "z", "ln", "sp", "cum", "a", "spv", "osc", "osh", "osl", "mevac", "mt", "m", "mh",
            "ml")}

        block = ctx.enter_context(nc.Block())

        PREP = {0: 0, 1: 1, 2: 2, 3: 3, 5: 4, 6: 5, 7: 6, 8: 7}
        GAIN = {0: 0, 1: 1, 2: 2, 3: 4, 4: 5, 5: 6, 6: 7, 7: 8, 8: 9, 9: 10}
        KV_MIX_GAIN = 3
        DOWN_TILES = KT - 1
        HYB_N = (5, 7)
        LAM_INIT = [0.8 - 0.6 * float(np.exp(-0.3 * layer)) for layer in range(2)]
        FILL = {n: 12 + 3 * (n // TT) + n % TT for n in range(DIFF_HEADS * TT) if n % TT < 3}
        SB_AT = [0, 512, 1024, 896]
        SB_W = [T - P * j for j in range(TT)]


        @block.sync
        def _(sp):
            sp.dma_start(const_sb[:, :], consts).then_inc(s_const, 16)
            sp.dma_start(x_tok[:, :, :], x_in.rearrange("a (c p) d -> p (a c) d", p=P)).then_inc(s_xin, 16)
            sp.dma_start(par_sb[:, :], params).then_inc(s_const, 16)
            sp.dma_start(masks_in[:, :, :], masks).then_inc(s_const, 16)
            for u in range(min(RING, UNITS)):
                sp.dma_start(w_raw[u][:, :, :], weights[u]).then_inc(s_raw[u], 16)
            rounds = UNITS // RING
            with sp.Fori(1, rounds) as i:
                for s in range(RING):
                    sp.wait_ge(s_used, i * RING + (s + 1 - RING))
                    sp.dma_start(w_raw[s][:, :, :],
                                 weights[bass.ds(i * RING + s, 1)].rearrange("a p k c -> p (a k) c"))\
                        .then_inc(s_raw[s], 16)
            for u in range(rounds * RING, UNITS):
                sp.wait_ge(s_used, u - RING + 1)
                sp.dma_start(w_raw[u % RING][:, :, :], weights[u]).then_inc(s_raw[u % RING], 16)
            for c in range(TT):
                sp.wait_ge(s_yc, 2 * c + 2)
                sp.dma_start(out[0, c * P:(c + 1) * P, :], y_tok[:, c, :]).then_inc(s_out, 16)
            sp.wait_ge(s_out, 16 * TT)

        @block.gpsimd
        def _(pool):
            pool.wait_ge(s_const, 48)
            ones_unit = ones_m[:, None, :].broadcast_to([P, KT, P])

            def split(s, landed, hi):
                pool.wait_ge(s_raw[s], landed)
                nc.gpsimd.tensor_tensor(w_hi[s][:, :, :], w_raw[s][:, :, :], ones_unit, ALU.mult).then_inc(s_hi, 1)
                pool.wait_ge(s_hi, hi)
                nc.gpsimd.tensor_tensor(w_lo[s][:, :, :], w_raw[s][:, :, :], w_hi[s][:, :, :].bitcast(F32),
                                        ALU.subtract).then_inc(s_w, 1)

            rounds = UNITS // RING
            with pool.Fori(0, rounds) as i:
                for s in range(RING):
                    split(s, i * 16 + 16, i * RING + (s + 1))
            for u in range(rounds * RING, UNITS):
                split(u % RING, 16 * (u // RING + 1), u + 1)

        @block.tensor
        def _(pe):
            def product(out_ap, slot, j, xh, xl, start, stop):
                nc.tensor.matmul(out_ap, w_hi[slot][:, j, :], xh, start=start, stop=False)
                nc.tensor.matmul(out_ap, w_hi[slot][:, j, :], xl, start=False, stop=False)
                return nc.tensor.matmul(out_ap, w_lo[slot][:, j, :], xh, start=False, stop=stop)

            def tile(u, b, xh, xl, k_sem=None, k_base=0):
                pe.wait_ge(s_w, u + 1)
                for k in range(KT):
                    if k_sem is not None:
                        pe.wait_ge(k_sem, k_base + k + 1)
                    mm = product(bank[b][:, :], u % RING, k, xh[:, k, :], xl[:, k, :], k == 0, k == KT - 1)
                mm.then_inc(s_used, 1)

            def stats(n):
                pe.wait_ge(s_ss, 8 * n + 8)
                nc.tensor.matmul(bank[7][:, :], ones_m, ss[:, :], start=True, stop=True).then_inc(s_stat, 1)

            def turn(b, src, done):
                for c in range(TT):
                    mm = nc.tensor.transpose(bank[b][:, c * P:(c + 1) * P], src[:, c * P:(c + 1) * P], ident)
                mm.then_inc(done, 1)

            def residual(n, name, xh, xl, k_sem, k_base, banks=(0, 1, 2, 3)):
                for f in range(KT):
                    if f >= 4:
                        pe.wait_ge(s_x, 8 * n + f - 3)
                    tile(START[name] + f, banks[f % 4], xh, xl, k_sem if f == 0 else None, k_base)

            def ffn(fi, n, name):
                u0 = START[name]
                xl_base = 8 * PREP[n]
                pe.wait_ge(s_x, 8 * n + 5)

                def up_tile(t, wait_u, first):
                    pe.wait_ge(s_w, wait_u)
                    for k in range(KT):
                        if first:
                            pe.wait_ge(s_xl, xl_base + k + 1)
                        mm = product(bank[t][:, :], (u0 + t) % RING, k, XH[:, k, :], XL[:, k, :], k == 0, k == KT - 1)
                    mm.then_inc(s_used, 1)

                for t in range(4):
                    up_tile(t, u0 + t + 1, t == 0)
                    if t == 0:
                        stats(n)
                with pe.Fori(1, 2 * FT // 4) as i:
                    for t in range(4):
                        pe.wait_ge(s_u, i * 4 + (2 * FT * fi + t - 3))
                        up_tile(t, i * 4 + (u0 + t + 1), False)

                d0 = u0 + 2 * FT
                tail = 4
                head = (FT - tail) % RING

                def down_unit(slot, wait_u, wait_h, xh, xl, start):
                    pe.wait_ge(s_w, wait_u)
                    pe.wait_ge(s_hl, wait_h)
                    for f in (4, 5, 6, 7, 0, 1, 2, 3):
                        if start and f == 0:
                            pe.wait_ge(s_u, 2 * FT * (fi + 1))
                        mm = product(bank[f][:, :], slot, f, xh, xl, start, False)
                    mm.then_inc(s_used, 1)

                for j in range(head):
                    down_unit((d0 + j) % RING, d0 + j + 1, FT * fi + j + 1, hid_h[:, j * T:(j + 1) * T], hid_l[:, j * T:(j + 1) * T], j == 0)
                with pe.Fori(0, (FT - tail) // RING) as i:
                    for s in range(RING):
                        j0 = head + s
                        cols = bass.ds(i * (RING * T) + j0 * T, T)
                        down_unit((d0 + j0) % RING, i * RING + (d0 + j0 + 1), i * RING + (FT * fi + j0 + 1),
                                  hid_h[:, cols], hid_l[:, cols], False)
                for j in range(FT - tail, FT):
                    pe.wait_ge(s_w, d0 + j + 1)
                    pe.wait_ge(s_hl, FT * fi + j + 1)
                for f in range(KT):
                    for j in range(FT - tail, FT):
                        mm = product(bank[f][:, :], (d0 + j) % RING, f, hid_h[:, j * T:(j + 1) * T], hid_l[:, j * T:(j + 1) * T], False, j == FT - 1)
                        if f == KT - 1:
                            mm.then_inc(s_used, 1)
                    if f < KT - 1:
                        mm.then_inc(s_res, 1)

            def gla():
                u0 = START["gla"]
                m_level = [0]

                def level(lv):
                    for c in range(TT):
                        m = m_level[0]
                        b = 5 + m % 3
                        if m >= 3:
                            pe.wait_ge(gs["ev"], m - 2)
                        if c == 0 and lv < LEVELS:
                            pe.wait_ge(gs["Z"], lv + 1)
                        cols = slice(c * P, (c + 1) * P)
                        for h in range(H4):
                            left = g_z[lv % 2] if lv < LEVELS else g_k
                            right = g_z[lv % 2] if lv < LEVELS else g_q
                            mm = nc.tensor.matmul(bank[b][:, h * P:(h + 1) * P], left[:, h, cols], right[:, h, cols],
                                                  start=True, stop=True)
                        mm.then_inc(gs["mm"], 1)
                        m_level[0] += 1

                def v_turn(f):
                    pe.wait_ge(gs["evac"], 9 + f + 1)
                    pe.wait_ge(gs["vc"], f) if f else pe.wait_ge(gs["b"], H4)
                    turn(4, g_vt[:, f % 2, :], gs["vT"])

                for t in range(U_GLA):
                    if t >= 4:
                        pe.wait_ge(gs["evac"], t - 3)
                    tile(u0 + t, t % 4, XH, XL, s_xl if t == 0 else None)
                    if t == 0:
                        stats(0)
                    if t == 2:
                        pe.wait_ge(gs["evac"], 1)
                        pe.wait_ge(s_rstd, 1)
                        for c in range(TT):
                            nc.tensor.matmul(bank[4 + c][:, :], g_a[:, c * P:(c + 1) * P], PAR("w_alpha"),
                                             start=True, stop=True).then_inc(gs["apre"], 1)
                    if t == 8:
                        pe.wait_ge(gs["g"], TT)
                        for h in range(H4):
                            for c in range(TT):
                                mm = nc.tensor.matmul(bank[4 + h][:, c * P:(c + 1) * P], g_g[:, c, h * P:(h + 1) * P],
                                                      C("cum"), start=True, stop=True)
                            mm.then_inc(gs["cum"], 1)
                    if t >= 9:
                        if 10 <= t <= 17:
                            v_turn(t - 10)
                        if t >= 11 and t % 2:
                            level((t - 11) // 2)
                level(LEVELS)
                pe.wait_ge(gs["evac"], U_GLA)
                pe.wait_ge(gs["kd"], 1)
                for c in range(TT - 1):
                    for h in range(H4):
                        mm = nc.tensor.transpose(bank[c][:, h * P:(h + 1) * P], g_z[1][:, h, c * P:(c + 1) * P], ident)
                    mm.then_inc(gs["kdT"], 1)
                pe.wait_ge(gs["ev"], 8 * TT)
                pe.wait_ge(gs["vc"], 8)
                pe.wait_ge(gs["kdc"], TT - 1)
                pe.wait_ge(gs["qd"], 1)
                for c in range(TT):
                    for hp in range(2):
                        m = 2 * c + hp
                        if m >= 4:
                            pe.wait_ge(gs["oc"], m - 3)
                        if c:
                            pe.wait_ge(gs["state"], 4 * c)
                        for q in range(4):
                            h, dv = 2 * hp + q // 2, q % 2
                            vc = slice(h * GLA_DV + dv * P, h * GLA_DV + (dv + 1) * P)
                            o = bank[4 + m % 4][:, q * P:(q + 1) * P]
                            mm = nc.tensor.matmul(o, g_v[:, c, vc], g_att[:, c, h, :], start=True, stop=c == 0)
                            if c:
                                mm = nc.tensor.matmul(o, g_state[:, h, dv * P:(dv + 1) * P], g_qd[:, h, c * P:(c + 1) * P],
                                                      start=False, stop=True)
                        mm.then_inc(gs["o"], 1)
                    if c < TT - 1:
                        if c == 2:
                            pe.wait_ge(gs["state"], 4)
                        for h in range(H4):
                            mm = nc.tensor.matmul(bank[(2 * c + h // 2) % 4][:, h % 2 * GLA_DV:(h % 2 + 1) * GLA_DV],
                                                  g_kdT[:, c, h, :], g_v[:, c, h * GLA_DV:(h + 1) * GLA_DV],
                                                  start=True, stop=True)
                            if h % 2:
                                mm.then_inc(gs["st"], 1)
                pe.wait_ge(gs["oc"], 2 * TT)
                for h in range(H4):
                    pe.wait_ge(gs["osq"], 2 * h + 2)
                    for j in range(2):
                        mm = nc.tensor.matmul(bank[4 + h][:, :], ones_m, g_osq[:, j, :], start=j == 0, stop=j == 1)
                    mm.then_inc(gs["on"], 1)
                residual(1, "gla_o", g_oh, g_ol, gs["ol"], 0)

            def nsa():
                u0 = START["kv"]

                def aux(t):
                    if t < 4:
                        return
                    pe.wait_ge(ns["evac"], t + 1)
                    if t in (4, 5, 8, 9):
                        m = (t - 4) % 4 + 2 * (t // 8)
                        if m:
                            pe.wait_ge(ns["rope"], m)
                        nc.tensor.matmul(bank[4][:, :], rot_m, n_raw[:, t % 2, :], start=True, stop=True)\
                            .then_inc(ns["rot"], 1)
                    else:
                        m = (t - 6) % 4 + 2 * (t // 10)
                        if m:
                            pe.wait_ge(ns["vc"], m)
                        turn(5, n_raw[:, t % 2, :], ns["vT"])

                for t in range(U_NSA_KV):
                    if t >= 4:
                        pe.wait_ge(ns["evac"], t - 3)
                    tile(u0 + t, t % 4, XH, XL, s_xl if t == 0 else None, 8 * PREP[2])
                    if t == 0:
                        stats(2)
                    if t:
                        aux(t - 1)
                aux(U_NSA_KV - 1)

                pe.wait_ge(ns["yh"], 4)
                pe.wait_ge(ns["yl"], 4)
                pe.wait_ge(s_rstd, 3)
                for kv in range(2):
                    o = bank[6 + kv][:, 0:CMP_HIDDEN]
                    for ip in range(16):
                        u = START["cmp"] + 4 * kv + ip // 4
                        i = ip % 4
                        if i == 0:
                            pe.wait_ge(s_w, u + 1)
                        blocks = slice(2 * ip, 2 * ip + CMP_STRIDE * (P - 1) + 1, CMP_STRIDE)
                        for n, (w, y, e) in enumerate(((w_hi, n_yh, n_peh), (w_hi, n_yl, n_pel), (w_lo, n_yh, n_peh))):
                            rhs = w[u % RING][:, 2 * i:2 * i + 2, :].rearrange("p a b -> p (a b)")
                            nc.tensor.matmul(o, y[kv][:, blocks], rhs, start=ip == 0 and n == 0, stop=False)
                            mm = nc.tensor.matmul(o, e[:, kv, ip:ip + 1].broadcast_to([P, P]), rhs, start=False,
                                                  stop=ip == 15 and n == 2)
                        if i == 3:
                            mm.then_inc(s_used, 1)

                def hidden_turn(kv):
                    pe.wait_ge(ns["hid"], kv + 1)
                    for jt in range(2):
                        mm = nc.tensor.transpose(bank[4 + kv][:, jt * P:(jt + 1) * P], n_hT[:, kv, jt * P:(jt + 1) * P], ident)
                    mm.then_inc(ns["hT"], 1)

                def compressed():
                    pe.wait_ge(ns["hTc"], 2)
                    for jt in range(2):
                        mm = nc.tensor.matmul(bank[6][:, 0:P], PAR("w2k")[:, jt * P:(jt + 1) * P], n_hid[:, 0, jt, :],
                                              start=jt == 0, stop=jt == 1)
                    mm.then_inc(ns["kvc"], 1)
                    for g in range(NSA_KV):
                        for jt in range(2):
                            for copy in range(4):
                                rows = slice(copy * NC_PAD, (copy + 1) * NC_PAD)
                                mm = nc.tensor.matmul(bank[7][rows, g * DH:(g + 1) * DH],
                                                      n_hid[:, 1, jt, g * NC_PAD:(g + 1) * NC_PAD],
                                                      PAR("w2v")[:, jt * DH:(jt + 1) * DH], start=jt == 0, stop=jt == 1)
                    mm.then_inc(ns["kvc"], 1)

                def query(e):
                    raw = n_raw[:, (e + 1) % 2, :]
                    rd = e // 2
                    pe.wait_ge(ns["evac"], U_NSA_KV + 1 + e + 1)
                    if e:
                        pe.wait_ge(ns["rope"], 4 + e)
                    nc.tensor.matmul(bank[4][:, :], rot_m, raw, start=True, stop=True).then_inc(ns["rot"], 1)
                    if e == 0:
                        pe.wait_ge(ns["kvcc"], 5)
                    if e % 2 == 0 and rd >= 2:
                        pe.wait_ge(ns["csub"], rd - 1)
                    for c in range(TT):
                        lo_ = c * P + e % 2 * 64
                        mm = nc.tensor.matmul(bank[6 + rd % 2][:, lo_:lo_ + 64], raw[:, c * P:(c + 1) * P], n_kc[:, rd, :, :],
                                              start=True, stop=True)
                    mm.then_inc(ns["cs"], 1)

                def cmp_turn(rd, b):
                    pe.wait_ge(ns["p"], rd + 1)
                    if rd:
                        pe.wait_ge(ns["pTc"], rd)
                    for c in range(TT):
                        mm = nc.tensor.transpose(bank[b][:, c * P:(c + 1) * P], n_sc[rd % 2][:, c * P:(c + 1) * P], ident)
                    mm.then_inc(ns["pT"], 1)

                u0 = START["nsa_q"]
                for t in range(U_NSA_Q):
                    pe.wait_ge(ns["evac"], U_NSA_KV + t - 3)
                    tile(u0 + t, t % 4, XH2, XL2, ns["xl2"] if t == 0 else None)
                    if t == 0:
                        pe.wait_ge(ns["rope"], 4)
                        pe.wait_ge(ns["vc"], 4)
                        hidden_turn(0)
                        hidden_turn(1)
                    if t == 1:
                        compressed()
                        pe.wait_ge(ns["evac"], U_NSA_KV + 1)
                        turn(5, n_raw[:, 0, :], ns["gT"])
                    if t >= 2:
                        query(t - 2)
                    if t == 5 or t == 7:
                        pe.wait_ge(ns["gate"], 1)
                        cmp_turn((t - 5) // 2, 5)
                query(7)
                cmp_turn(2, 5)

                pe.wait_ge(ns["rope"], 12)
                pe.wait_ge(ns["pTc"], 3)
                pe.wait_ge(ns["csub"], 4)
                jobs = NSA_HEADS * TT * 2
                for q in range(jobs + 5):
                    if q == 4:
                        cmp_turn(3, 0)
                    if q < jobs:
                        e, i, par, c = q // 16, q // 4 % 4, q // 2 % 2, q % 2
                        S = (i + 1) * P
                        b = bank[4 + q % 4]
                        if q >= 4:
                            pe.wait_ge(ns["exp"], q - 3)
                        nc.tensor.matmul(b[:, 0:S], n_qp[:, 2 * e + par, i * P:S], n_k[c][:, e // 2, 0:S], start=True, stop=False)
                        nc.tensor.matmul(b[:, i * P:S], ident_bf[:, :], causal_bf, start=False, stop=True)\
                            .then_inc(ns["s"], 1)
                    if 3 <= q < jobs + 3:
                        m = q - 3
                        i = m // 4 % 4
                        pe.wait_ge(ns["w"], m + 1)
                        if m >= 3:
                            pe.wait_ge(ns["tc"], m - 2)
                        for j in range(i + 1):
                            mm = nc.tensor.transpose(bank[1 + m % 3][:, j * P:(j + 1) * P], n_P[:, m % 4, j * P:(j + 1) * P], ident)
                        mm.then_inc(ns["t"], 1)
                    if q >= 8 and q % 4 == 0:
                        n = (q - 8) // 4
                        e, i = n // 4, n % 4
                        g = e // 2
                        pe.wait_ge(ns["tc"], 4 * n + 4)
                        if i == 0:
                            pe.wait_ge(ns["pTc"], g + 1)
                            if e:
                                pe.wait_ge(ns["o"], e)
                            nc.tensor.matmul(bank[0][:, :], n_bd[:, g, e % 2, :], n_pcT[:, g, :], start=True, stop=False,
                                             skip_group_check=True)
                        for j in range(i + 1):
                            for c in range(2):
                                for par in range(2):
                                    mm = nc.tensor.matmul(bank[0][par * DH:(par + 1) * DH, i * P:(i + 1) * P],
                                                          n_v[c][:, j, g * DH:(g + 1) * DH], n_PT[:, n % 2, 2 * par + c, j, :],
                                                          start=False, stop=j == i and c == 1, skip_group_check=True)
                        mm.then_inc(ns["pv"], 1)
                residual(3, "nsa_o", n_oh, n_ol, ns["o"], 0, (4, 5, 6, 7))

            def hybrid(ly):
                n0 = HYB_N[ly]
                u0 = START[f"hyb{ly}"]
                e0 = U_HYB * ly

                def aux(t):
                    pe.wait_ge(hs["evac"], e0 + t + 1)
                    if t < 8:
                        if t or ly:
                            pe.wait_ge(hs["rope"], 8 * ly + t)
                        nc.tensor.matmul(bank[4][:, :], rot_m, h_raw[:, t % 2, :], start=True, stop=True)\
                            .then_inc(hs["rot"], 1)
                    else:
                        m = t - 8 if t < 12 else t - 16
                        if m or ly:
                            pe.wait_ge(hs["vc"], 8 * ly + m)
                        turn(5 if m < 4 else 7, h_raw[:, t % 2, :], hs["vT"])

                def fill(t):
                    pe.wait_ge(hs["evac"], e0 + t - 1)
                    tile(u0 + t, t % 2, XH, XL)

                for t in range(12):
                    if t >= 4:
                        pe.wait_ge(hs["evac"], e0 + t - 3)
                    tile(u0 + t, t % 4, XH, XL, s_xl if t == 0 else None, 8 * PREP[n0])
                    if t == 0:
                        stats(n0)
                    if t == 1:
                        pe.wait_ge(hs["lp"], ly + 1)
                        nc.tensor.matmul(bank[6][:, 0:2], ones_m, h_lam[:, 0:2], start=True, stop=True)\
                            .then_inc(hs["lsum"], 1)
                    if t:
                        aux(t - 1)
                aux(11)

                pe.wait_ge(hs["vc"], 8 * ly + 4)
                pe.wait_ge(hs["rope"], 8 * ly + 8)
                pe.wait_ge(hs["lam"], ly + 1)
                pe.wait_ge(s_rstd, n0 + 1)
                pe.wait_ge(hs["evac"], e0 + 12)
                units = DIFF_HEADS * TT
                q0 = units * ly

                def d_turn(m):
                    pe.wait_ge(hs["w"], q0 + m + 1)
                    if m:
                        pe.wait_ge(hs["tc"], q0 + m)
                    for j in range(m % TT + 1):
                        mm = nc.tensor.transpose(bank[2][:, j * P:(j + 1) * P], h_W[:, m % 2, j * P:(j + 1) * P], ident)
                    mm.then_inc(hs["t"], 1)

                def d_values(h):
                    pe.wait_ge(hs["tc"], q0 + TT * (h + 1))
                    if h:
                        pe.wait_ge(hs["od"], 4 * ly + h)
                    for j in range(TT):
                        mm = nc.tensor.matmul(bank[3][:, j * P:T], h_dv[:, j, h * P:(h + 1) * P], h_WT[:, j, j * P:T],
                                              start=j == 0, stop=j == TT - 1)
                    mm.then_inc(hs["pv"], 1)

                def d_sumsq(h):
                    pe.wait_ge(hs["osq"], 4 * ly + h + 1)
                    if h:
                        pe.wait_ge(hs["ors"], 4 * ly + h)
                    nc.tensor.matmul(bank[6][:, :], ones_m, h_osq[:, :], start=True, stop=True).then_inc(hs["on"], 1)

                for n in range(units):
                    h, i = n // TT, n % TT
                    S = (i + 1) * P
                    if n:
                        pe.wait_ge(hs["exp"], 2 * (q0 + n))
                    for c in range(2):
                        b = bank[4 + c]
                        nc.tensor.matmul(b[:, 0:S], h_dq[:, h, i * P:S], h_dk[:, h, c, 0:S], start=True, stop=False)
                        nc.tensor.matmul(b[:, i * P:S], ident_bf[:, :], causal_bf, start=False, stop=True)\
                            .then_inc(hs["s"], 1)
                    if n:
                        d_turn(n - 1)
                        if FILL.get(n - 1, 0) >= 20:
                            aux(FILL[n - 1])
                    if n in FILL:
                        fill(FILL[n])
                    if n and (n - 1) % TT == TT - 1:
                        d_values((n - 1) // TT)
                    if n >= 2 and (n - 2) % TT == TT - 1:
                        d_sumsq((n - 2) // TT)
                d_turn(units - 1)

                pe.wait_ge(hs["vc"], 8 * ly + 8)
                k0 = SB_HEADS * ly

                def region(j):
                    return bank[(4, 5, 7, 5)[j]], 384 if j == 3 else 0

                def s_values(a):
                    pe.wait_ge(hs["a"], k0 + 2 * a + 2)
                    if a:
                        pe.wait_ge(hs["osc"], 3 * ly + a)
                    for j in range(TT):
                        for par in range(2):
                            h = 2 * a + par
                            mm = nc.tensor.matmul(bank[2][par * DH:(par + 1) * DH, j * P:T], h_sv[:, j, h * DH:(h + 1) * DH],
                                                  h_a[:, par, SB_AT[j]:SB_AT[j] + SB_W[j]], start=j == 0, stop=j == TT - 1)
                    mm.then_inc(hs["spv"], 1)

                for h in range(SB_HEADS):
                    if h:
                        pe.wait_ge(hs["a"], k0 + h)
                    else:
                        pe.wait_ge(hs["exp"], 2 * (q0 + units))
                    for j in range(TT):
                        b, lo = region(j)
                        mm = nc.tensor.matmul(b[:, lo:lo + SB_W[j]], h_sk[:, h, j * P:(j + 1) * P],
                                              h_sq[:, h // 2, j * P:T], start=j != 3, stop=False, skip_group_check=True)
                    mm.then_inc(hs["z"], 1)
                    if h % 2 == 0 and h:
                        s_values(h // 2 - 1)
                    fill(24 + 2 * h)
                    if h == 0:
                        d_values(DIFF_HEADS - 1)
                    fill(25 + 2 * h)
                    if h == 0:
                        d_sumsq(DIFF_HEADS - 1)
                    pe.wait_ge(hs["sp"], k0 + h + 1)
                    sp_ = h_sp[:, h % 2, :]
                    later = h_a[:, h % 2, :]
                    for j in range(TT):
                        b, lo = region(j)
                        nc.tensor.matmul(b[:, lo:lo + SB_W[j]], negtri, sp_[:, SB_AT[j]:SB_AT[j] + SB_W[j]],
                                         start=False, stop=False, skip_group_check=True)
                        if j < TT - 1:
                            nc.tensor.matmul(b[:, lo + P:lo + 2 * P], negones, sp_[:, SB_AT[j + 1]:SB_AT[j + 1] + P],
                                             start=False, stop=False, skip_group_check=True)
                        if j < TT - 2:
                            at_ = 256 * j
                            nc.tensor.matmul(b[:, lo + 2 * P:lo + SB_W[j]], negones, later[:, at_:at_ + SB_W[j] - 2 * P],
                                             start=False, stop=False, skip_group_check=True)
                        mm = nc.tensor.matmul(b[:, lo:lo + P], ident_bf[:, :], sb_neg_bf, start=False, stop=True,
                                              skip_group_check=True)
                    mm.then_inc(hs["cum"], 1)

                u0 = START[f"merge{ly}"]
                pe.wait_ge(hs["evac"], e0 + U_HYB)
                pe.wait_ge(hs["od"], 4 * ly + 4)
                for m in range(2 * KT):
                    u = u0 + m // 2
                    if m % 2 == 0:
                        pe.wait_ge(s_w, u + 1)
                    if m >= 4:
                        pe.wait_ge(hs["mevac"], 16 * ly + m - 3)
                    xh, xl, ready = (h_osh, h_osl, "osl") if m >= KT else (h_odh, h_odl, "odl")
                    for k in range(4):
                        if m % KT == 0:
                            pe.wait_ge(hs[ready], 4 * ly + k + 1)
                        mm = product(bank[(0, 1, 3, 6)[m % 4]][:, :], u % RING, m % 2 * 4 + k, xh[:, k, :], xl[:, k, :],
                                     k == 0, k == 3)
                    mm.then_inc(hs["mt"] if m % 2 == 0 else s_used, 1)
                    if m == 1:
                        s_values(3)
                residual(n0 + 1, f"out{ly}", h_mh, h_ml, hs["ml"], 8 * ly, (2, 4, 5, 7))

            pe.wait_ge(s_const, 48)
            pe.wait_ge(s_xin, 16)
            pe.wait_ge(s_bf, 2)
            for k in range(KT):
                for c in range(TT):
                    mm = nc.tensor.transpose(bank[k][:, c * P:(c + 1) * P], x_tok[:, c, k * P:(k + 1) * P], ident)
                mm.then_inc(s_xt, 1)
            gla()
            ffn(0, 1, "ffn0")
            nsa()
            ffn(1, 3, "ffn1")
            stats(4)
            hybrid(0)
            ffn(2, 6, "ffn2")
            hybrid(1)
            ffn(3, 8, "ffn3")
            stats(9)
            pe.wait_ge(s_y, KT)
            for c in range(TT):
                for half in range(2):
                    for k in range(4):
                        mm = nc.tensor.transpose(bank[2 * c + half][:, k * P:(k + 1) * P],
                                                 y_fm[:, 4 * half + k, c * P:(c + 1) * P], ident)
                    mm.then_inc(s_yt, 1)

        @block.scalar
        def _(act):
            steps = [0]

            def own(ins):
                steps[0] += 1
                ins.then_inc(s_act, 1)
                act.wait_ge(s_act, steps[0])

            def squares(n, k):
                act.wait_ge(s_x, 8 * n + k + 1)
                if 8 * n + k >= 2:
                    act.wait_ge(s_ss, 8 * n + k - 1)
                nc.scalar.activation(sq[:, k % 2, :], X[:, k, :], ACT.Square).then_inc(s_sq, 1)

            def prepare(n):
                for k in range(KT):
                    squares(n, k)
                    nc.scalar.activation(XH[:, k, :], X[:, k, :], ACT.Copy, scale=gain(GAIN[n], k)).then_inc(s_xh, 1)

            def inv_rms(n):
                act.wait_ge(s_stat, n + 1)
                nc.scalar.activation(rstd[:, :], bank[7][:, :], ACT.Ln, bias=eps_col, scale=1.0 / D).then_inc(s_rln, 1)
                act.wait_ge(s_rln, n + 1)
                nc.scalar.activation(rstd[:, :], rstd[:, :], ACT.Exp, scale=-0.5).then_inc(s_rstd, 1)

            def ffn(fi, n):
                conv = fi < 2
                nc.scalar.preload_act_table_set("silu_and_others")
                with act.Fori(0, FT // 2) as i:
                    for p in range(2):
                        up = i * 4 + (2 * FT * fi + 2 * p)
                        pair = i * 2 + (FT * fi + p)
                        if conv:
                            for side in range(2):
                                act.wait_ge(s_u, up + (side + 1))
                                if side:
                                    act.wait_ge(s_h, pair)
                                t = i * 4 + (2 * p + side)
                                w0, b0 = COLS["conv_w"][0] + (fi * 3 + 2) * 2 * FT, COLS["conv_b"][0] + fi * 2 * FT
                                nc.scalar.activation(f_c[side][:, :], f_u[side][:, 2:T + 2], ACT.Identity,
                                                     bias=par_sb[:, bass.ds(t + b0, 1)],
                                                     scale=par_sb[:, bass.ds(t + w0, 1)]).then_inc(s_c0, 1)
                            act.wait_ge(s_c2, up + 1)
                        else:
                            act.wait_ge(s_u, up + 1)
                        nc.scalar.activation(f_s[:, :], f_c[0][:, :], ACT.Silu).then_inc(s_silu, 1)
                        act.wait_ge(s_h, pair + 1)
                        nc.scalar.activation(hid_h[:, bass.ds(i * (2 * T) + p * T, T)], f_h[:, :], ACT.Copy)\
                            .then_inc(s_hh, 1)

            def gla():
                u0 = START["gla"]

                def v_copy(f):
                    act.wait_ge(gs["vT"], f + 1)
                    nc.scalar.activation(g_v[:, :, f * P:(f + 1) * P],
                                         bank[4][:, :].rearrange("p (c k) -> p c k", c=TT), ACT.Copy).then_inc(gs["vc"], 1)

                nc.scalar.preload_act_table_set("natural_log_exp_and_others")
                prepare(0)
                inv_rms(0)
                for c in range(TT):
                    act.wait_ge(gs["apre"], c + 1)
                    ins = nc.scalar.activation(g_z[0][:, c, :], bank[4 + c][:, :], ACT.Abs)
                own(ins)
                own(nc.scalar.activation(g_z[0][:, :, :], g_z[0][:, :, :], ACT.Exp, scale=-1.0))
                nc.scalar.activation(g_z[0][:, :, :], g_z[0][:, :, :], ACT.Ln, bias=one_col).then_inc(gs["soft"], 1)
                for h in range(H4):
                    act.wait_ge(gs["cum"], h + 1)
                    nc.scalar.activation(g_b[:, h, :], bank[4 + h][:, :], ACT.Copy).then_inc(gs["b"], 1)
                for lv in range(8):
                    if 1 <= lv <= 4:
                        v_copy(2 * lv - 1)
                    if lv < 4:
                        v_copy(2 * lv)
                    if lv < LEVELS:
                        act.wait_ge(gs["D"], lv + 1)
                        nc.scalar.activation(g_z[lv % 2][:, :, :], g_z[lv % 2][:, :, :], ACT.Exp).then_inc(gs["E"], 1)
                act.wait_ge(gs["mm"], LEVELS * TT)
                nc.scalar.activation(g_z[0][:, :, :], g_b[:, :, :], ACT.Exp).then_inc(gs["E"], 1)
                act.wait_ge(gs["D"], LEVELS + 1)
                nc.scalar.activation(g_z[1][:, :, :], g_z[1][:, :, :], ACT.Exp).then_inc(gs["E"], 1)
                for f in range(8):
                    act.wait_ge(gs["evac"], 17 + f + 1)
                    nc.scalar.activation(g_r[:, f, :], g_r[:, f, :], ACT.Silu).then_inc(gs["silu"], 1)
                for c in range(TT - 1):
                    act.wait_ge(gs["kdT"], c + 1)
                    nc.scalar.activation(g_kdT[:, c, :, :], bank[c][:, :].rearrange("p (h k) -> p h k", h=H4), ACT.Copy)\
                        .then_inc(gs["kdc"], 1)
                for m in range(2 * TT):
                    c, hp = m // 2, m % 2
                    act.wait_ge(gs["o"], m + 1)
                    ins = nc.scalar.activation(g_o[:, 4 * hp:4 * hp + 4, c * P:(c + 1) * P],
                                               bank[4 + m % 4][:, :].rearrange("p (q t) -> p q t", q=4), ACT.Copy)
                    ins.then_inc(gs["oc"], 1)
                act.wait_ge(gs["oc"], 2 * TT)
                nc.scalar.preload_act_table_set("natural_log_exp_and_others")

                def o_hi(f):
                    act.wait_ge(gs["ot"], f + 1)
                    nc.scalar.activation(g_oh[:, f, :], g_o[:, f, :], ACT.Copy).then_inc(gs["oh"], 1)

                for h in range(H4):
                    if h:
                        act.wait_ge(gs["on"], h)
                    for j in range(2):
                        nc.scalar.activation(g_osq[:, j, :], g_o[:, 2 * h + j, :], ACT.Square).then_inc(gs["osq"], 1)
                    if h:
                        o_hi(2 * h - 2)
                        o_hi(2 * h - 1)
                    act.wait_ge(gs["on"], h + 1)
                    own(nc.scalar.activation(g_ors[:, :], bank[4 + h][:, :], ACT.Ln, bias=eps_col, scale=1.0 / GLA_DV))
                    nc.scalar.activation(g_ors[:, :], g_ors[:, :], ACT.Exp, scale=-0.5).then_inc(gs["ors"], 1)
                o_hi(6)
                o_hi(7)

            def nsa():
                def v_copy(m):
                    act.wait_ge(ns["vT"], m + 1)
                    nc.scalar.activation(n_v[m // 2][:, :, m % 2 * P:(m % 2 + 1) * P],
                                         bank[5][:, :].rearrange("p (c k) -> p c k", c=TT), ACT.Copy).then_inc(ns["vc"], 1)

                nc.scalar.preload_act_table_set("natural_log_exp_and_others")
                prepare(2)
                inv_rms(2)
                for k in range(KT):
                    nc.scalar.activation(XH2[:, k, :], X[:, k, :], ACT.Copy, scale=gain(KV_MIX_GAIN, k)).then_inc(ns["xh2"], 1)
                for t in range(4):
                    act.wait_ge(ns["evac"], t + 1)
                    if t == 0:
                        act.wait_ge(ns["yl"], 1)
                    for e in range(2):
                        head = 2 * (t % 2) + e
                        r = slice(DH * e, DH * e + DH)
                        nc.scalar.activation(n_yh[t // 2][0:DH, head * T:(head + 1) * T], n_raw[r, t % 2, :], ACT.Copy)
                        ins = nc.scalar.activation(n_yh[t // 2][DH:P, head * T:(head + 1) * T - 1], n_raw[r, t % 2, 1:T], ACT.Copy)
                    ins.then_inc(ns["yh"], 1)
                for m in range(4):
                    v_copy(m)
                for kv in range(2):
                    act.wait_ge(s_used, START["cmp"] + 4 * kv + 4)
                    nc.scalar.activation(n_hT[:, kv, :], bank[6 + kv][:, 0:CMP_HIDDEN], ACT.Gelu_apprx_tanh).then_inc(ns["hid"], 1)
                for kv in range(2):
                    act.wait_ge(ns["hT"], kv + 1)
                    nc.scalar.activation(n_hid[:, kv, :, :], bank[4 + kv][:, 0:CMP_HIDDEN].rearrange("p (j n) -> p j n", j=2),
                                         ACT.Copy).then_inc(ns["hTc"], 1)
                act.wait_ge(ns["kvc"], 1)
                act.wait_ge(ns["p0"], 1)
                for par in range(2):
                    r = slice(par * DH, (par + 1) * DH)
                    ins = nc.scalar.activation(n_kc[r, :, par, :], bank[6][r, 0:P].rearrange("p (g n) -> p g n", g=NSA_KV), ACT.Copy)
                ins.then_inc(ns["kvcc"], 1)
                act.wait_ge(ns["kvc"], 2)
                for copy in range(4):
                    r = slice(copy * NC_PAD, (copy + 1) * NC_PAD)
                    nc.scalar.activation(n_bd[r, :, copy // 2, copy % 2 * DH:(copy % 2 + 1) * DH],
                                         bank[7][r, 0:NSA_KV * DH].rearrange("p (g d) -> p g d", g=NSA_KV), ACT.Copy)\
                        .then_inc(ns["kvcc"], 1)
                act.wait_ge(ns["gT"], 1)
                nc.scalar.activation(n_gate[:, :, :], bank[5][:, :].rearrange("p (c k) -> p c k", c=TT)[:, :, 0:48],
                                     ACT.Sigmoid).then_inc(ns["gate"], 1)
                nc.scalar.preload_act_table_set("natural_log_exp_and_others")

                def cmp_exp(rd):
                    act.wait_ge(ns["cmax"], rd + 1)
                    s = n_sc[rd % 2]
                    nc.scalar.activation(s[:, :], s[:, :], ACT.Exp).then_inc(ns["ce"], 1)

                def cmp_copy(rd, b):
                    act.wait_ge(ns["pT"], rd + 1)
                    nc.scalar.activation(n_pcT[:, rd, :], bank[b][:, :], ACT.Copy).then_inc(ns["pTc"], 1)

                cmp_exp(0)
                for rd in range(1, 4):
                    cmp_exp(rd)
                    cmp_copy(rd - 1, 5)
                jobs = NSA_HEADS * TT * 2
                for q in range(jobs + 6):
                    if q == 5:
                        cmp_copy(3, 0)
                    if q < jobs:
                        S = (q // 4 % 4 + 1) * P
                        if q >= 4:
                            act.wait_ge(ns["t"], q - 3)
                        act.wait_ge(ns["mx"], q + 1)
                        nc.scalar.activation(n_P[:, q % 4, 0:S], bank[4 + q % 4][:, 0:S], ACT.Exp, bias=n_st[:, 0, q:q + 1],
                                             accum_out=n_st[:, 1, q:q + 1]).then_inc(ns["exp"], 1)
                    if 4 <= q < jobs + 4:
                        m = q - 4
                        n, i = m // 4, m // 4 % 4
                        if m % 4 == 0 and n >= 2:
                            act.wait_ge(ns["pv"], n - 1)
                        act.wait_ge(ns["t"], m + 1)
                        nc.scalar.activation(n_PT[:, n % 2, m % 4, 0:i + 1, :],
                                             bank[1 + m % 3][:, 0:(i + 1) * P].rearrange("p (j t) -> p j t", t=P), ACT.Copy)\
                            .then_inc(ns["tc"], 1)
                    if q >= 21 and (q - 21) % 16 == 0:
                        e = (q - 21) // 16
                        act.wait_ge(ns["pv"], 4 * e + 4)
                        nc.scalar.activation(n_oh[:, e, :], bank[0][:, :], ACT.Copy).then_inc(ns["oh"], 1)

            def hybrid(ly):
                n0 = HYB_N[ly]

                def v_copy(m, b):
                    act.wait_ge(hs["vT"], 8 * ly + m + 1)
                    dst, f = (h_dv, m) if m < 4 else (h_sv, m - 4)
                    nc.scalar.activation(dst[:, :, f * P:(f + 1) * P], bank[b][:, :].rearrange("p (c k) -> p c k", c=TT),
                                         ACT.Copy).then_inc(hs["vc"], 1)

                nc.scalar.preload_act_table_set("natural_log_exp_and_others")
                prepare(n0)
                inv_rms(n0)
                act.wait_ge(hs["lsum"], ly + 1)
                nc.scalar.activation(h_lam[:, 2:4], bank[6][:, 0:2], ACT.Exp).then_inc(hs["le"], 1)
                for m in range(4):
                    v_copy(m, 5)
                units = DIFF_HEADS * TT
                q0 = units * ly

                def squares_of(h):
                    act.wait_ge(hs["pv"], 4 * ly + h + 1)
                    nc.scalar.activation(h_osq[:, :], bank[3][:, :], ACT.Square).then_inc(hs["osq"], 1)

                for n in range(units + 1):
                    if n < units:
                        S = (n % TT + 1) * P
                        if n:
                            act.wait_ge(hs["w"], q0 + n)
                        for c in range(2):
                            act.wait_ge(hs["mx"], 2 * (q0 + n) + c + 1)
                            nc.scalar.activation(h_P[:, c, 0:S], bank[4 + c][:, 0:S], ACT.Exp,
                                                 bias=h_st[:, 0, 2 * n + c:2 * n + c + 1],
                                                 accum_out=h_st[:, 1, 2 * n + c:2 * n + c + 1]).then_inc(hs["exp"], 1)
                    if n:
                        m = n - 1
                        h, i = m // TT, m % TT
                        if i == 0 and h:
                            act.wait_ge(hs["pv"], 4 * ly + h)
                        act.wait_ge(hs["t"], q0 + m + 1)
                        nc.scalar.activation(h_WT[:, 0:i + 1, i * P:(i + 1) * P],
                                             bank[2][:, 0:(i + 1) * P].rearrange("p (j t) -> p j t", t=P), ACT.Copy)\
                            .then_inc(hs["tc"], 1)
                        if FILL.get(m, 0) >= 20:
                            v_copy(FILL[m] - 16, 7)
                    if 5 <= n < units and (n - 5) % TT == 0:
                        squares_of((n - 5) // TT)
                    if 6 <= n < units and (n - 6) % TT == 0:
                        d_norm(ly, (n - 6) // TT)
                k0 = SB_HEADS * ly
                for h in range(SB_HEADS):
                    act.wait_ge(hs["z"], k0 + h + 1)
                    e = h_sp[:, h % 2, :]
                    nc.scalar.activation(e[:, 0:512], bank[4][:, :], ACT.Abs)
                    nc.scalar.activation(e[:, 512:1024], bank[5][:, :], ACT.Abs)
                    own(nc.scalar.activation(e[:, 1024:1280], bank[7][:, 0:256], ACT.Abs))
                    own(nc.scalar.activation(e, e, ACT.Exp, scale=-1.0))
                    nc.scalar.activation(e, e, ACT.Ln, bias=one_col).then_inc(hs["ln"], 1)
                    if h == 0:
                        squares_of(DIFF_HEADS - 1)
                        d_norm(ly, DIFF_HEADS - 1)
                    if h % 2 == 0 and h:
                        a = h // 2 - 1
                        act.wait_ge(hs["spv"], 4 * ly + a + 1)
                        nc.scalar.activation(h_os[:, a, :], bank[2][:, :], ACT.Copy).then_inc(hs["osc"], 1)
                    if h == SB_HEADS - 1:
                        act.wait_ge(s_used, START[f"hyb{ly}"] + U_HYB)
                        act.wait_ge(hs["od"], 4 * ly + 4)
                        for k in range(4):
                            nc.scalar.activation(h_odh[:, k, :], h_od[:, k, :], ACT.Copy).then_inc(hs["odh"], 1)
                    act.wait_ge(hs["cum"], k0 + h + 1)
                    a_ = h_a[:, h % 2, :]
                    nc.scalar.activation(a_[:, 0:512], bank[4][:, :], ACT.Exp)
                    nc.scalar.activation(a_[:, 512:1024], bank[5][:, :], ACT.Exp)
                    nc.scalar.activation(a_[:, 1024:1280], bank[7][:, 0:256], ACT.Exp).then_inc(hs["a"], 1)

                def gate(f):
                    act.wait_ge(hs["evac"], U_HYB * ly + 24 + f + 1)
                    lo = COLS["b_gate"][0] + 16 * ly + f
                    nc.scalar.activation(h_gate[:, f, :], h_gate[:, f, :], ACT.Sigmoid, bias=par_sb[:, lo:lo + 1])\
                        .then_inc(hs["gate"], 1)

                nc.scalar.preload_act_table_set("sigmoid_and_others")
                gate(0)
                gate(1)
                for a in range(3):
                    act.wait_ge(hs["osc"], 3 * ly + a + 1)
                    nc.scalar.activation(h_osh[:, a, :], h_os[:, a, :], ACT.Copy).then_inc(hs["osh"], 1)
                gate(2)
                act.wait_ge(hs["spv"], 4 * ly + 4)
                nc.scalar.activation(h_osh[:, 3, :], bank[2][:, :], ACT.Copy).then_inc(hs["osh"], 1)
                for f in range(3, 16):
                    gate(f)
                for f in range(KT):
                    act.wait_ge(hs["m"], 8 * ly + f + 1)
                    nc.scalar.activation(h_mh[:, f, :], h_m[:, f % 2, :], ACT.Copy).then_inc(hs["mh"], 1)

            def d_norm(ly, h):
                act.wait_ge(hs["on"], 4 * ly + h + 1)
                if h:
                    act.wait_ge(hs["od"], 4 * ly + h)
                own(nc.scalar.activation(h_ors[:, :], bank[6][:, :], ACT.Ln, bias=eps_col, scale=1.0 / (2 * DH)))
                nc.scalar.activation(h_ors[:, :], h_ors[:, :], ACT.Exp, scale=-0.5).then_inc(hs["ors"], 1)

            act.wait_ge(s_const, 48)
            gla()
            prepare(1)
            inv_rms(1)
            ffn(0, 1)
            nsa()
            prepare(3)
            inv_rms(3)
            ffn(1, 3)
            nc.scalar.preload_act_table_set("natural_log_exp_and_others")
            for k in range(KT):
                squares(4, k)
            inv_rms(4)
            hybrid(0)
            prepare(6)
            inv_rms(6)
            ffn(2, 6)
            hybrid(1)
            prepare(8)
            inv_rms(8)
            ffn(3, 8)
            nc.scalar.preload_act_table_set("natural_log_exp_and_others")
            for k in range(KT):
                squares(9, k)
            inv_rms(9)
            for c in range(TT):
                for half in range(2):
                    act.wait_ge(s_yt, 2 * c + half + 1)
                    nc.scalar.activation(y_tok[:, c, half * T:(half + 1) * T], bank[2 * c + half][:, :], ACT.Copy)\
                        .then_inc(s_yc, 1)

        @block.vector
        def _(dve):
            steps = [0]
            V = nc.vector

            def own(ins):
                steps[0] += 1
                ins.then_inc(s_dve, 1)
                dve.wait_ge(s_dve, steps[0])

            def lo(n, k, parts=True):
                if parts:
                    dve.wait_ge(s_xh, 8 * PREP[n] + k + 1)
                    V.scalar_tensor_tensor(XL[:, k, :], X[:, k, :], gain(GAIN[n], k), XH[:, k, :].bitcast(F32),
                                           ALU.mult, ALU.subtract).then_inc(s_xl, 1)
                dve.wait_ge(s_sq, 8 * n + k + 1)
                if k == 0:
                    if n:
                        dve.wait_ge(s_stat, n)
                    V.tensor_copy(ss[:, :], sq[:, 0, :]).then_inc(s_ss, 1)
                else:
                    dve.wait_ge(s_ss, 8 * n + k)
                    V.tensor_tensor(ss[:, :], ss[:, :], sq[:, k % 2, :], ALU.add).then_inc(s_ss, 1)

            def add_residual(n, ready, banks, parts=True):
                for k in range(KT):
                    dve.wait_ge(*ready(k))
                    V.tensor_tensor(X[:, k, :], X[:, k, :], bank[banks(k)][:, :], ALU.add).then_inc(s_x, 1)
                    if k:
                        lo(n, k - 1, parts)
                lo(n, KT - 1, parts)

            def projected(n, name, banks=(0, 1, 2, 3)):
                add_residual(n, lambda k: (s_used, START[name] + k + 1), lambda k: banks[k % 4])

            def ffn(fi, n, name, n_next):
                conv = fi < 2
                dve.wait_ge(s_rstd, n + 1)
                u0 = START[name]
                if conv:
                    for side in range(2):
                        V.memset(f_u[side][:, 0:2], 0.0)
                with dve.Fori(0, FT // 2) as i:
                    for p in range(2):
                        c = i * 4 + 2 * p
                        up = i * 4 + (2 * FT * fi + 2 * p)
                        pair = i * 2 + (FT * fi + p)
                        for side in range(2):
                            dve.wait_ge(s_used, i * 4 + (u0 + 2 * p + side + 1))
                            dst = f_u[side][:, 2:T + 2] if conv else f_c[side][:, :]
                            V.tensor_tensor(dst, bank[2 * p + side][:, :], rstd[:, :], ALU.mult).then_inc(s_u, 1)
                        if conv:
                            for side in range(2):
                                w0 = COLS["conv_w"][0] + fi * 3 * 2 * FT + side
                                f = f_c[side][:, :]
                                dve.wait_ge(s_c0, up + (side + 1))
                                V.scalar_tensor_tensor(f, f_u[side][:, 1:T + 1], par_sb[:, bass.ds(c + (w0 + 2 * FT), 1)], f,
                                                       ALU.mult, ALU.add).then_inc(s_c1, 1)
                                dve.wait_ge(s_c1, up + (side + 1))
                                V.scalar_tensor_tensor(f, f_u[side][:, 0:T], par_sb[:, bass.ds(c + w0, 1)], f,
                                                       ALU.mult, ALU.add).then_inc(s_c2, 1)
                            dve.wait_ge(s_c2, up + 2)
                        dve.wait_ge(s_silu, pair + 1)
                        if not conv:
                            dve.wait_ge(s_u, up + 2)
                        V.tensor_tensor(f_h[:, :], f_s[:, :], f_c[1][:, :], ALU.mult).then_inc(s_h, 1)
                        dve.wait_ge(s_hh, pair + 1)
                        V.tensor_tensor(hid_l[:, bass.ds(i * (2 * T) + p * T, T)], f_h[:, :],
                                        hid_h[:, bass.ds(i * (2 * T) + p * T, T)].bitcast(F32), ALU.subtract)\
                            .then_inc(s_hl, 1)
                add_residual(n_next,
                             lambda k: (s_res, DOWN_TILES * fi + k + 1) if k < KT - 1 else (s_used, u0 + U_FFN),
                             lambda k: k, n_next in PREP)

            def rotate(dst, raw, b, done):
                V.tensor_tensor(n_t1[:, :], raw, cos_t, ALU.mult)
                own(V.tensor_tensor(n_t2[:, :], bank[b][:, :], sin_t, ALU.mult))
                for d, r in dst:
                    ins = V.tensor_tensor(d, n_t1[r, :], n_t2[r, :], ALU.add)
                ins.then_inc(done, 1)

            def gla():
                u0 = START["gla"]

                def evac(t):
                    dve.wait_ge(s_used, u0 + t + 1)
                    b = bank[t % 4][:, :]
                    if t == 0:
                        dve.wait_ge(s_rstd, 1)
                        own(V.tensor_tensor(g_a[:, :], b, rstd[:, :], ALU.mult))
                        V.memset(g_a[0:1, :], 1.0).then_inc(gs["evac"], 1)
                        return
                    if t < 5:
                        V.scalar_tensor_tensor(g_q[:, t - 1, :], b, GLA_DK ** -0.5, rstd[:, :], ALU.mult, ALU.mult)\
                            .then_inc(gs["evac"], 1)
                        return
                    if t < 9:
                        dst = g_k[:, t - 5, :]
                    elif t < 17:
                        dst = g_vt[:, (t - 9) % 2, :]
                        if t >= 11:
                            dve.wait_ge(gs["vT"], t - 10)
                    else:
                        if t == 23:
                            dve.wait_ge(gs["vT"], 8)
                        dst = g_r[:, t - 17, :]
                    V.tensor_tensor(dst, b, rstd[:, :], ALU.mult).then_inc(gs["evac"], 1)

                def blocks(a, lv):
                    h = P >> (lv + 1)
                    return a[:, :, :].rearrange("p h (n two e) -> p (h n) two e", two=2, e=h)

                def exponents(lv):
                    z, b = blocks(g_z[lv % 2], lv), blocks(g_b, lv)
                    h = P >> (lv + 1)
                    ref = b[:, :, 0, h - 1:h].broadcast_to([P, H4 * T // (2 * h), h])
                    if lv >= 2:
                        dve.wait_ge(gs["mm"], TT * (lv - 1))
                    V.tensor_tensor(z[:, :, 1, :], b[:, :, 1, :], ref, ALU.subtract)
                    V.tensor_tensor(z[:, :, 0, :], ref, b[:, :, 0, :], ALU.subtract).then_inc(gs["D"], 1)

                def decayed(lv):
                    z, q, k = blocks(g_z[lv % 2], lv), blocks(g_q, lv), blocks(g_k, lv)
                    dve.wait_ge(gs["E"], lv + 1)
                    V.tensor_tensor(z[:, :, 1, :], z[:, :, 1, :], q[:, :, 1, :], ALU.mult)
                    V.tensor_tensor(z[:, :, 0, :], z[:, :, 0, :], k[:, :, 0, :], ALU.mult).then_inc(gs["Z"], 1)

                def place(lv):
                    mask = masks_bf[:, lv:lv + 1, :].bitcast(U16)
                    for c in range(TT):
                        m = TT * lv + c
                        dve.wait_ge(gs["mm"], m + 1)
                        V.copy_predicated(g_att[:, c, :, :], mask.broadcast_to([P, H4, P]),
                                          bank[5 + m % 3][:, :].rearrange("p (h t) -> p h t", h=H4)).then_inc(gs["ev"], 1)

                for t in range(9):
                    evac(t)
                    if t == 5:
                        dve.wait_ge(gs["soft"], 1)
                        for c in range(TT):
                            V.scalar_tensor_tensor(g_g[:, c, :], bank[4 + c][:, :], 0.0, g_z[0][:, c, :], ALU.min,
                                                   ALU.subtract).then_inc(gs["g"], 1)
                dve.wait_ge(gs["b"], H4)
                V.memset(g_att[:, :, :, :], 0.0)
                exponents(0)
                for lv in range(8):
                    evac(9 + 2 * lv)
                    if lv:
                        place(lv - 1)
                    evac(10 + 2 * lv)
                    if lv < LEVELS - 1:
                        exponents(lv + 1)
                    if lv < LEVELS:
                        decayed(lv)
                z1 = g_z[1][:, :, :].rearrange("p h (c t) -> p h c t", t=P)
                bb = g_b[:, :, :].rearrange("p h (c t) -> p h c t", t=P)
                for h in range(H4):
                    ins = V.tensor_tensor(z1[:, h, :, :], bb[:, h, :, P - 1:P].broadcast_to([P, TT, P]), bb[:, h, :, :],
                                          ALU.subtract)
                ins.then_inc(gs["D"], 1)
                place(7)
                dve.wait_ge(gs["E"], LEVELS + 1)
                z0 = g_z[0][:, :, :].rearrange("p h (c t) -> p h c t", t=P)
                V.tensor_copy(g_elast[:, :, :], z0[:, :, :, P - 1])
                V.tensor_tensor(g_qd[:, :, :], g_z[0][:, :, :], g_q[:, :, :], ALU.mult).then_inc(gs["qd"], 1)
                dve.wait_ge(gs["E"], LEVELS + 2)
                V.tensor_tensor(g_z[1][:, :, :], g_z[1][:, :, :], g_k[:, :, :], ALU.mult).then_inc(gs["kd"], 1)
                for c in range(TT - 1):
                    for h in range(H4):
                        dve.wait_ge(gs["st"], 2 * c + h // 2 + 1)
                        b = bank[(2 * c + h // 2) % 4][:, h % 2 * GLA_DV:(h % 2 + 1) * GLA_DV]
                        if c == 0:
                            ins = V.tensor_copy(g_state[:, h, :], b)
                        else:
                            if h == 0:
                                dve.wait_ge(gs["state"], 4 * c)
                            ins = V.scalar_tensor_tensor(g_state[:, h, :], g_state[:, h, :], g_elast[:, h, c:c + 1], b,
                                                         ALU.mult, ALU.add)
                        ins.then_inc(gs["state"], 1)
                for h in range(H4):
                    dve.wait_ge(gs["ors"], h + 1)
                    for f in (2 * h, 2 * h + 1):
                        lo_ = COLS["gla_norm"][0] + f
                        own(V.scalar_tensor_tensor(g_o[:, f, :], g_o[:, f, :], par_sb[:, lo_:lo_ + 1], g_ors[:, :],
                                                   ALU.mult, ALU.mult))
                        dve.wait_ge(gs["silu"], f + 1)
                        V.tensor_tensor(g_o[:, f, :], g_o[:, f, :], g_r[:, f, :], ALU.mult).then_inc(gs["ot"], 1)
                    for f in (2 * h, 2 * h + 1):
                        dve.wait_ge(gs["oh"], f + 1)
                        V.tensor_tensor(g_ol[:, f, :], g_o[:, f, :], g_oh[:, f, :].bitcast(F32), ALU.subtract)\
                            .then_inc(gs["ol"], 1)
                projected(1, "gla_o")

            def nsa():
                dve.wait_ge(s_rstd, 3)
                for k in range(KT):
                    dve.wait_ge(ns["xh2"], k + 1)
                    V.scalar_tensor_tensor(XL2[:, k, :], X[:, k, :], gain(KV_MIX_GAIN, k), XH2[:, k, :].bitcast(F32),
                                           ALU.mult, ALU.subtract).then_inc(ns["xl2"], 1)
                u0 = START["kv"]
                pe_in = PAR("pe").rearrange("p (kv i) -> p kv i", kv=2)
                own(V.tensor_copy(n_peh[:, :, :], pe_in))
                V.tensor_tensor(n_pel[:, :, :], pe_in, n_peh[:, :, :].bitcast(F32), ALU.subtract)
                for s in range(2):
                    for y in (n_yh, n_yl):
                        V.memset(y[s][DH:P, T - 1:NSA_KV * T:T].bitcast(F32), 0.0)
                        V.memset(y[s][:, NSA_KV * T:YW].bitcast(F32), 0.0)

                def evac(t):
                    dve.wait_ge(s_used, u0 + t + 1)
                    raw = n_raw[:, t % 2, :]
                    if 2 <= t <= 5:
                        dve.wait_ge(ns["yh"], t - 1)
                    if t in (8, 9):
                        dve.wait_ge(ns["vT"], t - 7)
                    V.tensor_tensor(raw, bank[t % 4][:, :], rstd[:, :], ALU.mult).then_inc(ns["evac"], 1)

                def lower(t):
                    raw = n_raw[:, t % 2, :]
                    dve.wait_ge(ns["evac"], t + 1)
                    own(V.tensor_copy(n_yt_h[:, :], raw))
                    own(V.tensor_tensor(n_yt_l[:, :], raw, n_yt_h[:, :].bitcast(F32), ALU.subtract))
                    for e in range(2):
                        head = 2 * (t % 2) + e
                        r = slice(DH * e, DH * e + DH)
                        V.tensor_copy(n_yl[t // 2][0:DH, head * T:(head + 1) * T], n_yt_l[r, :].bitcast(F32))
                        ins = V.tensor_copy(n_yl[t // 2][DH:P, head * T:(head + 1) * T - 1], n_yt_l[r, 1:T].bitcast(F32))
                    ins.then_inc(ns["yl"], 1)

                def key(t):
                    m = (t - 4) % 4 + 2 * (t // 8)
                    dve.wait_ge(ns["rot"], m + 1)
                    rotate([(n_k[m // 2][d:d + DH, 2 * (m % 2) + e, :], slice(DH * e, DH * e + DH))
                            for e in range(2) for d in (0, DH)], n_raw[:, t % 2, :], 4, ns["rope"])

                for t in range(U_NSA_KV):
                    evac(t)
                    if t < 4:
                        lower(t)
                    if t - 1 in (4, 5, 8, 9):
                        key(t - 1)
                V.memset(n_kc[:, :, :, :], 0.0)
                dve.wait_ge(ns["hTc"], 2)
                V.memset(n_bd[:, :, :, :], 0.0).then_inc(ns["p0"], 1)
                dve.wait_ge(s_used, START["nsa_q"] + 1)
                dve.wait_ge(ns["vT"], 3)
                V.tensor_tensor(n_raw[:, 0, :], bank[0][:, :], rstd[:, :], ALU.mult).then_inc(ns["evac"], 1)
                for par in range(2):
                    ins = V.memset(n_qp[DH * (1 - par):DH * (2 - par), par:NSA_HEADS:2, :], 0.0)

                def query(e):
                    raw = n_raw[:, (e + 1) % 2, :]
                    dve.wait_ge(ns["rot"], 4 + e + 1)
                    if e:
                        dve.wait_ge(ns["rope"], 4 + e)
                    V.tensor_tensor(n_t1[:, :], raw, cos_t, ALU.mult)
                    own(V.tensor_tensor(n_t2[:, :], bank[4][:, :], sin_t, ALU.mult))
                    for par in range(2):
                        r = slice(par * DH, (par + 1) * DH)
                        ins = V.tensor_tensor(n_qp[r, 2 * e + par, :], n_t1[r, :], n_t2[r, :], ALU.add)
                    ins.then_inc(ns["rope"], 1)

                mask = C("cmp_mask").rearrange("p (c n) -> p c n", c=TT)[:, :, None, :].broadcast_to([P, TT, 4, NC_PAD])
                valid = C("cmp_valid")[:, :, None].broadcast_to([P, TT, 4])

                def cmp_scores(rd):
                    s = n_sc[rd % 2][:, :].rearrange("p (c h n) -> p c h n", c=TT, h=4)
                    b = bank[6 + rd % 2][:, :].rearrange("p (c h n) -> p c h n", c=TT, h=4)
                    dve.wait_ge(ns["cs"], 2 * rd + 2)
                    if rd >= 2:
                        dve.wait_ge(ns["pT"], rd - 1)
                    V.tensor_tensor(s, b, mask, ALU.add).then_inc(ns["csub"], 1)
                    dve.wait_ge(ns["csub"], rd + 1)
                    s3 = n_sc[rd % 2][:, :].rearrange("p (m n) -> p m n", n=NC_PAD)
                    own(V.tensor_reduce(n_cst[:, 0, :], s3, AX_X, ALU.max))
                    V.tensor_tensor(s3, s3, n_cst[:, 0, :, None].broadcast_to([P, 16, NC_PAD]), ALU.subtract)\
                        .then_inc(ns["cmax"], 1)

                def cmp_weights(rd):
                    s3 = n_sc[rd % 2][:, :].rearrange("p (m n) -> p m n", n=NC_PAD)
                    dve.wait_ge(ns["ce"], rd + 1)
                    own(V.tensor_reduce(n_cst[:, 1, :], s3, AX_X, ALU.add))
                    own(V.reciprocal(n_cst[:, 2, :], n_cst[:, 1, :]))
                    r4 = n_cst[:, 2, :].rearrange("p (c h) -> p c h", c=TT)
                    own(V.tensor_tensor(r4, r4, n_gate[:, :, 4 * rd:4 * rd + 4], ALU.mult))
                    own(V.tensor_tensor(r4, r4, valid, ALU.mult))
                    V.tensor_tensor(s3, s3, n_cst[:, 2, :, None].broadcast_to([P, 16, NC_PAD]), ALU.mult).then_inc(ns["p"], 1)

                for e in range(8):
                    dve.wait_ge(s_used, START["nsa_q"] + 1 + e + 1)
                    if e == 1:
                        dve.wait_ge(ns["gT"], 1)
                    if e >= 2:
                        dve.wait_ge(ns["cs"], e - 1)
                        dve.wait_ge(ns["rope"], 4 + e - 1)
                    V.scalar_tensor_tensor(n_raw[:, (e + 1) % 2, :], bank[(1 + e) % 4][:, :], QSCALE, rstd[:, :], ALU.mult,
                                           ALU.mult).then_inc(ns["evac"], 1)
                    if e:
                        query(e - 1)
                    if e >= 2:
                        dve.wait_ge(ns["gate"], 1)
                        (cmp_scores if e % 2 == 0 else cmp_weights)(e // 2 - 1)
                query(7)
                cmp_scores(3)
                cmp_weights(3)

                jobs = NSA_HEADS * TT * 2
                for q in range(jobs + 8):
                    if q < jobs:
                        S = (q // 4 % 4 + 1) * P
                        dve.wait_ge(ns["s"], q + 1)
                        V.tensor_reduce(n_st[:, 0, q:q + 1], bank[4 + q % 4][:, 0:S], AX_X, ALU.max, negate=True)\
                            .then_inc(ns["mx"], 1)
                    if 1 <= q <= jobs:
                        m = q - 1
                        e, i, par, c = m // 16, m // 4 % 4, m // 2 % 2, m % 2
                        dve.wait_ge(ns["exp"], m + 1)
                        w = n_P[:, m % 4, 0:(i + 1) * P]
                        col = 16 * (c + 1) + 2 * e + par
                        own(V.reciprocal(n_st[:, 1, m:m + 1], n_st[:, 1, m:m + 1]))
                        V.tensor_scalar(w, w, n_st[:, 1, m:m + 1], n_gate[:, i, col:col + 1], ALU.mult, ALU.mult)\
                            .then_inc(ns["w"], 1)
                    if q >= 22 and (q - 22) % 16 == 0:
                        e = (q - 22) // 16
                        dve.wait_ge(ns["oh"], e + 1)
                        V.tensor_tensor(n_ol[:, e, :], bank[0][:, :], n_oh[:, e, :].bitcast(F32), ALU.subtract)\
                            .then_inc(ns["o"], 1)
                projected(3, "nsa_o", (4, 5, 6, 7))

            def hybrid(ly):
                n0 = HYB_N[ly]
                u0 = START[f"hyb{ly}"]
                lam_init = LAM_INIT[ly]
                lam_in = PAR("lam")[:, 4 * ly:4 * ly + 4]
                V.tensor_tensor(h_lam[:, 0:2], lam_in[:, 0:4:2], lam_in[:, 1:4:2], ALU.mult).then_inc(hs["lp"], 1)
                lo_ = COLS["subln"][0] + ly
                V.tensor_scalar(h_sub[:, ly:ly + 1], par_sb[:, lo_:lo_ + 1], 1.0 - lam_init, None, ALU.mult)
                dve.wait_ge(s_rstd, n0 + 1)

                for c in range(2):
                    other = slice(DH * (1 - c), DH * (2 - c))
                    V.memset(h_dk[other, :, c, :], 0.0)
                    ins = V.memset(h_sk[other, c:SB_HEADS:2, :], 0.0)

                def rot(t):
                    dve.wait_ge(hs["rot"], 8 * ly + t + 1)
                    if t:
                        dve.wait_ge(hs["rope"], 8 * ly + t)
                    V.tensor_tensor(h_t1[:, :], h_raw[:, t % 2, :], cos_t, ALU.mult)
                    own(V.tensor_tensor(h_t2[:, :], bank[4][:, :], sin_t, ALU.mult))
                    if t < 4:
                        ins = V.tensor_tensor(h_dq[:, t, :], h_t1[:, :], h_t2[:, :], ALU.add)
                    else:
                        for c in range(2):
                            r = slice(DH * c, DH * (c + 1))
                            ins = V.tensor_tensor(h_dk[r, t - 4, c, :], h_t1[r, :], h_t2[r, :], ALU.add)
                    ins.then_inc(hs["rope"], 1)

                def evac(t):
                    dve.wait_ge(s_used, u0 + t + 1)
                    b = bank[t % 4 if t < 12 else t % 2]
                    if 16 <= t < 20:
                        for c in range(2):
                            r = slice(DH * c, DH * (c + 1))
                            ins = V.tensor_tensor(h_sk[r, 2 * (t - 16) + c, :], b[r, :], rstd[r, :], ALU.mult)
                        ins.then_inc(hs["evac"], 1)
                        return
                    if t < 12 or 20 <= t < 24:
                        dst = h_raw[:, t % 2, :]
                        if 2 <= t < 10:
                            dve.wait_ge(hs["rope"], 8 * ly + t - 1)
                        if t in (10, 11):
                            dve.wait_ge(hs["vT"], 8 * ly + t - 9)
                        if t >= 20:
                            dve.wait_ge(hs["vT"], 8 * ly + t - 17)
                    elif t < 16:
                        dst = h_sq[:, t - 12, :]
                    else:
                        dst = h_gate[:, t - 24, :]
                    if t < 4 or 12 <= t < 16:
                        ins = V.scalar_tensor_tensor(dst, b[:, :], QSCALE, rstd[:, :], ALU.mult, ALU.mult)
                    else:
                        ins = V.tensor_tensor(dst, b[:, :], rstd[:, :], ALU.mult)
                    ins.then_inc(hs["evac"], 1)

                for t in range(12):
                    evac(t)
                    if 1 <= t <= 8:
                        rot(t - 1)
                    if t == 9:
                        dve.wait_ge(hs["le"], ly + 1)
                        own(V.tensor_tensor(h_lam[:, 4:5], h_lam[:, 3:4], h_lam[:, 2:3], ALU.subtract))
                        V.tensor_scalar(h_lam[:, 5:6], h_lam[:, 4:5], -lam_init, None, ALU.add).then_inc(hs["lam"], 1)

                units = DIFF_HEADS * TT
                q0 = units * ly

                def combine(m):
                    S = (m % TT + 1) * P
                    dve.wait_ge(hs["exp"], 2 * (q0 + m) + 2)
                    if m >= 2:
                        dve.wait_ge(hs["t"], q0 + m - 1)
                    st = h_st[:, 2, 2 * m:2 * m + 2]
                    own(V.reciprocal(st, h_st[:, 1, 2 * m:2 * m + 2]))
                    own(V.tensor_scalar(h_st[:, 3, 2 * m:2 * m + 1], h_st[:, 2, 2 * m + 1:2 * m + 2], h_lam[:, 5:6], None,
                                        ALU.mult))
                    w = h_W[:, m % 2, 0:S]
                    own(V.tensor_scalar(w, h_P[:, 0, 0:S], h_st[:, 2, 2 * m:2 * m + 1], None, ALU.mult))
                    V.scalar_tensor_tensor(w, h_P[:, 1, 0:S], h_st[:, 3, 2 * m:2 * m + 1], w, ALU.mult, ALU.add)\
                        .then_inc(hs["w"], 1)

                def d_out(h):
                    dve.wait_ge(hs["ors"], 4 * ly + h + 1)
                    V.scalar_tensor_tensor(h_od[:, h, :], bank[3][:, :], h_sub[:, ly:ly + 1], h_ors[:, :], ALU.mult, ALU.mult)\
                        .then_inc(hs["od"], 1)

                for n in range(units):
                    S = (n % TT + 1) * P
                    for c in range(2):
                        dve.wait_ge(hs["s"], 2 * (q0 + n) + c + 1)
                        V.tensor_reduce(h_st[:, 0, 2 * n + c:2 * n + c + 1], bank[4 + c][:, 0:S], AX_X,
                                        ALU.max, negate=True).then_inc(hs["mx"], 1)
                    combine(n)
                    if n in FILL:
                        evac(FILL[n])
                    if n >= 6 and (n - 6) % TT == 0:
                        d_out((n - 6) // TT)

                k0 = SB_HEADS * ly
                for h in range(SB_HEADS):
                    if h == 0:
                        dve.wait_ge(hs["pv"], 4 * ly + 4)
                    evac(24 + 2 * h)
                    dve.wait_ge(hs["ln"], k0 + h + 1)
                    sp_ = h_sp[:, h % 2, :]
                    for at_, w, b in ((0, 512, 4), (512, 512, 5), (1024, 256, 7)):
                        ins = V.scalar_tensor_tensor(sp_[:, at_:at_ + w], bank[b][:, 0:w], 0.0, sp_[:, at_:at_ + w],
                                                     ALU.max, ALU.add)
                    own(ins)
                    keep = C("sb_keep")[:, None, :].broadcast_to([P, 2, P])
                    d = sp_[:, 0:1024].rearrange("p (j t) -> p j t", j=2)[:, :, 0:P]
                    V.tensor_tensor(d, d, keep, ALU.mult)
                    d = sp_[:, 896:1152].rearrange("p (j t) -> p j t", j=2)
                    own(V.tensor_tensor(d, d, keep, ALU.mult))
                    if h >= 2:
                        dve.wait_ge(hs["spv"], 4 * ly + h // 2)
                    later = h_a[:, h % 2, :]
                    own(V.tensor_tensor(later[:, 256:384], sp_[:, 1152:1280], sp_[:, 896:1024], ALU.add))
                    V.tensor_tensor(later[:, 0:128], sp_[:, 640:768], sp_[:, 1024:1152], ALU.add)
                    V.tensor_tensor(later[:, 128:256], sp_[:, 768:896], later[:, 256:384], ALU.add).then_inc(hs["sp"], 1)
                    evac(25 + 2 * h)
                    if h == 0:
                        d_out(DIFF_HEADS - 1)

                for k in range(4):
                    dve.wait_ge(hs["odh"], 4 * ly + k + 1)
                    V.tensor_tensor(h_odl[:, k, :], h_od[:, k, :], h_odh[:, k, :].bitcast(F32), ALU.subtract)\
                        .then_inc(hs["odl"], 1)
                for a in range(3):
                    dve.wait_ge(hs["osh"], 4 * ly + a + 1)
                    V.tensor_tensor(h_osl[:, a, :], h_os[:, a, :], h_osh[:, a, :].bitcast(F32), ALU.subtract)\
                        .then_inc(hs["osl"], 1)

                u0 = START[f"merge{ly}"]

                def merged_lo(f):
                    dve.wait_ge(hs["mh"], 8 * ly + f + 1)
                    V.tensor_tensor(h_ml[:, f, :], h_m[:, f % 2, :], h_mh[:, f, :].bitcast(F32), ALU.subtract)\
                        .then_inc(hs["ml"], 1)

                for m in range(2 * KT):
                    f = m % KT
                    if m == 2:
                        dve.wait_ge(hs["osh"], 4 * ly + 4)
                        V.tensor_tensor(h_osl[:, 3, :], bank[2][:, :], h_osh[:, 3, :].bitcast(F32), ALU.subtract)\
                            .then_inc(hs["osl"], 1)
                    if m % 2 == 0:
                        dve.wait_ge(hs["mt"], 8 * ly + m // 2 + 1)
                    else:
                        dve.wait_ge(s_used, u0 + m // 2 + 1)
                    dve.wait_ge(hs["gate"], 16 * ly + m + 1)
                    b = bank[(0, 1, 3, 6)[m % 4]][:, :]
                    if m < KT:
                        V.tensor_tensor(h_mt[:, f, :], b, h_gate[:, f, :], ALU.mult).then_inc(hs["mevac"], 1)
                    else:
                        if f:
                            dve.wait_ge(hs["m"], 8 * ly + f)
                        V.tensor_tensor(h_m2[:, :], b, h_gate[:, m, :], ALU.mult).then_inc(hs["mevac"], 1)
                        dve.wait_ge(hs["mevac"], 16 * ly + m + 1)
                        if f >= 2:
                            dve.wait_ge(hs["ml"], 8 * ly + f - 1)
                        V.tensor_tensor(h_m[:, f % 2, :], h_m2[:, :], h_mt[:, f, :], ALU.add).then_inc(hs["m"], 1)
                        if f:
                            merged_lo(f - 1)
                merged_lo(7)
                projected(n0 + 1, f"out{ly}", (2, 4, 5, 7))

            dve.wait_ge(s_const, 48)
            V.tensor_copy(ident_bf[:, :], ident).then_inc(s_bf, 1)
            V.tensor_copy(masks_bf[:, :, :], masks_in[:, :, :]).then_inc(s_bf, 1)
            for k in range(KT):
                dve.wait_ge(s_xt, k + 1)
                V.tensor_copy(X[:, k, :], bank[k][:, :]).then_inc(s_x, 1)
                if k:
                    lo(0, k - 1)
            lo(0, KT - 1)
            gla()
            ffn(0, 1, "ffn0", 2)
            nsa()
            ffn(1, 3, "ffn1", 4)
            dve.wait_ge(s_rstd, 5)
            for k in range(KT):
                V.scalar_tensor_tensor(X[:, k, :], X[:, k, :], gain(GAIN[4], k), rstd[:, :], ALU.mult, ALU.mult)\
                    .then_inc(s_x, 1)
                if k:
                    lo(5, k - 1)
            lo(5, KT - 1)
            hybrid(0)
            ffn(2, 6, "ffn2", 7)
            hybrid(1)
            ffn(3, 8, "ffn3", 9)
            dve.wait_ge(s_rstd, 10)
            for k in range(KT):
                V.scalar_tensor_tensor(y_fm[:, k, :], X[:, k, :], gain(GAIN[9], k), rstd[:, :], ALU.mult, ALU.mult)\
                    .then_inc(s_y, 1)


def _units(w, cols):
    w = np.ascontiguousarray(w[:, :cols])
    return w.reshape(KT, P, cols // P, P).transpose(2, 1, 0, 3)


def _row_units(w):
    return w.reshape(w.shape[0] // P, P, KT, P)


def _padded(w):
    return np.concatenate([w, np.zeros((w.shape[0], P - w.shape[1]), w.dtype)], axis=1)


def lay_out(a):
    def pairs(w):
        return np.stack([w[..., :FFN].reshape(*w.shape[:-1], FT, P), w[..., FFN:].reshape(*w.shape[:-1], FT, P)], axis=-2)\
            .reshape(*w.shape[:-1], 2 * FFN)

    def ffn(up, down):
        return [_units(pairs(up), 2 * FFN), _row_units(down)]

    def half_units(w):
        return w.reshape(4, P, 4, 2, P).transpose(2, 1, 3, 0, 4).reshape(4, P, KT, P)

    g = a["gla_w_in"][0]
    qk, kv, r0, a0 = 512, 1024, 2048, 3072
    low = np.concatenate([np.zeros((D, P - GLA_RANK), g.dtype), g[:, a0:]], axis=1)
    units = [_units(low, P), _units(g[:, :a0], a0), _units(a["gla_w_o"][0], D)]
    units += ffn(a["ffn_w_up"][0], a["ffn_w_down"][0])
    units += [_units(a["nsa_w_kv"], 1536)]
    for w in (a["cmp_k_w1"], a["cmp_v_w1"]):
        units.append(w.reshape(4, 4, P, CMP_HIDDEN).transpose(0, 2, 1, 3).reshape(4, P, KT, P))
    w = a["nsa_w_in"][0]
    units += [_units(_padded(w[:, D:]), P), _units(w, D), _units(a["nsa_w_o"][0], D)]
    units += ffn(a["ffn_w_up"][1], a["ffn_w_down"][1])
    for ly in range(2):
        units.append(_units(a["w_in_2"][ly], U_HYB * P))
        units += [half_units(a["w_o_diff_2"][ly]), half_units(a["w_o_sb_2"][ly])]
        units.append(_units(a["w_out_2"][ly], D))
        units += ffn(a["w_ffn_in_2"][ly], a["w_ffn_out_2"][ly])
    stream = np.concatenate(units)
    assert stream.shape == (UNITS, P, KT, P), stream.shape

    params = np.zeros((P, N_COLS), np.float32)

    def put(name, x):
        lo, hi = COLS[name]
        params[:, lo:hi] = x.reshape(P, hi - lo)

    def cols(v):
        return np.moveaxis(v.reshape(*v.shape[:-1], -1, P), -1, 0)

    gains = np.stack([a["norm_mix"][0], a["norm_ffn"][0], a["kv_norm"], a["norm_mix"][1], a["norm_ffn"][1], a["norm_final"],
                      a["norm_attn_2"][0], a["norm_ffn_2"][0], a["norm_attn_2"][1], a["norm_ffn_2"][1],
                      a["norm_final_2"]])
    put("gain", cols(gains))
    put("conv_w", cols(pairs(a["ffn_conv_w"])))
    put("conv_b", cols(pairs(a["ffn_conv_b"])))
    put("b_gate", cols(a["b_gate_2"]))
    put("subln", cols(a["diff_subln_2"]))
    put("gla_norm", cols(a["gla_norm"][0]))
    up = np.zeros((P, 512), np.float32)
    up[0] = a["gla_b_alpha"][0]
    up[P - GLA_RANK:] = a["gla_w_alpha_up"][0]
    put("w_alpha", up)
    pe = np.stack([a["cmp_pe_k"], a["cmp_pe_v"]])
    pe = pe.reshape(2, 16, P).transpose(2, 0, 1)
    put("pe", pe)
    w2 = a["cmp_k_w2"].reshape(2, P, DH).transpose(1, 0, 2)
    put("w2k", np.concatenate([w2, w2], axis=-1))
    put("w2v", a["cmp_v_w2"].reshape(2, P, DH).transpose(1, 0, 2))
    lam = np.zeros((P, 8), np.float32)
    lam[:DH] = a["diff_lambda_2"].transpose(2, 0, 1).reshape(DH, 8)
    put("lam", lam)
    return stream, params


def kernel(**inputs):
    import concourse.bacc as _bacc
    from concourse.bass_utils import run_bass_kernel_spmd as _run

    a = {n: np.asarray(v) for n, v in inputs.items()}
    stream, params = lay_out(a)
    tables, masks = constants()
    arrays = {"x_dram": np.ascontiguousarray(a["x"]), "weights_dram": stream, "params_dram": params,
              "consts_dram": tables, "masks_dram": masks}
    nc = _bacc.Bacc("TRN2", target_bir_lowering=False, num_devices=1)
    args = [nc.dram_tensor(n, v.shape, mybir.dt.from_np(v.dtype), kind="ExternalInput").ap() for n, v in arrays.items()]
    args.append(nc.dram_tensor("out_dram", (1, T, D), F32, kind="ExternalOutput").ap())
    build(nc, *args)
    r = _run(nc, [arrays], core_ids=[0])
    return r.results[0]["out_dram"]
```

```python
from contextlib import ExitStack

import numpy as np

import concourse.bass as bass
from concourse import mybir

ALU = mybir.AluOpType
ACT = mybir.ActivationFunctionType
F32 = mybir.dt.float32
F32R = mybir.dt.float32r
BF16 = mybir.dt.bfloat16
U16 = mybir.dt.uint16
AX_X = mybir.AxisListType.X

P = 128
T = 512
D = 1024
KT = D // P
TT = T // P
FFN = 2816
FT = FFN // P
EPS = 1e-6
NEG = -1e30

GLA_HEADS, GLA_DK, GLA_DV, GLA_TAU, GLA_RANK = 4, 128, 256, 16.0, 16
LEVELS = 7
NSA_HEADS, NSA_KV, DH = 16, 4, 64
CMP_BLOCK, CMP_STRIDE, CMP_HIDDEN = 32, 16, 256
N_CMP = (T - CMP_BLOCK) // CMP_STRIDE + 1
NC_PAD = 32
YW = NSA_KV * T + CMP_STRIDE
DIFF_HEADS, SB_HEADS = 4, 8
QSCALE = DH ** -0.5

SBUF_WORDS = 53200
RING = 4
UNIT = KT * P

U_GLA = 1 + 4 + 4 + 8 + 8
U_FFN = 2 * FT + FT
U_NSA_KV = 12
U_CMP = 8
U_NSA_Q = 1 + 8
U_HYB = 40
U_MERGE = 8
U_RES = 8

START = {}
_u = 0
for _name, _n in (("gla", U_GLA), ("gla_o", U_RES), ("ffn0", U_FFN), ("kv", U_NSA_KV), ("cmp", U_CMP),
                  ("nsa_q", U_NSA_Q), ("nsa_o", U_RES), ("ffn1", U_FFN),
                  ("hyb0", U_HYB), ("merge0", U_MERGE), ("out0", U_RES), ("ffn2", U_FFN),
                  ("hyb1", U_HYB), ("merge1", U_MERGE), ("out1", U_RES), ("ffn3", U_FFN)):
    START[_name] = _u
    _u += _n
UNITS = _u

COLS = {}
_c = 0
for _name, _n in (("gain", 11 * KT), ("conv_w", 2 * 3 * 2 * FT), ("conv_b", 2 * 2 * FT), ("b_gate", 2 * 16),
                  ("subln", 2), ("gla_norm", 8), ("w_alpha", 512), ("pe", 2 * 16), ("w2k", 256),
                  ("w2v", 128), ("lam", 2 * 4)):
    COLS[_name] = (_c, _c + _n)
    _c += _n
N_COLS = _c

CONST = {}
_c = 0
for _name, _n in (("ident", P), ("ones", P), ("eps", 1), ("one", 1), ("cum", P), ("negtri", P), ("negones", P),
                  ("cos", T), ("sin", T), ("sb_keep", P),
                  ("cmp_mask", TT * NC_PAD), ("cmp_valid", TT)):
    CONST[_name] = (_c, _c + _n)
    _c += _n
N_CONST = _c
MASKS = 10


def constants():
    out = np.zeros((P, N_CONST), np.float32)

    def put(name, a):
        lo, hi = CONST[name]
        out[:, lo:hi] = np.asarray(a, np.float32).reshape(P, hi - lo)

    a, b = np.arange(P)[:, None], np.arange(P)[None, :]
    put("ident", a == b)
    put("ones", np.ones((P, P)))
    put("cum", (a <= b) / GLA_TAU)
    put("negtri", -1.0 * (a >= b))
    put("negones", -np.ones((P, P)))
    half = DH // 2
    inv = np.float32(10000.0) ** (-np.arange(half, dtype=np.float32) / np.float32(half))
    ang = (np.arange(T, dtype=np.float32)[:, None] * inv[None, :]).astype(np.float32)
    put("cos", np.cos(ang).T[np.arange(P) % half])
    put("sin", np.sin(ang).T[np.arange(P) % half] * np.where(np.arange(P) % DH < half, -1.0, 1.0)[:, None])
    lv = np.zeros((P, 8, P))
    for n in range(LEVELS):
        h = P >> (n + 1)
        lv[:, n] = (a // (2 * h) == b // (2 * h)) & ((a // h) % 2 == 0) & ((b // h) % 2 == 1)
    lv[:, 7] = a == b
    masks = np.concatenate([lv, np.where(b <= a, 0.0, NEG)[:, None], np.where(a < b, 0.0, NEG)[:, None]], axis=1)
    put("sb_keep", a < b)
    n = np.arange(NC_PAD)
    pos = np.arange(TT)[None, :, None] * P + np.arange(P)[:, None, None]
    seen = (n * CMP_STRIDE + CMP_BLOCK - 1 <= pos) & (n < N_CMP)
    put("cmp_mask", np.where(seen, 0.0, NEG))
    put("cmp_valid", seen.any(-1))
    put("eps", np.full((P, 1), EPS))
    put("one", np.ones((P, 1)))
    return out, masks.astype(np.float32)


def build(nc, x_in, weights, params, consts, masks, gain_out, out):
    ctx = ExitStack()
    with ctx:
        def sem(name):
            return ctx.enter_context(nc.semaphore(name))

        top = [0]

        def at(name, shape, dt, offset):
            return nc.alloc_sbuf_tensor_at(name, shape, dt, offset=first_byte + 4 * offset)

        def words(n):
            lo = top[0]
            top[0] += -(-n // 8) * 8
            return lo

        first_byte = -(-nc.sbuf_base // 32) * 32
        ctx.enter_context(nc.sbuf_tensor("all_of_sbuf", [P, SBUF_WORDS], F32))
        o_X = words(KT * T)
        o_XH = words(KT * T)
        o_XL = words(KT * T)
        o_ring = words(RING * 2 * UNIT)
        o_const = words(N_CONST)
        o_par = words(N_COLS)
        o_rstd = words(T)
        o_ss = words(T)
        o_sq = words(2 * T)
        o_small = words(800)
        o_masks = words(MASKS * P // 2)
        o_A = words(0)
        HID = FT * T
        assert o_A + 25690 <= SBUF_WORDS, o_A

        X = at("X", [P, KT, T], F32, o_X)
        XH = at("XH", [P, KT, T], F32R, o_XH)
        XL = at("XL", [P, KT, T], F32R, o_XL)
        w_raw = [at(f"w_raw{s}", [P, KT, P], F32, o_ring + 2 * s * UNIT) for s in range(RING)]
        w_lo = [at(f"w_lo{s}", [P, KT, P], F32R, o_ring + 2 * s * UNIT) for s in range(RING)]
        w_hi = [at(f"w_hi{s}", [P, KT, P], F32R, o_ring + (2 * s + 1) * UNIT) for s in range(RING)]
        const_sb = at("const_sb", [P, N_CONST], F32, o_const)
        par_sb = at("par_sb", [P, N_COLS], F32, o_par)
        rstd = at("rstd", [P, T], F32, o_rstd)
        ss = at("ss", [P, T], F32, o_ss)
        sq = at("sq", [P, 2, T], F32, o_sq)
        o_s = [o_small]

        def small(name, shape, dt=F32):
            n = int(np.prod(shape[1:])) * (2 if dt == BF16 else 4) // 4
            t = at(name, shape, dt, o_s[0])
            o_s[0] += (n + 7) // 8 * 8
            assert o_s[0] <= o_small + 800
            return t

        masks_bf = at("masks_bf", [P, MASKS, P], BF16, o_masks)
        causal_bf, sb_neg_bf = masks_bf[:, 8, :], masks_bf[:, 9, :]
        ident_bf = small("ident_bf", [P, P], BF16)

        def query_tile(job):
            return (0, 3, 1, 2)[job // 4 % TT]

        def C(name):
            lo, hi = CONST[name]
            return const_sb[:, lo:hi]

        def PAR(name):
            lo, hi = COLS[name]
            return par_sb[:, lo:hi]

        ident, ones_m, cos_t, sin_t = C("ident"), C("ones"), C("cos"), C("sin")
        negtri, negones = C("negtri"), C("negones")

        def gain(n, k):
            lo = COLS["gain"][0] + n * KT + k
            return par_sb[:, lo:lo + 1]

        def parts_gain(n, k):
            return mid_gain[:, k:k + 1] if n == MID else gain(GAIN[n], k)

        eps_col, one_col = C("eps"), C("one")

        hid_h = at("hid_h", [P, FT * T], F32R, o_A)
        hid_l = at("hid_l", [P, FT * T], F32R, o_A + HID)
        o_T = o_A + 2 * HID
        f_u = [at(f"f_u{s}", [P, T + 2], F32, o_T + s * 520) for s in range(2)]
        f_c = [at(f"f_c{s}", [P, T], F32, o_T + 1040 + s * T) for s in range(2)]
        f_s = at("f_s", [P, T], F32, o_T + 1040 + 2 * T)
        f_h = at("f_h", [P, T], F32, o_T + 1040 + 3 * T)

        x_tok = at("x_tok", [P, TT, D], F32, o_A)
        masks_in = at("masks_in", [P, MASKS, P], F32, o_A + 8192)
        y_tok = at("y_tok", [P, TT, D], F32, o_A + 8192)
        y_gain = at("y_gain", [P, D], F32, o_T)

        H4 = GLA_HEADS
        g_q = at("g_q", [P, H4, T], F32, o_A)
        g_k = at("g_k", [P, H4, T], F32, o_A + 2048)
        g_b = at("g_b", [P, H4, T], F32, o_A + 4096)
        g_z = [at(f"g_z{s}", [P, H4, T], F32, o_A + 6144 + 2048 * s) for s in range(2)]
        g_v = at("g_v", [P, TT, D], F32, o_A + 10240)
        g_a = at("g_a", [P, T], F32, o_A + 10240)
        g_r = at("g_r", [P, 8, T], F32, o_A + 14336)
        g_vt = at("g_vt", [P, 2, T], F32, o_A + 14336 + 6 * T)
        g_g = at("g_g", [P, TT, T], F32, o_A + 18432)
        g_att = at("g_att", [P, TT, H4, P], F32, o_A + 18432)
        g_state = at("g_state", [P, H4, GLA_DV], F32, o_A + 20480)
        g_kdT = at("g_kdT", [P, TT - 1, H4, P], F32, o_A + 21504)
        g_qd = at("g_qd", [P, H4, T], F32, o_A + 23040)
        g_elast = small("g_elast", [P, H4, TT])
        g_o = at("g_o", [P, 8, T], F32, o_A)
        g_oh = at("g_oh", [P, 8, T], F32R, o_A + 4096)
        g_ol = at("g_ol", [P, 8, T], F32R, o_A + 8192)
        g_osq = at("g_osq", [P, 8, T], F32, o_A + 18432)
        g_ors = at("g_ors", [P, H4, T], F32, o_A + 23040)

        XH2 = at("XH2", [P, KT, T], F32R, o_A + 14592)
        XL2 = at("XL2", [P, KT, T], F32R, o_A + 14592 + 4096)
        n_yh = [at(f"n_yh{s}", [P, YW], F32R, o_A + s * YW) for s in range(2)]
        n_yl = [at(f"n_yl{s}", [P, YW], F32R, o_A + (2 + s) * YW) for s in range(2)]
        n_k = [at(f"n_k{s}", [P, NSA_KV, T], F32, o_A + 8448 + 2048 * s) for s in range(2)]
        n_v = [at(f"n_v{s}", [P, TT, NSA_KV * DH], F32, o_A + 12544 + 1024 * s) for s in range(2)]
        o_N = o_A + 22784
        n_raw = at("n_raw", [P, 2, T], F32, o_N)
        n_t1 = at("n_t1", [P, T], F32, o_sq)
        n_t2 = at("n_t2", [P, T], F32, o_sq + T)
        n_yt_h = at("n_yt_h", [P, T], F32R, o_sq)
        n_yt_l = at("n_yt_l", [P, T], F32R, o_sq + T)
        n_qp = at("n_qp", [P, NSA_HEADS, T], F32R, o_XH)
        n_kl = [at(f"n_kl{s}", [P, NSA_KV, T], F32R, o_A + 8448 + 2048 * s) for s in range(2)]
        n_kh = [[at(f"n_kh{s}{g}", [P, T], F32R, o) for g, o in enumerate(places)] for s, places in enumerate((
            (o_ss, o_A + 15616 + 4 * T, o_A + 15616 + 6 * T, o_rstd),
            (o_A + 15616 + 2 * T, o_A + 15616 + 5 * T, o_A + 15616 + 7 * T, o_sq)))]
        n_hT = at("n_hT", [P, 2, CMP_HIDDEN], F32, o_N + 1024)
        n_hid = at("n_hid", [P, 2, 2, P], F32, o_N + 2048)
        n_kc = small("n_kc", [P, NSA_KV, 2, NC_PAD])
        n_bd = at("n_bd", [P, NSA_KV, 2, P], F32, o_N + 1024)
        n_peh = at("n_peh", [P, 2, 16], F32R, o_N + 2560)
        n_pel = at("n_pel", [P, 2, 16], F32R, o_N + 2592)
        n_gate = at("n_gate", [P, TT, 48], F32, o_N + 2624)
        n_st = at("n_st", [P, 2, P], F32, o_N + 2048)
        n_PT = at("n_PT", [P, 2, 4, TT, P], F32, o_A)
        n_P = [at(f"n_P{s}", [P, T], F32, o_A + 4096 + s * T if s < 4 else o_A + 14592 + (s - 4) * T) for s in range(6)]
        n_sc = [at(f"n_sc{s}", [P, T], F32, o_A + 2048 + s * T) for s in range(2)]
        n_pcT = at("n_pcT", [P, 4, T], F32, o_A + 6144)
        n_cst = small("n_cst", [P, 3, 16])
        n_oh = at("n_oh", [P, 8, T], F32R, o_A + 15616)
        n_ol = at("n_ol", [P, 8, T], F32R, o_A + 15616 + 4096)

        h_dq = at("h_dq", [P, 4, T], F32, o_A)
        h_dk = at("h_dk", [P, 4, 2, T], F32, o_A + 2048)
        h_dv = at("h_dv", [P, TT, T], F32, o_A + 6144)
        h_gate = at("h_gate", [P, 16, T], F32, o_A)
        h_sq = at("h_sq", [P, 4, T], F32, o_A + 8192)
        h_sk = at("h_sk", [P, SB_HEADS, T], F32, o_A + 10240)
        h_sv = at("h_sv", [P, TT, T], F32, o_A + 14336)
        h_od = at("h_od", [P, 4, T], F32, o_A + 16384)
        h_os = at("h_os", [P, 4, T], F32, o_A + 18432)
        o_H = o_A + 20480
        h_raw = at("h_raw", [P, 2, T], F32, o_H)
        h_P = at("h_P", [P, 2, T], F32, o_H + 1024)
        h_W = at("h_W", [P, 2, T], F32, o_H + 2048)
        h_WT = at("h_WT", [P, TT, T], F32, o_H + 3072)
        h_sp = at("h_sp", [P, 2, 1280], F32, o_H)
        h_a = at("h_a", [P, 2, 1280], F32, o_H + 2560)
        h_sp_lo = at("h_sp_lo", [P, 2, 1280], F32R, o_H)
        h_later_lo = at("h_later_lo", [P, 2, 1280], F32R, o_H + 2560)
        h_later_hi = at("h_later_hi", [P, 2, 1280], F32R, o_H + 2560)
        h_sp_hi = [at(f"h_sp_hi{s}", [P, 1280], F32R, o) for s, o in enumerate((o_A + 18432 + T, o_ss))]
        negtri_r = small("negtri_r", [P, P], F32R)
        negones_r = small("negones_r", [P, P], F32R)
        h_t2 = n_t2
        h_osq = at("h_osq", [P, T], F32, o_sq)
        h_ors = at("h_ors", [P, T], F32, o_sq + T)
        h_m = at("h_m", [P, 2, T], F32, o_sq)
        h_st = small("h_st", [P, 4, 32])
        h_lam = small("h_lam", [P, 8])
        h_sub = small("h_sub", [P, 2])
        mid_gain = small("mid_gain", [P, KT])
        mid_ss = at("mid_ss", [P, T], F32, o_T)
        mid_r = at("mid_r", [P, T], F32, o_T + T)
        h_odh = at("h_odh", [P, 4, T], F32R, o_XH)
        h_odl = at("h_odl", [P, 4, T], F32R, o_XH + 2048)
        h_osh = at("h_osh", [P, 4, T], F32R, o_XL)
        h_osl = at("h_osl", [P, 4, T], F32R, o_XL + 2048)
        h_mt = at("h_mt", [P, 8, T], F32, o_H)
        h_m2 = at("h_m2", [P, T], F32, o_H + 4096)
        h_mh = at("h_mh", [P, 8, T], F32R, o_A + 8192)
        h_ml = at("h_ml", [P, 8, T], F32R, o_A + 12288)

        bank = [ctx.enter_context(nc.psum_tensor(f"bank{b}", [P, T], F32)) for b in range(8)]

        s_gain = sem("gains_in")
        s_ident = sem("ident_ones_eps_in")
        s_const = sem("const_in")
        s_masks = sem("masks_in")
        s_xin = [sem(f"x_in{c}") for c in range(TT)]
        s_bf = sem("masks_bf16_ready")
        s_raw = [sem(f"unit_in{s}") for s in range(RING)]
        s_hi = sem("w_hi_ready")
        s_w = sem("unit_split")
        s_used = sem("unit_used")
        s_xt = sem("xT_ready")
        s_x = sem("x_written")
        s_sq = sem("sq_ready")
        s_xh = sem("xh_ready")
        s_xl = sem("xl_ready")
        s_ss = sem("sumsq_step")
        s_stat = sem("sumsq_ready")
        s_rln = sem("rstd_ln_ready")
        s_rstd = sem("rstd_ready")
        s_mid = sem("mid_sum_scaled")
        s_res = sem("down_tile_ready")
        s_dve = sem("dve_step")
        s_act = sem("act_step")
        s_u, s_c0, s_c1, s_c2, s_silu, s_h, s_hh, s_hl = (sem("ffn_" + n) for n in (
            "u_ready", "tap2_ready", "tap1_ready", "conv_ready", "silu_ready", "h_ready", "hid_hi_ready", "hid_ready"))
        s_ygain, s_yt, s_y, s_out = (sem("out_" + n) for n in ("gain_in", "xT_ready", "y_ready", "stored"))
        gs = {n: sem("gla_" + n) for n in (
            "evac", "vT", "vc", "silu", "apre", "soft", "g", "cum", "b", "D", "E", "Z", "mm", "ev", "qd", "kd", "kdT",
            "kdc", "o", "oc", "st", "state", "osq", "on", "ors", "ot", "oh", "ol")}
        ns = {n: sem("nsa_" + n) for n in (
            "xh2", "xl2", "kh", "kl", "evac", "yh", "yl", "rot", "rope", "vT", "vc", "hid", "hT", "hTc", "kvc", "kvcc", "gT",
            "gate", "p0", "cs", "csub", "cmax", "ce", "p", "s", "mx", "exp", "w", "t", "tc", "pT", "pTc", "pv", "oh", "o")}
        hs = {n: sem("hyb_" + n) for n in (
            "evac", "rot", "rope", "vT", "vc", "gate", "lp", "lsum", "le", "lam", "s", "mx", "exp", "w", "t", "tc", "pv",
            "osq", "on", "ors", "od", "odh", "odl", "z", "ln", "soft", "sphi", "sp", "cum", "a", "spv", "osc", "osh", "osl", "mevac", "mt", "m", "mh",
            "ml")}

        block = ctx.enter_context(nc.Block())

        MID = 4
        PREP = {0: 0, 1: 1, 2: 2, 3: 3, MID: 4, 6: 5, 7: 6, 8: 7}
        GAIN = {0: 0, 1: 1, 2: 2, 3: 4, 4: 5, 5: 6, 6: 7, 7: 8, 8: 9, 9: 10}
        KV_MIX_GAIN = 3
        DOWN_TILES = KT - 1
        HYB_N = (5, 7)
        LAM_INIT = [0.8 - 0.6 * float(np.exp(-0.3 * layer)) for layer in range(2)]
        FILL = {(KT * i + 7) // 6: 12 + i for i in range(12)}
        SB_AT = [0, 512, 1024, 896]
        SB_W = [T - P * j for j in range(TT)]

        def fill_bank(t):
            return t % 2 if t < 26 else 7 if t == U_HYB - 1 else 0

        SB_BANKS = ((4, 5, 7), (3, 6, 1))


        @block.sync
        def _(sp):
            first, gains = CONST["cum"][0], COLS["gain"][1]
            sp.dma_start(const_sb[:, 0:first], consts[:, 0:first]).then_inc(s_ident, 16)
            for c in range(TT):
                sp.dma_start(x_tok[:, c, :], x_in[0, c * P:(c + 1) * P, :]).then_inc(s_xin[c], 16)
            sp.dma_start(par_sb[:, 0:gains], params[:, 0:gains]).then_inc(s_gain, 16)
            for u in range(min(RING, UNITS)):
                sp.dma_start(w_raw[u][:, :, :], weights[u]).then_inc(s_raw[u], 16)
            sp.dma_start(par_sb[:, gains:N_COLS], params[:, gains:N_COLS]).then_inc(s_const, 16)
            sp.dma_start(const_sb[:, first:N_CONST], consts[:, first:N_CONST]).then_inc(s_const, 16)
            sp.dma_start(masks_in[:, :, :], masks).then_inc(s_masks, 16)
            rounds = UNITS // RING
            with sp.Fori(1, rounds) as i:
                for s in range(RING):
                    sp.wait_ge(s_used, i * RING + (s + 1 - RING))
                    sp.dma_start(w_raw[s][:, :, :],
                                 weights[bass.ds(i * RING + s, 1)].rearrange("a p k c -> p (a k) c"))\
                        .then_inc(s_raw[s], 16)
            for u in range(rounds * RING, UNITS):
                sp.wait_ge(s_used, u - RING + 1)
                sp.dma_start(w_raw[u % RING][:, :, :], weights[u]).then_inc(s_raw[u % RING], 16)
            sp.wait_ge(s_hl, 4 * FT)
            sp.dma_start(y_gain[:, :], gain_out.broadcast_to([P, D])).then_inc(s_ygain, 16)
            for c in range(TT):
                sp.wait_ge(s_y, 2 * c + 2)
                sp.dma_start(out[0, c * P:(c + 1) * P, :], y_tok[:, c, :]).then_inc(s_out, 16)
            sp.wait_ge(s_out, 16 * TT)

        @block.gpsimd
        def _(pool):
            pool.wait_ge(s_ident, 16)
            ones_unit = ones_m[:, None, :].broadcast_to([P, KT, P])

            def split(s, landed, hi):
                pool.wait_ge(s_raw[s], landed)
                nc.gpsimd.tensor_tensor(w_hi[s][:, :, :], w_raw[s][:, :, :], ones_unit, ALU.mult).then_inc(s_hi, 1)
                pool.wait_ge(s_hi, hi)
                nc.gpsimd.tensor_tensor(w_lo[s][:, :, :], w_raw[s][:, :, :], w_hi[s][:, :, :].bitcast(F32),
                                        ALU.subtract).then_inc(s_w, 1)

            rounds = UNITS // RING
            with pool.Fori(0, rounds) as i:
                for s in range(RING):
                    split(s, i * 16 + 16, i * RING + (s + 1))
            for u in range(rounds * RING, UNITS):
                split(u % RING, 16 * (u // RING + 1), u + 1)

        @block.tensor
        def _(pe):
            def product(out_ap, slot, j, xh, xl, start, stop):
                nc.tensor.matmul(out_ap, w_hi[slot][:, j, :], xh, start=start, stop=False)
                nc.tensor.matmul(out_ap, w_hi[slot][:, j, :], xl, start=False, stop=False)
                return nc.tensor.matmul(out_ap, w_lo[slot][:, j, :], xh, start=False, stop=stop)

            def tile(u, b, xh, xl, k_sem=None, k_base=0):
                pe.wait_ge(s_w, u + 1)
                for k in range(KT):
                    if k_sem is not None:
                        pe.wait_ge(k_sem, k_base + k + 1)
                    mm = product(bank[b][:, :], u % RING, k, xh[:, k, :], xl[:, k, :], k == 0, k == KT - 1)
                mm.then_inc(s_used, 1)

            def stats(n):
                pe.wait_ge(s_ss, 8 * n + 8)
                nc.tensor.matmul(bank[7][:, :], ones_m, ss[:, :], start=True, stop=True).then_inc(s_stat, 1)

            def turn(b, src, done):
                for c in range(TT):
                    mm = nc.tensor.transpose(bank[b][:, c * P:(c + 1) * P], src[:, c * P:(c + 1) * P], ident)
                mm.then_inc(done, 1)

            def residual(n, name, xh, xl, k_sem, k_base, banks=(0, 1, 2, 3)):
                for f in range(KT):
                    if f >= 4:
                        pe.wait_ge(s_x, 8 * n + f - 3)
                    tile(START[name] + f, banks[f % 4], xh, xl, k_sem if f == 0 else None, k_base)

            def ffn(fi, n, name):
                u0 = START[name]
                xl_base = 8 * PREP[n]
                pe.wait_ge(s_x, 8 * n + 5)

                def up_tile(t, wait_u, first):
                    pe.wait_ge(s_w, wait_u)
                    for k in range(KT):
                        if first:
                            pe.wait_ge(s_xl, xl_base + k + 1)
                        mm = product(bank[t][:, :], (u0 + t) % RING, k, XH[:, k, :], XL[:, k, :], k == 0, k == KT - 1)
                    mm.then_inc(s_used, 1)

                for t in range(4):
                    up_tile(t, u0 + t + 1, t == 0)
                    if t == 0:
                        stats(n)
                with pe.Fori(1, 2 * FT // 4) as i:
                    for t in range(4):
                        pe.wait_ge(s_u, i * 4 + (2 * FT * fi + t - 3))
                        up_tile(t, i * 4 + (u0 + t + 1), False)

                d0 = u0 + 2 * FT
                tail = 4
                head = (FT - tail) % RING

                def down_unit(slot, wait_u, wait_h, xh, xl, start):
                    pe.wait_ge(s_w, wait_u)
                    pe.wait_ge(s_hl, wait_h)
                    for f in (4, 5, 6, 7, 0, 1, 2, 3):
                        if start and f == 0:
                            pe.wait_ge(s_u, 2 * FT * (fi + 1))
                        mm = product(bank[f][:, :], slot, f, xh, xl, start, False)
                    mm.then_inc(s_used, 1)

                for j in range(head):
                    down_unit((d0 + j) % RING, d0 + j + 1, FT * fi + j + 1, hid_h[:, j * T:(j + 1) * T], hid_l[:, j * T:(j + 1) * T], j == 0)
                with pe.Fori(0, (FT - tail) // RING) as i:
                    for s in range(RING):
                        j0 = head + s
                        cols = bass.ds(i * (RING * T) + j0 * T, T)
                        down_unit((d0 + j0) % RING, i * RING + (d0 + j0 + 1), i * RING + (FT * fi + j0 + 1),
                                  hid_h[:, cols], hid_l[:, cols], False)
                def part(f, js, stop):
                    for j in js:
                        mm = product(bank[f][:, :], (d0 + j) % RING, f, hid_h[:, j * T:(j + 1) * T], hid_l[:, j * T:(j + 1) * T],
                                     False, stop and j == js[-1])
                    return mm

                def prepared(js):
                    for j in js:
                        pe.wait_ge(s_w, d0 + j + 1)
                        pe.wait_ge(s_hl, FT * fi + j + 1)

                first, second = range(FT - tail, FT - 2), range(FT - 2, FT)
                prepared(first)
                for f in (4, 5, 6, 7, 0, 1):
                    part(f, first, False)
                prepared(second)
                for f in (0, 1):
                    part(f, second, True).then_inc(s_res, 1)
                part(2, range(FT - tail, FT), True).then_inc(s_res, 1)
                for j in first:
                    part(3, (j,), False).then_inc(s_used, 1)
                for f in (3, 4, 5, 6):
                    part(f, second, True).then_inc(s_res, 1)
                for j in second:
                    part(7, (j,), j == FT - 1).then_inc(s_used, 1)

            def gla():
                u0 = START["gla"]
                def level(lv):
                    pe.wait_ge(gs["Z"], lv + 1)
                    for pair in range(2):
                        m = 2 * lv + pair
                        if m >= 3:
                            pe.wait_ge(gs["ev"], 2 * m - 4)
                        for c in (2 * pair, 2 * pair + 1):
                            for h in range(H4):
                                z = g_z[lv % 2][:, h, c * P:(c + 1) * P]
                                odd = z.rearrange("p (n two e) -> p n two e", two=2, e=P >> (lv + 1))[:, :, 1, :]
                                to = c % 2 * 2 * P + h * P // 2
                                mm = nc.tensor.matmul(bank[5 + m % 3][:, to:to + P // 2], z, odd, start=True, stop=True)
                        mm.then_inc(gs["mm"], 1)

                def diagonal():
                    for c in range(TT):
                        m = 2 * LEVELS + c
                        pe.wait_ge(gs["ev"], 2 * m - 4 if c < 3 else 4 * LEVELS + 1)
                        for h in range(H4):
                            cols = slice(c * P, (c + 1) * P)
                            mm = nc.tensor.matmul(bank[5 + m % 3][:, h * P:(h + 1) * P], g_k[:, h, cols], g_q[:, h, cols],
                                                  start=True, stop=True)
                        mm.then_inc(gs["mm"], 1)

                def v_turn(f):
                    pe.wait_ge(gs["evac"], 9 + f + 1)
                    pe.wait_ge(gs["vc"], f) if f else pe.wait_ge(gs["b"], H4)
                    turn(4, g_vt[:, f % 2, :], gs["vT"])

                def end_keys():
                    pe.wait_ge(gs["kd"], 1)
                    pe.wait_ge(gs["evac"], 16)
                    pe.wait_ge(gs["ev"], 8 * TT)
                    for c, b in enumerate((2, 3, 6)):
                        for h in range(H4):
                            mm = nc.tensor.transpose(bank[b][:, h * P:(h + 1) * P], g_z[1][:, h, c * P:(c + 1) * P], ident)
                        mm.then_inc(gs["kdT"], 1)

                def outputs(c):
                    if c:
                        pe.wait_ge(gs["state"], 4 * c)
                    else:
                        pe.wait_ge(gs["vc"], 8)
                        pe.wait_ge(gs["qd"], 1)
                    for hp in range(2):
                        m = 2 * c + hp
                        if m >= 4:
                            pe.wait_ge(gs["oc"], m - 3)
                        for q in range(4):
                            h, dv = 2 * hp + q // 2, q % 2
                            vc = slice(h * GLA_DV + dv * P, h * GLA_DV + (dv + 1) * P)
                            o = bank[4 + m % 4][:, q * P:(q + 1) * P]
                            mm = nc.tensor.matmul(o, g_v[:, c, vc], g_att[:, c, h, :], start=True, stop=c == 0)
                            if c:
                                mm = nc.tensor.matmul(o, g_state[:, h, dv * P:(dv + 1) * P], g_qd[:, h, c * P:(c + 1) * P],
                                                      start=False, stop=True)
                        mm.then_inc(gs["o"], 1)

                def state_products(c):
                    if c == 0:
                        pe.wait_ge(gs["kdc"], TT - 1)
                    for h in range(H4):
                        mm = nc.tensor.matmul(bank[2 + h // 2][:, h % 2 * GLA_DV:(h % 2 + 1) * GLA_DV],
                                              g_kdT[:, c, h, :], g_v[:, c, h * GLA_DV:(h + 1) * GLA_DV], start=True, stop=True)
                        if h % 2:
                            mm.then_inc(gs["st"], 1)

                def half_tile(t, half):
                    ks = range(half * KT // 2, (half + 1) * KT // 2)
                    if half == 0:
                        pe.wait_ge(gs["evac"], t - 1)
                        pe.wait_ge(s_w, u0 + t + 1)
                    for k in ks:
                        mm = product(bank[t % 2][:, :], (u0 + t) % RING, k, XH[:, k, :], XL[:, k, :], k == 0, k == KT - 1)
                    if half == 1:
                        mm.then_inc(s_used, 1)

                for t in range(17):
                    if t >= 4:
                        pe.wait_ge(gs["evac"], t - 3)
                    tile(u0 + t, t % 4, XH, XL, s_xl if t == 0 else None)
                    if t == 0:
                        stats(0)
                    if t == 2:
                        pe.wait_ge(gs["evac"], 1)
                        pe.wait_ge(s_rstd, 1)
                        pe.wait_ge(s_const, 32)
                        for c in range(TT):
                            nc.tensor.matmul(bank[4 + c][:, :], g_a[:, c * P:(c + 1) * P], PAR("w_alpha"),
                                             start=True, stop=True).then_inc(gs["apre"], 1)
                    if t == 8:
                        pe.wait_ge(gs["g"], TT)
                        for h in range(H4):
                            for c in range(TT):
                                mm = nc.tensor.matmul(bank[4 + h][:, c * P:(c + 1) * P], g_g[:, c, h * P:(h + 1) * P],
                                                      C("cum"), start=True, stop=True)
                            mm.then_inc(gs["cum"], 1)
                    if t >= 10:
                        v_turn(t - 10)
                        level(t - 10)
                for t in range(17, U_GLA):
                    half_tile(t, 0)
                    if t == 19:
                        state_products(0)
                    if t == 20:
                        outputs(2)
                        state_products(2)
                    half_tile(t, 1)
                    if t == 17:
                        v_turn(7)
                        diagonal()
                    if t == 18:
                        end_keys()
                        outputs(0)
                    if t == 19:
                        outputs(1)
                        state_products(1)
                    if t == 20:
                        outputs(3)
                    if t == 21:
                        pe.wait_ge(gs["oc"], 2 * TT)
                        for h in range(H4):
                            pe.wait_ge(gs["osq"], 2 * h + 2)
                            for j in range(2):
                                mm = nc.tensor.matmul(bank[4 + h][:, :], ones_m, g_osq[:, 2 * h + j, :], start=j == 0, stop=j == 1)
                            mm.then_inc(gs["on"], 1)
                residual(1, "gla_o", g_oh, g_ol, gs["ol"], 0, (2, 3, 4, 5))

            def nsa():
                u0 = START["kv"]

                def aux(t):
                    if t in (6, 7, 10, 11):
                        m = (t - 6) % 4 + 2 * (t // 10)
                        pe.wait_ge(ns["evac"], t + 1)
                        if m:
                            pe.wait_ge(ns["vc"], m)
                        turn(5, n_raw[:, t % 2, :], ns["vT"])

                for t in range(U_NSA_KV):
                    if t >= 4:
                        pe.wait_ge(ns["evac"], t - 3)
                    tile(u0 + t, t % 4, XH, XL, s_xl if t == 0 else None, 8 * PREP[2])
                    if t == 0:
                        stats(2)
                    if t:
                        aux(t - 1)
                aux(U_NSA_KV - 1)

                pe.wait_ge(ns["yh"], 4)
                pe.wait_ge(ns["yl"], 4)
                pe.wait_ge(s_rstd, 3)
                for kv in range(2):
                    o = bank[6 + kv][:, 0:CMP_HIDDEN]
                    for ip in range(16):
                        u = START["cmp"] + 4 * kv + ip // 4
                        i = ip % 4
                        if i == 0:
                            pe.wait_ge(s_w, u + 1)
                        blocks = slice(2 * ip, 2 * ip + CMP_STRIDE * (P - 1) + 1, CMP_STRIDE)
                        for n, (w, y, e) in enumerate(((w_hi, n_yh, n_peh), (w_hi, n_yl, n_pel), (w_lo, n_yh, n_peh))):
                            rhs = w[u % RING][:, 2 * i:2 * i + 2, :].rearrange("p a b -> p (a b)")
                            nc.tensor.matmul(o, y[kv][:, blocks], rhs, start=ip == 0 and n == 0, stop=False)
                            mm = nc.tensor.matmul(o, e[:, kv, ip:ip + 1].broadcast_to([P, P]), rhs, start=False,
                                                  stop=ip == 15 and n == 2)
                        if i == 3:
                            mm.then_inc(s_used, 1)

                def hidden_turn(kv):
                    pe.wait_ge(ns["hid"], kv + 1)
                    for jt in range(2):
                        mm = nc.tensor.transpose(bank[4 + kv][:, jt * P:(jt + 1) * P], n_hT[:, kv, jt * P:(jt + 1) * P], ident)
                    mm.then_inc(ns["hT"], 1)

                def compressed():
                    pe.wait_ge(ns["hTc"], 2)
                    for jt in range(2):
                        mm = nc.tensor.matmul(bank[6][:, 0:P], PAR("w2k")[:, jt * P:(jt + 1) * P], n_hid[:, 0, jt, :],
                                              start=jt == 0, stop=jt == 1)
                    mm.then_inc(ns["kvc"], 1)
                    for g in range(NSA_KV):
                        for jt in range(2):
                            for copy in range(4):
                                rows = slice(copy * NC_PAD, (copy + 1) * NC_PAD)
                                mm = nc.tensor.matmul(bank[7][rows, g * DH:(g + 1) * DH],
                                                      n_hid[:, 1, jt, g * NC_PAD:(g + 1) * NC_PAD],
                                                      PAR("w2v")[:, jt * DH:(jt + 1) * DH], start=jt == 0, stop=jt == 1)
                    mm.then_inc(ns["kvc"], 1)

                def query(e):
                    raw = n_raw[:, (e + 1) % 2, :]
                    rd = e // 2
                    pe.wait_ge(ns["evac"], U_NSA_KV + 1 + e + 1)
                    if e == 0:
                        pe.wait_ge(ns["kvcc"], 5)
                    if e % 2 == 0 and rd >= 2:
                        pe.wait_ge(ns["csub"], rd - 1)
                    for c in range(TT):
                        lo_ = c * P + e % 2 * 64
                        mm = nc.tensor.matmul(bank[6 + rd % 2][:, lo_:lo_ + 64], raw[:, c * P:(c + 1) * P], n_kc[:, rd, :, :],
                                              start=True, stop=True)
                    mm.then_inc(ns["cs"], 1)

                def cmp_turn(rd, b):
                    pe.wait_ge(ns["p"], rd + 1)
                    if rd:
                        pe.wait_ge(ns["pTc"], rd)
                    for c in range(TT):
                        mm = nc.tensor.transpose(bank[b][:, c * P:(c + 1) * P], n_sc[rd % 2][:, c * P:(c + 1) * P], ident)
                    mm.then_inc(ns["pT"], 1)

                u0 = START["nsa_q"]
                for t in range(U_NSA_Q):
                    pe.wait_ge(ns["evac"], U_NSA_KV + t - 3)
                    tile(u0 + t, t % 4, XH2, XL2, ns["xl2"] if t == 0 else None)
                    if t == 0:
                        pe.wait_ge(ns["vc"], 4)
                        hidden_turn(0)
                        hidden_turn(1)
                    if t == 1:
                        compressed()
                        pe.wait_ge(ns["evac"], U_NSA_KV + 1)
                        turn(5, n_raw[:, 0, :], ns["gT"])
                    if t >= 2:
                        query(t - 2)
                    if t == 5 or t == 7:
                        pe.wait_ge(ns["gate"], 1)
                        cmp_turn((t - 5) // 2, 5)
                query(7)

                ring = (4, 6, 7, 5)
                pe.wait_ge(s_bf, 2)
                jobs = NSA_HEADS * TT * 2
                for q in range(jobs + 8):
                    if q == 4:
                        cmp_turn(2, 0)
                    if q == 7:
                        cmp_turn(3, 0)
                    if q < jobs:
                        e, i, par, c = q // 16, query_tile(q), q // 2 % 2, q % 2
                        S = (i + 1) * P
                        b = bank[ring[q % 4]]
                        if q >= 4:
                            pe.wait_ge(ns["exp"], q - 3)
                        elif q == 3:
                            pe.wait_ge(ns["pTc"], 2)
                        elif q:
                            pe.wait_ge(ns["csub"], q + 2)
                        if q % 16 == 0:
                            pe.wait_ge(ns["rope"], 4 + e + 1)
                        if q % 32 < 2:
                            pe.wait_ge(ns["kl"], e + c + 1)
                        N = max(S, 2 * P)
                        for k, keys in enumerate((n_kh[c][e // 2][:, 0:N], n_kl[c][:, e // 2, 0:N])):
                            nc.tensor.matmul(b[:, 0:N], n_qp[:, 2 * e + par, i * P:S], keys, start=k == 0, stop=False)
                        nc.tensor.matmul(b[:, i * P:S], ident_bf[:, :], causal_bf, start=False, stop=True)\
                            .then_inc(ns["s"], 1)
                    if 4 <= q < jobs + 4:
                        m = q - 4
                        i = query_tile(m)
                        pe.wait_ge(ns["w"], m + 1)
                        if m >= 3:
                            pe.wait_ge(ns["tc"], m - 2)
                        for j in range(i + 1):
                            mm = nc.tensor.transpose(bank[1 + m % 3][:, j * P:(j + 1) * P], n_P[m % 6][:, j * P:(j + 1) * P], ident)
                        mm.then_inc(ns["t"], 1)
                    if q >= 11 and q % 4 == 3:
                        n = (q - 11) // 4
                        e, i = n // 4, query_tile(4 * n)
                        g = e // 2
                        pe.wait_ge(ns["tc"], 4 * n + 4)
                        if n % 4 == 0:
                            pe.wait_ge(ns["pTc"], 4)
                            if e:
                                pe.wait_ge(ns["o"], e)
                            nc.tensor.matmul(bank[0][:, :], n_bd[:, g, e % 2, :], n_pcT[:, g, :], start=True, stop=False,
                                             skip_group_check=True)
                        for j in range(i + 1):
                            for c in range(2):
                                for par in range(2):
                                    mm = nc.tensor.matmul(bank[0][par * DH:(par + 1) * DH, i * P:(i + 1) * P],
                                                          n_v[c][:, j, g * DH:(g + 1) * DH], n_PT[:, n % 2, 2 * par + c, j, :],
                                                          start=False, stop=j == i and c == 1, skip_group_check=True)
                        mm.then_inc(ns["pv"], 1)
                residual(3, "nsa_o", n_oh, n_ol, ns["o"], 0, (4, 5, 6, 7))

            def hybrid(ly):
                n0 = HYB_N[ly]
                u0 = START[f"hyb{ly}"]
                e0 = U_HYB * ly

                def aux(t):
                    m = t - 8 if t < 12 else t - 16
                    pe.wait_ge(hs["evac"], e0 + t + 1)
                    if m or ly:
                        pe.wait_ge(hs["vc"], 8 * ly + m)
                    turn(5 if m < 4 else 7, h_raw[:, t % 2, :], hs["vT"])

                def fill(t, part=range(KT)):
                    if t == U_HYB - 1:
                        pe.wait_ge(hs["a"], SB_HEADS * (ly + 1) - 1)
                    elif part[0] == 0:
                        pe.wait_ge(hs["evac"], e0 + t - (t <= 26))
                    if part[0] == 0:
                        pe.wait_ge(s_w, u0 + t + 1)
                    for k in part:
                        mm = product(bank[fill_bank(t)][:, :], (u0 + t) % RING, k, XH[:, k, :], XL[:, k, :], k == 0, k == KT - 1)
                    if part[-1] == KT - 1:
                        mm.then_inc(s_used, 1)

                for t in range(12):
                    if t >= 4:
                        pe.wait_ge(hs["evac"], e0 + t - 3)
                    tile(u0 + t, t % 4, XH, XL, s_xl if t == 0 else None, 8 * PREP[n0 if ly else MID])
                    if t == 0:
                        stats(n0 if ly else MID)
                    if t == 1 and ly == 0:
                        pe.wait_ge(s_ss, 8 * n0 + 8)
                        nc.tensor.matmul(bank[5][:, :], ones_m, mid_ss[:, :], start=True, stop=True).then_inc(s_stat, 1)
                    if t == 3:
                        pe.wait_ge(hs["lp"], ly + 1)
                        nc.tensor.matmul(bank[6][:, 0:2], ones_m, h_lam[:, 0:2], start=True, stop=True)\
                            .then_inc(hs["lsum"], 1)
                    if t > 8:
                        aux(t - 1)
                aux(11)

                pe.wait_ge(hs["vc"], 8 * ly + 4)
                pe.wait_ge(hs["rope"], 8 * ly + 8)
                pe.wait_ge(hs["lam"], ly + 1)
                pe.wait_ge(s_rstd, n0 + 1)
                pe.wait_ge(hs["evac"], e0 + 12)
                units = DIFF_HEADS * TT
                q0 = units * ly

                def d_turn(m):
                    pe.wait_ge(hs["w"], q0 + m + 1)
                    if m:
                        pe.wait_ge(hs["tc"], q0 + m)
                    for j in range(m % TT + 1):
                        mm = nc.tensor.transpose(bank[2][:, j * P:(j + 1) * P], h_W[:, m % 2, j * P:(j + 1) * P], ident)
                    mm.then_inc(hs["t"], 1)

                def d_values(h):
                    pe.wait_ge(hs["tc"], q0 + TT * (h + 1))
                    if h:
                        pe.wait_ge(hs["od"], 4 * ly + h)
                    for j in range(TT):
                        mm = nc.tensor.matmul(bank[3][:, j * P:T], h_dv[:, j, h * P:(h + 1) * P], h_WT[:, j, j * P:T],
                                              start=j == 0, stop=j == TT - 1)
                    mm.then_inc(hs["pv"], 1)

                def d_sumsq(h):
                    pe.wait_ge(hs["osq"], 4 * ly + h + 1)
                    if h:
                        pe.wait_ge(hs["ors"], 4 * ly + h)
                    nc.tensor.matmul(bank[6][:, :], ones_m, h_osq[:, :], start=True, stop=True).then_inc(hs["on"], 1)

                for n in range(units):
                    h, i = n // TT, n % TT
                    S = (i + 1) * P
                    if n:
                        pe.wait_ge(hs["exp"], 2 * (q0 + n))
                    for c in range(2):
                        b = bank[4 + c]
                        nc.tensor.matmul(b[:, 0:S], h_dq[:, h, i * P:S], h_dk[:, h, c, 0:S], start=True, stop=False)
                        nc.tensor.matmul(b[:, i * P:S], ident_bf[:, :], causal_bf, start=False, stop=True)\
                            .then_inc(hs["s"], 1)
                    if n:
                        d_turn(n - 1)
                        if FILL.get(n - 1, 0) >= 20:
                            aux(FILL[n - 1])
                    for p_ in range(6 * n, 6 * n + 6):
                        fill(12 + p_ // KT, (p_ % KT,))
                    if n and (n - 1) % TT == TT - 1:
                        d_values((n - 1) // TT)
                    if n >= 2 and (n - 2) % TT == TT - 1:
                        d_sumsq((n - 2) // TT)
                d_turn(units - 1)
                aux(FILL[units - 1])

                pe.wait_ge(hs["vc"], 8 * ly + 8)
                k0 = SB_HEADS * ly

                def region(h, j):
                    return bank[SB_BANKS[h % 2][(0, 1, 2, 1)[j]]], 384 if j == 3 else 0

                def s_scores(h):
                    if h == 0:
                        pe.wait_ge(hs["exp"], 2 * (q0 + units))
                    elif h == 1:
                        pe.wait_ge(hs["od"], 4 * ly + 4)
                        pe.wait_ge(hs["evac"], e0 + 26)
                    else:
                        pe.wait_ge(hs["a"], k0 + h - 1)
                    for j in range(TT):
                        b, lo = region(h, j)
                        mm = nc.tensor.matmul(b[:, lo:lo + SB_W[j]], h_sk[:, h, j * P:(j + 1) * P],
                                              h_sq[:, h // 2, j * P:T], start=j != 3, stop=False, skip_group_check=True)
                    mm.then_inc(hs["z"], 1)

                def s_values(a):
                    pe.wait_ge(hs["a"], k0 + 2 * a + 2)
                    if a:
                        pe.wait_ge(hs["osc"], 3 * ly + a)
                    for j in range(TT):
                        for par in range(2):
                            h = 2 * a + par
                            mm = nc.tensor.matmul(bank[2][par * DH:(par + 1) * DH, j * P:T], h_sv[:, j, h * DH:(h + 1) * DH],
                                                  h_a[:, par, SB_AT[j]:SB_AT[j] + SB_W[j]], start=j == 0, stop=j == TT - 1)
                    mm.then_inc(hs["spv"], 1)

                for h in range(SB_HEADS):
                    if h == 0:
                        s_scores(0)
                    fill(24 + 2 * h)
                    if h == 0:
                        d_values(DIFF_HEADS - 1)
                    elif h < SB_HEADS - 1:
                        s_scores(h + 1)
                    if h % 2 == 0 and h:
                        s_values(h // 2 - 1)
                    cut = KT if 0 < h < SB_HEADS - 1 else 6
                    fill(25 + 2 * h, range(cut))
                    if h == 0:
                        d_sumsq(DIFF_HEADS - 1)
                    pe.wait_ge(hs["sp"], k0 + h + 1)
                    b0, b1, b2 = (bank[b] for b in SB_BANKS[h % 2])
                    for sp_, later in ((h_sp_hi[h // 4][:, :], h_later_hi[:, h % 2, 640:1280]),
                                       (h_sp_lo[:, h % 2, :], h_later_lo[:, h % 2, 0:640])):
                        for o, w, x in ((b0[:, :], negtri_r, sp_[:, 0:512]), (b1[:, :], negtri_r, sp_[:, 512:1024]),
                                        (b2[:, 0:256], negtri_r, sp_[:, 1024:1280]), (b0[:, P:T], negones_r, later[:, 0:384]),
                                        (b1[:, P:384], negones_r, later[:, 384:640]), (b2[:, P:256], negones_r, sp_[:, 896:1024])):
                            nc.tensor.matmul(o, w[:, :], x, start=False, stop=False, skip_group_check=True)
                    for j in range(TT):
                        b, lo = region(h, j)
                        mm = nc.tensor.matmul(b[:, lo:lo + P], ident_bf[:, :], sb_neg_bf, start=False, stop=True,
                                              skip_group_check=True)
                    mm.then_inc(hs["cum"], 1)
                    if cut < KT:
                        fill(25 + 2 * h, range(cut, KT))
                    if h == 0:
                        s_scores(1)

                u0 = START[f"merge{ly}"]
                pe.wait_ge(hs["a"], k0 + SB_HEADS - 1)
                for m in range(2 * KT):
                    u = u0 + m // 2
                    if m % 2 == 0:
                        pe.wait_ge(s_w, u + 1)
                    if m >= 4:
                        pe.wait_ge(hs["mevac"], 16 * ly + m - 3)
                    elif m == 2:
                        pe.wait_ge(hs["evac"], e0 + U_HYB)
                    xh, xl, ready = (h_osh, h_osl, "osl") if m >= KT else (h_odh, h_odl, "odl")
                    for k in range(4):
                        if m % KT == 0:
                            pe.wait_ge(hs[ready], 4 * ly + k + 1)
                        mm = product(bank[(4, 5, 0, 7)[m % 4]][:, :], u % RING, m % 2 * 4 + k, xh[:, k, :], xl[:, k, :],
                                     k == 0, k == 3)
                    mm.then_inc(hs["mt"] if m % 2 == 0 else s_used, 1)
                    if m == 1:
                        s_values(3)
                residual(n0 + 1, f"out{ly}", h_mh, h_ml, hs["ml"], 8 * ly, (2, 4, 5, 7))

            pe.wait_ge(s_ident, 16)
            for c in range(TT):
                pe.wait_ge(s_xin[c], 16)
                for k in range(KT):
                    mm = nc.tensor.transpose(bank[k][:, c * P:(c + 1) * P], x_tok[:, c, k * P:(k + 1) * P], ident)
                    if c == TT - 1:
                        mm.then_inc(s_xt, 1)
            gla()
            ffn(0, 1, "ffn0")
            nsa()
            ffn(1, 3, "ffn1")
            hybrid(0)
            ffn(2, 6, "ffn2")
            hybrid(1)
            ffn(3, 8, "ffn3")
            def y_turn(c, half):
                for k in range(4):
                    mm = nc.tensor.transpose(bank[4 * half + c][:, k * P:(k + 1) * P], X[:, 4 * half + k, c * P:(c + 1) * P], ident)
                mm.then_inc(s_yt, 1)

            pe.wait_ge(s_x, 8 * 9 + 4)
            for c in range(TT):
                y_turn(c, 0)
            pe.wait_ge(s_x, 8 * 9 + 8)
            for c in range(TT - 1):
                y_turn(c, 1)
            pe.wait_ge(s_ss, 8 * 9 + 8)
            for c in range(TT):
                mm = nc.tensor.matmul(bank[7][:, 2 * c:2 * c + 2], ss[:, c * P:(c + 1) * P], ones_m[:, 0:2], start=True, stop=True)
            mm.then_inc(s_stat, 1)
            pe.wait_ge(s_rln, 10)
            y_turn(TT - 1, 1)

        @block.scalar
        def _(act):
            steps = [0]

            def own(ins):
                steps[0] += 1
                ins.then_inc(s_act, 1)
                act.wait_ge(s_act, steps[0])

            def squares(n, k):
                act.wait_ge(s_x, 8 * n + k + 1)
                if 8 * n + k >= 2:
                    act.wait_ge(s_ss, 8 * n + k - 1)
                nc.scalar.activation(sq[:, k % 2, :], X[:, k, :], ACT.Square).then_inc(s_sq, 1)

            def prepare(n):
                for k in range(KT):
                    squares(n, k)
                    nc.scalar.activation(XH[:, k, :], X[:, k, :], ACT.Copy, scale=parts_gain(n, k)).then_inc(s_xh, 1)

            def inv_rms(n, width=T):
                r = rstd[:, 0:width]
                act.wait_ge(s_stat, n + 1)
                nc.scalar.activation(r, bank[7][:, 0:width], ACT.Ln, bias=eps_col, scale=1.0 / D).then_inc(s_rln, 1)
                act.wait_ge(s_rln, n + 1)
                nc.scalar.activation(r, r, ACT.Exp, scale=-0.5).then_inc(s_rstd, 1)

            def ffn(fi, n):
                conv = fi < 2
                nc.scalar.preload_act_table_set("silu_and_others")
                with act.Fori(0, FT // 2) as i:
                    for p in range(2):
                        up = i * 4 + (2 * FT * fi + 2 * p)
                        pair = i * 2 + (FT * fi + p)
                        if conv:
                            for side in range(2):
                                act.wait_ge(s_u, up + (side + 1))
                                if side:
                                    act.wait_ge(s_h, pair)
                                t = i * 4 + (2 * p + side)
                                w0, b0 = COLS["conv_w"][0] + (fi * 3 + 2) * 2 * FT, COLS["conv_b"][0] + fi * 2 * FT
                                nc.scalar.activation(f_c[side][:, :], f_u[side][:, 2:T + 2], ACT.Identity,
                                                     bias=par_sb[:, bass.ds(t + b0, 1)],
                                                     scale=par_sb[:, bass.ds(t + w0, 1)]).then_inc(s_c0, 1)
                            act.wait_ge(s_c2, up + 1)
                        else:
                            act.wait_ge(s_u, up + 1)
                        nc.scalar.activation(f_s[:, :], f_c[0][:, :], ACT.Silu).then_inc(s_silu, 1)
                        act.wait_ge(s_h, pair + 1)
                        nc.scalar.activation(hid_h[:, bass.ds(i * (2 * T) + p * T, T)], f_h[:, :], ACT.Copy)\
                            .then_inc(s_hh, 1)

            def gla():
                u0 = START["gla"]

                def v_copy(f):
                    act.wait_ge(gs["vT"], f + 1)
                    nc.scalar.activation(g_v[:, :, f * P:(f + 1) * P],
                                         bank[4][:, :].rearrange("p (c k) -> p c k", c=TT), ACT.Copy).then_inc(gs["vc"], 1)

                nc.scalar.preload_act_table_set("natural_log_exp_and_others")
                prepare(0)
                inv_rms(0)
                for c in range(TT):
                    act.wait_ge(gs["apre"], c + 1)
                    ins = nc.scalar.activation(g_z[0][:, c, :], bank[4 + c][:, :], ACT.Abs)
                own(ins)
                own(nc.scalar.activation(g_z[0][:, :, :], g_z[0][:, :, :], ACT.Exp, scale=-1.0))
                nc.scalar.activation(g_z[0][:, :, :], g_z[0][:, :, :], ACT.Ln, bias=one_col).then_inc(gs["soft"], 1)
                for h in range(H4):
                    act.wait_ge(gs["cum"], h + 1)
                    nc.scalar.activation(g_b[:, h, :], bank[4 + h][:, :], ACT.Copy).then_inc(gs["b"], 1)
                for lv in range(8):
                    if lv < LEVELS:
                        act.wait_ge(gs["D"], lv + 1)
                        nc.scalar.activation(g_z[lv % 2][:, :, :], g_z[lv % 2][:, :, :], ACT.Exp).then_inc(gs["E"], 1)
                    if lv:
                        v_copy(lv - 1)
                act.wait_ge(gs["mm"], 2 * LEVELS)
                nc.scalar.activation(g_z[0][:, :, :], g_b[:, :, :], ACT.Exp).then_inc(gs["E"], 1)
                act.wait_ge(gs["D"], LEVELS + 1)
                nc.scalar.activation(g_z[1][:, :, :], g_z[1][:, :, :], ACT.Exp).then_inc(gs["E"], 1)
                v_copy(7)
                for c, b in enumerate((2, 3, 6)):
                    act.wait_ge(gs["kdT"], c + 1)
                    nc.scalar.activation(g_kdT[:, c, :, :], bank[b][:, :].rearrange("p (h k) -> p h k", h=H4), ACT.Copy)\
                        .then_inc(gs["kdc"], 1)
                for m in range(2 * TT):
                    c, hp = m // 2, m % 2
                    act.wait_ge(gs["o"], m + 1)
                    nc.scalar.activation(g_o[:, 4 * hp:4 * hp + 4, c * P:(c + 1) * P],
                                         bank[4 + m % 4][:, :].rearrange("p (q t) -> p q t", q=4), ACT.Copy).then_inc(gs["oc"], 1)
                act.wait_ge(gs["oc"], 2 * TT)
                for f in range(8):
                    nc.scalar.activation(g_osq[:, f, :], g_o[:, f, :], ACT.Square).then_inc(gs["osq"], 1)
                for h in range(H4):
                    act.wait_ge(gs["on"], h + 1)
                    own(nc.scalar.activation(g_ors[:, h, :], bank[4 + h][:, :], ACT.Ln, bias=eps_col, scale=1.0 / GLA_DV))
                    nc.scalar.activation(g_ors[:, h, :], g_ors[:, h, :], ACT.Exp, scale=-0.5).then_inc(gs["ors"], 1)

                def silu(f):
                    act.wait_ge(gs["evac"], 17 + f + 1)
                    nc.scalar.activation(g_r[:, f, :], g_r[:, f, :], ACT.Silu).then_inc(gs["silu"], 1)

                nc.scalar.preload_act_table_set("silu_and_others")
                for f in range(5):
                    silu(f)
                for f in range(8):
                    act.wait_ge(gs["ot"], f + 1)
                    nc.scalar.activation(g_oh[:, f, :], g_o[:, f, :], ACT.Copy).then_inc(gs["oh"], 1)
                    if f % 2 and f < 7:
                        silu(5 + f // 2)
                nc.scalar.preload_act_table_set("natural_log_exp_and_others")

            def half_swap(to, raw, done):
                for b in range(4):
                    r, other = slice(32 * b, 32 * b + 32), slice(32 * (b ^ 1), 32 * (b ^ 1) + 32)
                    ins = nc.scalar.activation(to[r, :], raw[other, :], ACT.Copy)
                ins.then_inc(done, 1)

            def nsa():
                def v_copy(m):
                    act.wait_ge(ns["vT"], m + 1)
                    nc.scalar.activation(n_v[m // 2][:, :, m % 2 * P:(m % 2 + 1) * P],
                                         bank[5][:, :].rearrange("p (c k) -> p c k", c=TT), ACT.Copy).then_inc(ns["vc"], 1)

                nc.scalar.preload_act_table_set("natural_log_exp_and_others")
                prepare(2)
                inv_rms(2)
                for k in range(KT):
                    nc.scalar.activation(XH2[:, k, :], X[:, k, :], ACT.Copy, scale=gain(KV_MIX_GAIN, k)).then_inc(ns["xh2"], 1)
                for t in range(4):
                    act.wait_ge(ns["evac"], t + 1)
                    if t == 0:
                        act.wait_ge(ns["yl"], 1)
                    for e in range(2):
                        head = 2 * (t % 2) + e
                        r = slice(DH * e, DH * e + DH)
                        nc.scalar.activation(n_yh[t // 2][0:DH, head * T:(head + 1) * T], n_raw[r, t % 2, :], ACT.Copy)
                        ins = nc.scalar.activation(n_yh[t // 2][DH:P, head * T:(head + 1) * T - 1], n_raw[r, t % 2, 1:T], ACT.Copy)
                    ins.then_inc(ns["yh"], 1)
                act.wait_ge(ns["yl"], 4)
                for t in (4, 5, 6, 7, 8, 9, 10, 11):
                    if t % 4 < 2:
                        m = t % 4 + 2 * (t // 8)
                        act.wait_ge(ns["evac"], t + 1)
                        if m:
                            act.wait_ge(ns["rope"], m)
                        half_swap(n_t2, n_raw[:, t % 2, :], ns["rot"])
                    else:
                        v_copy(t % 4 - 2 + 2 * (t // 8))
                for kv in range(2):
                    act.wait_ge(s_used, START["cmp"] + 4 * kv + 4)
                    nc.scalar.activation(n_hT[:, kv, :], bank[6 + kv][:, 0:CMP_HIDDEN], ACT.Gelu_apprx_tanh).then_inc(ns["hid"], 1)
                for kv in range(2):
                    act.wait_ge(ns["hT"], kv + 1)
                    nc.scalar.activation(n_hid[:, kv, :, :], bank[4 + kv][:, 0:CMP_HIDDEN].rearrange("p (j n) -> p j n", j=2),
                                         ACT.Copy).then_inc(ns["hTc"], 1)
                act.wait_ge(ns["kvc"], 1)
                act.wait_ge(ns["p0"], 1)
                for par in range(2):
                    r = slice(par * DH, (par + 1) * DH)
                    ins = nc.scalar.activation(n_kc[r, :, par, :], bank[6][r, 0:P].rearrange("p (g n) -> p g n", g=NSA_KV), ACT.Copy)
                ins.then_inc(ns["kvcc"], 1)
                act.wait_ge(ns["kvc"], 2)
                for copy in range(4):
                    r = slice(copy * NC_PAD, (copy + 1) * NC_PAD)
                    nc.scalar.activation(n_bd[r, :, copy // 2, copy % 2 * DH:(copy % 2 + 1) * DH],
                                         bank[7][r, 0:NSA_KV * DH].rearrange("p (g d) -> p g d", g=NSA_KV), ACT.Copy)\
                        .then_inc(ns["kvcc"], 1)
                act.wait_ge(ns["gT"], 1)
                nc.scalar.activation(n_gate[:, :, :], bank[5][:, :].rearrange("p (c k) -> p c k", c=TT)[:, :, 0:48],
                                     ACT.Sigmoid).then_inc(ns["gate"], 1)
                nc.scalar.preload_act_table_set("natural_log_exp_and_others")

                def cmp_exp(rd):
                    act.wait_ge(ns["cmax"], rd + 1)
                    s = n_sc[rd % 2]
                    nc.scalar.activation(s[:, :], s[:, :], ACT.Exp).then_inc(ns["ce"], 1)

                def cmp_copy(rd, b):
                    act.wait_ge(ns["pT"], rd + 1)
                    nc.scalar.activation(n_pcT[:, rd, :], bank[b][:, :], ACT.Copy).then_inc(ns["pTc"], 1)

                def key_high(g):
                    for c in range(2):
                        nc.scalar.activation(n_kh[c][g][:, :], n_k[c][:, g, :], ACT.Copy).then_inc(ns["kh"], 1)

                def swap(e):
                    act.wait_ge(ns["evac"], U_NSA_KV + 1 + e + 1)
                    act.wait_ge(ns["rope"], 4 + e)
                    half_swap(n_t2, n_raw[:, (e + 1) % 2, :], ns["rot"])

                swap(0)
                swap(1)
                for rd in range(2):
                    swap(2 * rd + 2)
                    cmp_exp(rd)
                    swap(2 * rd + 3)
                    cmp_copy(rd, 5)
                swap(6)
                cmp_exp(2)
                act.wait_ge(s_used, START["nsa_q"] + U_NSA_Q)
                key_high(0)
                cmp_exp(3)
                jobs = NSA_HEADS * TT * 2
                for q in range(jobs + 9):
                    if q == 5:
                        cmp_copy(2, 0)
                    if q == 8:
                        cmp_copy(3, 0)
                    if q == 4:
                        swap(7)
                    if q in (10, 12):
                        key_high(q // 2 - 4)
                    if q == 44:
                        act.wait_ge(ns["rope"], 12)
                        key_high(3)
                    if 5 <= q < jobs + 5:
                        m = q - 5
                        n, i = m // 4, query_tile(m)
                        if m % 4 == 0 and n >= 2:
                            act.wait_ge(ns["pv"], n - 1)
                        act.wait_ge(ns["t"], m + 1)
                        nc.scalar.activation(n_PT[:, n % 2, m % 4, 0:i + 1, :],
                                             bank[1 + m % 3][:, 0:(i + 1) * P].rearrange("p (j t) -> p j t", t=P), ACT.Copy)\
                            .then_inc(ns["tc"], 1)
                    if q < jobs:
                        S = (query_tile(q) + 1) * P
                        if q >= 6:
                            act.wait_ge(ns["t"], q - 5)
                        act.wait_ge(ns["mx"], q + 1)
                        nc.scalar.activation(n_P[q % 6][:, 0:S], bank[(4, 6, 7, 5)[q % 4]][:, 0:S], ACT.Exp, bias=n_st[:, 0, q:q + 1],
                                             accum_out=n_st[:, 1, q:q + 1]).then_inc(ns["exp"], 1)
                    if q >= 24 and (q - 24) % 16 == 0:
                        e = (q - 24) // 16
                        act.wait_ge(ns["pv"], 4 * e + 4)
                        nc.scalar.activation(n_oh[:, e, :], bank[0][:, :], ACT.Copy).then_inc(ns["oh"], 1)

            def hybrid(ly):
                n0 = HYB_N[ly]

                def v_copy(m, b):
                    act.wait_ge(hs["vT"], 8 * ly + m + 1)
                    dst, f = (h_dv, m) if m < 4 else (h_sv, m - 4)
                    nc.scalar.activation(dst[:, :, f * P:(f + 1) * P], bank[b][:, :].rearrange("p (c k) -> p c k", c=TT),
                                         ACT.Copy).then_inc(hs["vc"], 1)

                nc.scalar.preload_act_table_set("natural_log_exp_and_others")
                if ly:
                    prepare(n0)
                    inv_rms(n0)
                else:
                    prepare(MID)
                    for k in range(KT):
                        act.wait_ge(s_ss, 8 * n0 + k - 1)
                        nc.scalar.activation(sq[:, k % 2, :], X[:, k, :], ACT.Square, scale=gain(GAIN[MID], k)).then_inc(s_sq, 1)
                    inv_rms(MID)
                    act.wait_ge(s_mid, 1)
                    nc.scalar.activation(mid_r[:, :], mid_r[:, :], ACT.Ln, bias=eps_col, scale=1.0 / D).then_inc(s_rln, 1)
                    act.wait_ge(s_rln, n0 + 1)
                    nc.scalar.activation(mid_r[:, :], mid_r[:, :], ACT.Exp, scale=-0.5).then_inc(s_rstd, 1)
                for t in range(8):
                    act.wait_ge(hs["evac"], U_HYB * ly + t + 1)
                    if t:
                        act.wait_ge(hs["rope"], 8 * ly + t)
                    half_swap(h_t2, h_raw[:, t % 2, :], hs["rot"])
                    if t == 2:
                        act.wait_ge(hs["lsum"], ly + 1)
                        nc.scalar.activation(h_lam[:, 2:4], bank[6][:, 0:2], ACT.Exp).then_inc(hs["le"], 1)
                for m in range(4):
                    v_copy(m, 5)
                units = DIFF_HEADS * TT
                q0 = units * ly

                def squares_of(h):
                    act.wait_ge(hs["pv"], 4 * ly + h + 1)
                    nc.scalar.activation(h_osq[:, :], bank[3][:, :], ACT.Square).then_inc(hs["osq"], 1)

                for n in range(units + 1):
                    if n < units:
                        S = (n % TT + 1) * P
                        if n:
                            act.wait_ge(hs["w"], q0 + n)
                        for c in range(2):
                            act.wait_ge(hs["mx"], 2 * (q0 + n) + c + 1)
                            nc.scalar.activation(h_P[:, c, 0:S], bank[4 + c][:, 0:S], ACT.Exp,
                                                 bias=h_st[:, 0, 2 * n + c:2 * n + c + 1],
                                                 accum_out=h_st[:, 1, 2 * n + c:2 * n + c + 1]).then_inc(hs["exp"], 1)
                    if n:
                        m = n - 1
                        h, i = m // TT, m % TT
                        if i == 0 and h:
                            act.wait_ge(hs["pv"], 4 * ly + h)
                        act.wait_ge(hs["t"], q0 + m + 1)
                        nc.scalar.activation(h_WT[:, 0:i + 1, i * P:(i + 1) * P],
                                             bank[2][:, 0:(i + 1) * P].rearrange("p (j t) -> p j t", t=P), ACT.Copy)\
                            .then_inc(hs["tc"], 1)
                        if FILL.get(m, 0) >= 20:
                            v_copy(FILL[m] - 16, 7)
                    if 5 <= n < units and (n - 5) % TT == 0:
                        squares_of((n - 5) // TT)
                    if 6 <= n < units and (n - 6) % TT == 0:
                        d_norm(ly, (n - 6) // TT)
                k0 = SB_HEADS * ly
                def softplus_log(h):
                    act.wait_ge(hs["z"], k0 + h + 1)
                    e = h_sp[:, h % 2, :]
                    b0, b1, b2 = (bank[b] for b in SB_BANKS[h % 2])
                    nc.scalar.activation(e[:, 0:512], b0[:, :], ACT.Abs)
                    nc.scalar.activation(e[:, 512:1024], b1[:, :], ACT.Abs)
                    own(nc.scalar.activation(e[:, 1024:1280], b2[:, 0:256], ACT.Abs))
                    own(nc.scalar.activation(e, e, ACT.Exp, scale=-1.0))
                    nc.scalar.activation(e, e, ACT.Ln, bias=one_col).then_inc(hs["ln"], 1)

                softplus_log(0)
                squares_of(DIFF_HEADS - 1)
                for h in range(SB_HEADS):
                    act.wait_ge(hs["soft"], k0 + h + 1)
                    nc.scalar.activation(h_sp_hi[h // 4][:, :], h_sp[:, h % 2, :], ACT.Copy).then_inc(hs["sphi"], 1)
                    if h == 0:
                        d_norm(ly, DIFF_HEADS - 1)
                    elif h < SB_HEADS - 1:
                        softplus_log(h + 1)
                    if h % 2 == 0 and h:
                        a = h // 2 - 1
                        act.wait_ge(hs["spv"], 4 * ly + a + 1)
                        nc.scalar.activation(h_os[:, a, :], bank[2][:, :], ACT.Copy).then_inc(hs["osc"], 1)
                    if h == SB_HEADS - 1:
                        act.wait_ge(s_used, START[f"hyb{ly}"] + U_HYB)
                        act.wait_ge(hs["od"], 4 * ly + 4)
                        for k in range(4):
                            nc.scalar.activation(h_odh[:, k, :], h_od[:, k, :], ACT.Copy).then_inc(hs["odh"], 1)
                    act.wait_ge(hs["cum"], k0 + h + 1)
                    a_ = h_a[:, h % 2, :]
                    b0, b1, b2 = (bank[b] for b in SB_BANKS[h % 2])
                    nc.scalar.activation(a_[:, 0:512], b0[:, :], ACT.Exp)
                    nc.scalar.activation(a_[:, 512:1024], b1[:, :], ACT.Exp)
                    nc.scalar.activation(a_[:, 1024:1280], b2[:, 0:256], ACT.Exp).then_inc(hs["a"], 1)
                    if h == 0:
                        softplus_log(1)

                def gate(f):
                    act.wait_ge(hs["evac"], U_HYB * ly + 24 + f + 1)
                    lo = COLS["b_gate"][0] + 16 * ly + f
                    nc.scalar.activation(h_gate[:, f, :], h_gate[:, f, :], ACT.Sigmoid, bias=par_sb[:, lo:lo + 1])\
                        .then_inc(hs["gate"], 1)

                nc.scalar.preload_act_table_set("sigmoid_and_others")
                gate(0)
                gate(1)
                for a in range(3):
                    act.wait_ge(hs["osc"], 3 * ly + a + 1)
                    nc.scalar.activation(h_osh[:, a, :], h_os[:, a, :], ACT.Copy).then_inc(hs["osh"], 1)
                gate(2)
                act.wait_ge(hs["spv"], 4 * ly + 4)
                nc.scalar.activation(h_osh[:, 3, :], bank[2][:, :], ACT.Copy).then_inc(hs["osh"], 1)
                for f in range(3, 16):
                    gate(f)
                for f in range(KT):
                    act.wait_ge(hs["m"], 8 * ly + f + 1)
                    nc.scalar.activation(h_mh[:, f, :], h_m[:, f % 2, :], ACT.Copy).then_inc(hs["mh"], 1)

            def d_norm(ly, h):
                act.wait_ge(hs["on"], 4 * ly + h + 1)
                if h:
                    act.wait_ge(hs["od"], 4 * ly + h)
                own(nc.scalar.activation(h_ors[:, :], bank[6][:, :], ACT.Ln, bias=eps_col, scale=1.0 / (2 * DH)))
                nc.scalar.activation(h_ors[:, :], h_ors[:, :], ACT.Exp, scale=-0.5).then_inc(hs["ors"], 1)

            act.wait_ge(s_ident, 16)
            act.wait_ge(s_gain, 16)
            gla()
            prepare(1)
            inv_rms(1)
            ffn(0, 1)
            nsa()
            prepare(3)
            inv_rms(3)
            ffn(1, 3)
            hybrid(0)
            prepare(6)
            inv_rms(6)
            ffn(2, 6)
            hybrid(1)
            prepare(8)
            inv_rms(8)
            ffn(3, 8)
            nc.scalar.preload_act_table_set("natural_log_exp_and_others")
            for k in range(KT):
                squares(9, k)
            inv_rms(9, 2 * TT)
        @block.vector
        def _(dve):
            steps = [0]
            V = nc.vector

            def own(ins):
                steps[0] += 1
                ins.then_inc(s_dve, 1)
                dve.wait_ge(s_dve, steps[0])

            def lo(n, k, parts=True):
                if parts:
                    dve.wait_ge(s_xh, 8 * PREP[n] + k + 1)
                    V.scalar_tensor_tensor(XL[:, k, :], X[:, k, :], parts_gain(n, k), XH[:, k, :].bitcast(F32),
                                           ALU.mult, ALU.subtract).then_inc(s_xl, 1)
                dve.wait_ge(s_sq, 8 * n + k + 1)
                if k == 0:
                    if n:
                        dve.wait_ge(s_stat, n)
                    V.tensor_copy(ss[:, :], sq[:, 0, :]).then_inc(s_ss, 1)
                else:
                    dve.wait_ge(s_ss, 8 * n + k)
                    V.tensor_tensor(ss[:, :], ss[:, :], sq[:, k % 2, :], ALU.add).then_inc(s_ss, 1)

            def add_residual(n, ready, banks, parts=True):
                for k in range(KT):
                    dve.wait_ge(*ready(k))
                    V.tensor_tensor(X[:, k, :], X[:, k, :], bank[banks(k)][:, :], ALU.add).then_inc(s_x, 1)
                    if k:
                        lo(n, k - 1, parts)
                lo(n, KT - 1, parts)

            def projected(n, name, banks=(0, 1, 2, 3)):
                add_residual(n, lambda k: (s_used, START[name] + k + 1), lambda k: banks[k % 4])

            def ffn(fi, n, name, n_next):
                conv = fi < 2
                dve.wait_ge(s_rstd, n + 1)
                u0 = START[name]
                if conv:
                    for side in range(2):
                        V.memset(f_u[side][:, 0:2], 0.0)
                with dve.Fori(0, FT // 2) as i:
                    for p in range(2):
                        c = i * 4 + 2 * p
                        up = i * 4 + (2 * FT * fi + 2 * p)
                        pair = i * 2 + (FT * fi + p)
                        for side in range(2):
                            dve.wait_ge(s_used, i * 4 + (u0 + 2 * p + side + 1))
                            dst = f_u[side][:, 2:T + 2] if conv else f_c[side][:, :]
                            V.tensor_tensor(dst, bank[2 * p + side][:, :], rstd[:, :], ALU.mult).then_inc(s_u, 1)
                        if conv:
                            for side in range(2):
                                w0 = COLS["conv_w"][0] + fi * 3 * 2 * FT + side
                                f = f_c[side][:, :]
                                dve.wait_ge(s_c0, up + (side + 1))
                                V.scalar_tensor_tensor(f, f_u[side][:, 1:T + 1], par_sb[:, bass.ds(c + (w0 + 2 * FT), 1)], f,
                                                       ALU.mult, ALU.add).then_inc(s_c1, 1)
                                dve.wait_ge(s_c1, up + (side + 1))
                                V.scalar_tensor_tensor(f, f_u[side][:, 0:T], par_sb[:, bass.ds(c + w0, 1)], f,
                                                       ALU.mult, ALU.add).then_inc(s_c2, 1)
                            dve.wait_ge(s_c2, up + 2)
                        dve.wait_ge(s_silu, pair + 1)
                        if not conv:
                            dve.wait_ge(s_u, up + 2)
                        V.tensor_tensor(f_h[:, :], f_s[:, :], f_c[1][:, :], ALU.mult).then_inc(s_h, 1)
                        dve.wait_ge(s_hh, pair + 1)
                        V.tensor_tensor(hid_l[:, bass.ds(i * (2 * T) + p * T, T)], f_h[:, :],
                                        hid_h[:, bass.ds(i * (2 * T) + p * T, T)].bitcast(F32), ALU.subtract)\
                            .then_inc(s_hl, 1)
                add_residual(n_next,
                             lambda k: (s_res, DOWN_TILES * fi + k + 1) if k < KT - 1 else (s_used, u0 + U_FFN),
                             lambda k: k, n_next in PREP)

            def rotate(dst, raw, swapped, done):
                V.tensor_tensor(n_t1[:, :], raw, cos_t, ALU.mult)
                own(V.tensor_tensor(swapped[:, :], swapped[:, :], sin_t, ALU.mult))
                for d, r in dst:
                    ins = V.tensor_tensor(d, n_t1[r, :], swapped[r, :], ALU.add)
                ins.then_inc(done, 1)

            def gla():
                u0 = START["gla"]

                def evac(t):
                    dve.wait_ge(s_used, u0 + t + 1)
                    b = bank[t % 4 if t < 17 else t % 2][:, :]
                    if t == 0:
                        dve.wait_ge(s_rstd, 1)
                        own(V.tensor_tensor(g_a[:, :], b, rstd[:, :], ALU.mult))
                        V.memset(g_a[0:1, :], 1.0).then_inc(gs["evac"], 1)
                        return
                    if t < 5:
                        V.scalar_tensor_tensor(g_q[:, t - 1, :], b, GLA_DK ** -0.5, rstd[:, :], ALU.mult, ALU.mult)\
                            .then_inc(gs["evac"], 1)
                        return
                    if t < 9:
                        dst = g_k[:, t - 5, :]
                    elif t < 17:
                        dst = g_vt[:, (t - 9) % 2, :]
                        if t >= 11:
                            dve.wait_ge(gs["vT"], t - 10)
                    else:
                        if t == 23:
                            dve.wait_ge(gs["vT"], 8)
                        dst = g_r[:, t - 17, :]
                    V.tensor_tensor(dst, b, rstd[:, :], ALU.mult).then_inc(gs["evac"], 1)

                def blocks(a, lv):
                    h = P >> (lv + 1)
                    return a[:, :, :].rearrange("p h (n two e) -> p (h n) two e", two=2, e=h)

                def exponents(lv):
                    z, b = blocks(g_z[lv % 2], lv), blocks(g_b, lv)
                    h = P >> (lv + 1)
                    ref = b[:, :, 0, h - 1:h].broadcast_to([P, H4 * T // (2 * h), h])
                    if lv >= 2:
                        dve.wait_ge(gs["mm"], 2 * (lv - 1))
                    V.tensor_tensor(z[:, :, 1, :], b[:, :, 1, :], ref, ALU.subtract)
                    V.tensor_tensor(z[:, :, 0, :], ref, b[:, :, 0, :], ALU.subtract).then_inc(gs["D"], 1)

                def decayed(lv):
                    z, q, k = blocks(g_z[lv % 2], lv), blocks(g_q, lv), blocks(g_k, lv)
                    dve.wait_ge(gs["E"], lv + 1)
                    V.tensor_tensor(z[:, :, 1, :], z[:, :, 1, :], q[:, :, 1, :], ALU.mult)
                    V.tensor_tensor(z[:, :, 0, :], z[:, :, 0, :], k[:, :, 0, :], ALU.mult).then_inc(gs["Z"], 1)

                def place(lv):
                    mask = masks_bf[:, lv:lv + 1, :].bitcast(U16).broadcast_to([P, H4, P])
                    if lv < LEVELS:
                        h = P >> (lv + 1)
                        mask = mask.rearrange("p h (n two e) -> p h n two e", two=2, e=h)[:, :, :, 1, :]
                    for c in range(TT):
                        if lv < LEVELS:
                            m = 2 * lv + c // 2
                        else:
                            m = 2 * LEVELS + c
                        dve.wait_ge(gs["mm"], m + 1)
                        if lv:
                            dve.wait_ge(gs["ev"], TT * (lv - 1) + c + 1)
                        to, products = g_att[:, c, :, :], bank[5 + m % 3]
                        if lv < LEVELS:
                            to = to.rearrange("p h (n two e) -> p h n two e", two=2, e=h)[:, :, :, 1, :]
                            products = products[:, c % 2 * 2 * P:(c % 2 + 1) * 2 * P].rearrange("p (h n e) -> p h n e", h=H4, e=h)
                        else:
                            products = products[:, :].rearrange("p (h t) -> p h t", h=H4)
                        V.copy_predicated(to, mask, products).then_inc(gs["ev"], 1)

                for t in range(9):
                    evac(t)
                    if t == 5:
                        dve.wait_ge(gs["soft"], 1)
                        for c in range(TT):
                            V.scalar_tensor_tensor(g_g[:, c, :], bank[4 + c][:, :], 0.0, g_z[0][:, c, :], ALU.min,
                                                   ALU.subtract).then_inc(gs["g"], 1)
                dve.wait_ge(s_masks, 16)
                V.tensor_copy(ident_bf[:, :], ident).then_inc(s_bf, 1)
                V.tensor_copy(masks_bf[:, :, :], masks_in[:, :, :]).then_inc(s_bf, 1)
                dve.wait_ge(s_bf, 2)
                dve.wait_ge(s_const, 32)
                dve.wait_ge(gs["b"], H4)
                V.memset(g_att[:, :, :, :], 0.0)
                exponents(0)
                z1 = g_z[1][:, :, :].rearrange("p h (c t) -> p h c t", t=P)
                bb = g_b[:, :, :].rearrange("p h (c t) -> p h c t", t=P)
                for lv in range(8):
                    evac(9 + lv)
                    if lv < LEVELS:
                        decayed(lv)
                        if lv:
                            place(lv - 1)
                    if lv < LEVELS - 1:
                        exponents(lv + 1)
                    if lv == LEVELS - 1:
                        dve.wait_ge(gs["mm"], 2 * (LEVELS - 1))
                        for h in range(H4):
                            ins = V.tensor_tensor(z1[:, h, :, :], bb[:, h, :, P - 1:P].broadcast_to([P, TT, P]), bb[:, h, :, :],
                                                  ALU.subtract)
                        ins.then_inc(gs["D"], 1)
                place(LEVELS - 1)
                dve.wait_ge(gs["E"], LEVELS + 1)
                z0 = g_z[0][:, :, :].rearrange("p h (c t) -> p h c t", t=P)
                V.tensor_copy(g_elast[:, :, :], z0[:, :, :, P - 1])
                V.tensor_tensor(g_qd[:, :, :], g_z[0][:, :, :], g_q[:, :, :], ALU.mult).then_inc(gs["qd"], 1)
                evac(17)
                place(LEVELS)
                dve.wait_ge(gs["E"], LEVELS + 2)
                V.tensor_tensor(g_z[1][:, :, :], g_z[1][:, :, :], g_k[:, :, :], ALU.mult).then_inc(gs["kd"], 1)
                evac(18)

                def state(c):
                    for h in range(H4):
                        dve.wait_ge(gs["st"], 2 * c + h // 2 + 1)
                        b = bank[2 + h // 2][:, h % 2 * GLA_DV:(h % 2 + 1) * GLA_DV]
                        if c == 0:
                            ins = V.tensor_copy(g_state[:, h, :], b)
                        else:
                            if h == 0:
                                dve.wait_ge(gs["state"], 4 * c)
                            ins = V.scalar_tensor_tensor(g_state[:, h, :], g_state[:, h, :], g_elast[:, h, c:c + 1], b,
                                                         ALU.mult, ALU.add)
                        ins.then_inc(gs["state"], 1)

                state(0)
                evac(19)
                state(1)
                state(2)
                evac(20)
                evac(21)
                for h in range(H4):
                    dve.wait_ge(gs["ors"], h + 1)
                    for f in (2 * h, 2 * h + 1):
                        lo_ = COLS["gla_norm"][0] + f
                        own(V.scalar_tensor_tensor(g_o[:, f, :], g_o[:, f, :], par_sb[:, lo_:lo_ + 1], g_ors[:, h, :],
                                                   ALU.mult, ALU.mult))
                        dve.wait_ge(gs["silu"], f + 1)
                        V.tensor_tensor(g_o[:, f, :], g_o[:, f, :], g_r[:, f, :], ALU.mult).then_inc(gs["ot"], 1)
                    for f in (2 * h, 2 * h + 1):
                        dve.wait_ge(gs["oh"], f + 1)
                        V.tensor_tensor(g_ol[:, f, :], g_o[:, f, :], g_oh[:, f, :].bitcast(F32), ALU.subtract)\
                            .then_inc(gs["ol"], 1)
                    if h < 3:
                        evac(22 + h)
                projected(1, "gla_o", (2, 3, 4, 5))

            def nsa():
                dve.wait_ge(s_rstd, 3)
                for k in range(KT):
                    dve.wait_ge(ns["xh2"], k + 1)
                    V.scalar_tensor_tensor(XL2[:, k, :], X[:, k, :], gain(KV_MIX_GAIN, k), XH2[:, k, :].bitcast(F32),
                                           ALU.mult, ALU.subtract).then_inc(ns["xl2"], 1)
                u0 = START["kv"]
                pe_in = PAR("pe").rearrange("p (kv i) -> p kv i", kv=2)
                own(V.tensor_copy(n_peh[:, :, :], pe_in))
                V.tensor_tensor(n_pel[:, :, :], pe_in, n_peh[:, :, :].bitcast(F32), ALU.subtract)
                for s in range(2):
                    for y in (n_yh, n_yl):
                        V.memset(y[s][DH:P, T - 1:NSA_KV * T:T].bitcast(F32), 0.0)
                        V.memset(y[s][:, NSA_KV * T:YW].bitcast(F32), 0.0)

                def evac(t):
                    dve.wait_ge(s_used, u0 + t + 1)
                    raw = n_raw[:, t % 2, :]
                    if 2 <= t <= 5:
                        dve.wait_ge(ns["yh"], t - 1)
                    if t in (8, 9):
                        dve.wait_ge(ns["vT"], t - 7)
                    V.tensor_tensor(raw, bank[t % 4][:, :], rstd[:, :], ALU.mult).then_inc(ns["evac"], 1)

                def lower(t):
                    raw = n_raw[:, t % 2, :]
                    dve.wait_ge(ns["evac"], t + 1)
                    own(V.tensor_copy(n_yt_h[:, :], raw))
                    own(V.tensor_tensor(n_yt_l[:, :], raw, n_yt_h[:, :].bitcast(F32), ALU.subtract))
                    for e in range(2):
                        head = 2 * (t % 2) + e
                        r = slice(DH * e, DH * e + DH)
                        V.tensor_copy(n_yl[t // 2][0:DH, head * T:(head + 1) * T], n_yt_l[r, :].bitcast(F32))
                        ins = V.tensor_copy(n_yl[t // 2][DH:P, head * T:(head + 1) * T - 1], n_yt_l[r, 1:T].bitcast(F32))
                    ins.then_inc(ns["yl"], 1)

                def key(t):
                    m = (t - 4) % 4 + 2 * (t // 8)
                    dve.wait_ge(ns["rot"], m + 1)
                    rotate([(n_k[m // 2][d:d + DH, 2 * (m % 2) + e, :], slice(DH * e, DH * e + DH))
                            for e in range(2) for d in (0, DH)], n_raw[:, t % 2, :], n_t2, ns["rope"])

                for t in range(U_NSA_KV):
                    evac(t)
                    if t < 4:
                        lower(t)
                    if t - 1 in (4, 5, 8, 9):
                        key(t - 1)
                V.memset(n_kc[:, :, :, :], 0.0)
                dve.wait_ge(ns["hTc"], 2)
                V.memset(n_bd[:, :, :, :], 0.0).then_inc(ns["p0"], 1)
                dve.wait_ge(s_used, START["nsa_q"] + 1)
                dve.wait_ge(ns["vT"], 3)
                V.tensor_tensor(n_raw[:, 0, :], bank[0][:, :], rstd[:, :], ALU.mult).then_inc(ns["evac"], 1)
                def query(e):
                    raw = n_raw[:, (e + 1) % 2, :]
                    dve.wait_ge(ns["rot"], 4 + e + 1)
                    if e:
                        dve.wait_ge(ns["rope"], 4 + e)
                    V.tensor_tensor(n_t1[:, :], raw, cos_t, ALU.mult)
                    own(V.tensor_tensor(n_t2[:, :], n_t2[:, :], sin_t, ALU.mult))
                    own(V.tensor_tensor(n_t1[:, :], n_t1[:, :], n_t2[:, :], ALU.add))
                    halves = (slice(0, DH), slice(DH, P))
                    V.tensor_copy(n_qp[halves[0], 2 * e, :], n_t1[halves[0], :])
                    own(V.tensor_copy(n_qp[halves[1], 2 * e + 1, :], n_t1[halves[1], :]))
                    for par, r in enumerate(halves):
                        ins = V.tensor_tensor(n_qp[halves[1 - par], 2 * e + par, :], n_t1[r, :],
                                              n_qp[r, 2 * e + par, :].bitcast(F32), ALU.subtract)
                    ins.then_inc(ns["rope"], 1)

                def key_low(g):
                    for c in range(2):
                        dve.wait_ge(ns["kh"], 2 * g + c + 1)
                        V.tensor_tensor(n_kl[c][:, g, :], n_k[c][:, g, :], n_kh[c][g][:, :].bitcast(F32), ALU.subtract)\
                            .then_inc(ns["kl"], 1)

                mask = C("cmp_mask").rearrange("p (c n) -> p c n", c=TT)[:, :, None, :].broadcast_to([P, TT, 4, NC_PAD])
                valid = C("cmp_valid")[:, :, None].broadcast_to([P, TT, 4])

                def cmp_scores(rd):
                    s = n_sc[rd % 2][:, :].rearrange("p (c h n) -> p c h n", c=TT, h=4)
                    b = bank[6 + rd % 2][:, :].rearrange("p (c h n) -> p c h n", c=TT, h=4)
                    dve.wait_ge(ns["cs"], 2 * rd + 2)
                    if rd >= 2:
                        dve.wait_ge(ns["pT"], rd - 1)
                    V.tensor_tensor(s, b, mask, ALU.add).then_inc(ns["csub"], 1)
                    dve.wait_ge(ns["csub"], rd + 1)
                    s3 = n_sc[rd % 2][:, :].rearrange("p (m n) -> p m n", n=NC_PAD)
                    own(V.tensor_reduce(n_cst[:, 0, :], s3, AX_X, ALU.max))
                    V.tensor_tensor(s3, s3, n_cst[:, 0, :, None].broadcast_to([P, 16, NC_PAD]), ALU.subtract)\
                        .then_inc(ns["cmax"], 1)

                def cmp_weights(rd):
                    s3 = n_sc[rd % 2][:, :].rearrange("p (m n) -> p m n", n=NC_PAD)
                    dve.wait_ge(ns["ce"], rd + 1)
                    own(V.tensor_reduce(n_cst[:, 1, :], s3, AX_X, ALU.add))
                    own(V.reciprocal(n_cst[:, 2, :], n_cst[:, 1, :]))
                    r4 = n_cst[:, 2, :].rearrange("p (c h) -> p c h", c=TT)
                    own(V.tensor_tensor(r4, r4, n_gate[:, :, 4 * rd:4 * rd + 4], ALU.mult))
                    own(V.tensor_tensor(r4, r4, valid, ALU.mult))
                    V.tensor_tensor(s3, s3, n_cst[:, 2, :, None].broadcast_to([P, 16, NC_PAD]), ALU.mult).then_inc(ns["p"], 1)

                for e in range(8):
                    dve.wait_ge(s_used, START["nsa_q"] + 1 + e + 1)
                    if e == 1:
                        dve.wait_ge(ns["gT"], 1)
                    if e >= 2:
                        dve.wait_ge(ns["cs"], e - 1)
                        dve.wait_ge(ns["rope"], 4 + e - 1)
                    V.scalar_tensor_tensor(n_raw[:, (e + 1) % 2, :], bank[(1 + e) % 4][:, :], QSCALE, rstd[:, :], ALU.mult,
                                           ALU.mult).then_inc(ns["evac"], 1)
                    if 1 <= e <= 6:
                        query(e - 1)
                    if e >= 2:
                        dve.wait_ge(ns["gate"], 1)
                        if e % 2 == 0:
                            cmp_scores(e // 2 - 1)
                        elif e < 7:
                            cmp_weights(e // 2 - 1)
                key_low(0)
                cmp_scores(3)

                jobs = NSA_HEADS * TT * 2
                for q in range(jobs + 10):
                    if q == 1:
                        cmp_weights(2)
                    if q == 4:
                        cmp_weights(3)
                    if q == 2:
                        query(6)
                    if q == 8:
                        query(7)
                    if q in (16, 20, 60):
                        key_low(1 + (16, 20, 60).index(q))
                    if q < jobs:
                        S = (query_tile(q) + 1) * P
                        dve.wait_ge(ns["s"], q + 1)
                        V.tensor_reduce(n_st[:, 0, q:q + 1], bank[(4, 6, 7, 5)[q % 4]][:, 0:S], AX_X, ALU.max, negate=True)\
                            .then_inc(ns["mx"], 1)
                    if 1 <= q <= jobs:
                        m = q - 1
                        e, i, par, c = m // 16, query_tile(m), m // 2 % 2, m % 2
                        dve.wait_ge(ns["exp"], m + 1)
                        w = n_P[m % 6][:, 0:(i + 1) * P]
                        col = 16 * (c + 1) + 2 * e + par
                        own(V.reciprocal(n_st[:, 1, m:m + 1], n_st[:, 1, m:m + 1]))
                        V.tensor_scalar(w, w, n_st[:, 1, m:m + 1], n_gate[:, i, col:col + 1], ALU.mult, ALU.mult)\
                            .then_inc(ns["w"], 1)
                    if q >= 25 and (q - 25) % 16 == 0:
                        e = (q - 25) // 16
                        dve.wait_ge(ns["oh"], e + 1)
                        V.tensor_tensor(n_ol[:, e, :], bank[0][:, :], n_oh[:, e, :].bitcast(F32), ALU.subtract)\
                            .then_inc(ns["o"], 1)
                projected(3, "nsa_o", (4, 5, 6, 7))

            def hybrid(ly):
                n0 = HYB_N[ly]
                u0 = START[f"hyb{ly}"]
                lam_init = LAM_INIT[ly]
                lam_in = PAR("lam")[:, 4 * ly:4 * ly + 4]
                V.tensor_tensor(h_lam[:, 0:2], lam_in[:, 0:4:2], lam_in[:, 1:4:2], ALU.mult).then_inc(hs["lp"], 1)
                lo_ = COLS["subln"][0] + ly
                V.tensor_scalar(h_sub[:, ly:ly + 1], par_sb[:, lo_:lo_ + 1], 1.0 - lam_init, None, ALU.mult)
                dve.wait_ge(s_rstd, n0 + 1)

                def rot(t):
                    dve.wait_ge(hs["rot"], 8 * ly + t + 1)
                    if t:
                        dve.wait_ge(hs["rope"], 8 * ly + t)
                    halves = (slice(0, DH), slice(DH, P))
                    dst = [(h_dq[:, t, :], slice(0, P))] if t < 4 else [(h_dk[r, t - 4, c, :], r) for c, r in enumerate(halves)]
                    rotate(dst, h_raw[:, t % 2, :], h_t2, hs["rope"])

                def evac(t):
                    dve.wait_ge(s_used, u0 + t + 1)
                    b = bank[t % 4 if t < 12 else fill_bank(t)]
                    if 16 <= t < 20:
                        for c in range(2):
                            r = slice(DH * c, DH * (c + 1))
                            ins = V.tensor_tensor(h_sk[r, 2 * (t - 16) + c, :], b[r, :], rstd[r, :], ALU.mult)
                        ins.then_inc(hs["evac"], 1)
                        return
                    if t < 12 or 20 <= t < 24:
                        dst = h_raw[:, t % 2, :]
                        if 2 <= t < 10:
                            dve.wait_ge(hs["rope"], 8 * ly + t - 1)
                        if t in (10, 11):
                            dve.wait_ge(hs["vT"], 8 * ly + t - 9)
                        if t >= 20:
                            dve.wait_ge(hs["vT"], 8 * ly + t - 17)
                    elif t < 16:
                        dst = h_sq[:, t - 12, :]
                    else:
                        dst = h_gate[:, t - 24, :]
                    if t < 4 or 12 <= t < 16:
                        ins = V.scalar_tensor_tensor(dst, b[:, :], QSCALE, rstd[:, :], ALU.mult, ALU.mult)
                    else:
                        ins = V.tensor_tensor(dst, b[:, :], rstd[:, :], ALU.mult)
                    ins.then_inc(hs["evac"], 1)

                for t in range(12):
                    evac(t)
                    if t in (1, 2, 9, 10):
                        c = t % 2
                        other = slice(DH * (1 - c), DH * (2 - c))
                        V.memset(h_dk[other, :, c, :] if t < 4 else h_sk[other, c:SB_HEADS:2, :], 0.0)
                    if 1 <= t <= 8:
                        rot(t - 1)
                    if t == 9:
                        dve.wait_ge(hs["le"], ly + 1)
                        own(V.tensor_tensor(h_lam[:, 4:5], h_lam[:, 3:4], h_lam[:, 2:3], ALU.subtract))
                        V.tensor_scalar(h_lam[:, 5:6], h_lam[:, 4:5], -lam_init, None, ALU.add).then_inc(hs["lam"], 1)

                units = DIFF_HEADS * TT
                q0 = units * ly

                def combine(m):
                    S = (m % TT + 1) * P
                    dve.wait_ge(hs["exp"], 2 * (q0 + m) + 2)
                    if m >= 2:
                        dve.wait_ge(hs["t"], q0 + m - 1)
                    st = h_st[:, 2, 2 * m:2 * m + 2]
                    own(V.reciprocal(st, h_st[:, 1, 2 * m:2 * m + 2]))
                    own(V.tensor_scalar(h_st[:, 3, 2 * m:2 * m + 1], h_st[:, 2, 2 * m + 1:2 * m + 2], h_lam[:, 5:6], None,
                                        ALU.mult))
                    w = h_W[:, m % 2, 0:S]
                    own(V.tensor_scalar(w, h_P[:, 0, 0:S], h_st[:, 2, 2 * m:2 * m + 1], None, ALU.mult))
                    V.scalar_tensor_tensor(w, h_P[:, 1, 0:S], h_st[:, 3, 2 * m:2 * m + 1], w, ALU.mult, ALU.add)\
                        .then_inc(hs["w"], 1)

                def d_out(h):
                    dve.wait_ge(hs["ors"], 4 * ly + h + 1)
                    V.scalar_tensor_tensor(h_od[:, h, :], bank[3][:, :], h_sub[:, ly:ly + 1], h_ors[:, :], ALU.mult, ALU.mult)\
                        .then_inc(hs["od"], 1)

                for n in range(units):
                    S = (n % TT + 1) * P
                    for c in range(2):
                        dve.wait_ge(hs["s"], 2 * (q0 + n) + c + 1)
                        V.tensor_reduce(h_st[:, 0, 2 * n + c:2 * n + c + 1], bank[4 + c][:, 0:S], AX_X,
                                        ALU.max, negate=True).then_inc(hs["mx"], 1)
                    combine(n)
                    if n in FILL:
                        evac(FILL[n])
                    if n >= 6 and (n - 6) % TT == 0:
                        d_out((n - 6) // TT)

                k0 = SB_HEADS * ly
                for h in range(SB_HEADS):
                    dve.wait_ge(hs["ln"], k0 + h + 1)
                    sp_ = h_sp[:, h % 2, :]
                    for at_, w, b in zip((0, 512, 1024), (512, 512, 256), SB_BANKS[h % 2]):
                        ins = V.scalar_tensor_tensor(sp_[:, at_:at_ + w], bank[b][:, 0:w], 0.0, sp_[:, at_:at_ + w],
                                                     ALU.max, ALU.add)
                    own(ins)
                    keep = C("sb_keep")[:, None, :].broadcast_to([P, 2, P])
                    d = sp_[:, 0:1024].rearrange("p (j t) -> p j t", j=2)[:, :, 0:P]
                    V.tensor_tensor(d, d, keep, ALU.mult)
                    d = sp_[:, 896:1152].rearrange("p (j t) -> p j t", j=2)
                    V.tensor_tensor(d, d, keep, ALU.mult).then_inc(hs["soft"], 1)
                    if h == 0:
                        dve.wait_ge(hs["pv"], 4 * ly + 4)
                    evac(24 + 2 * h)
                    if h >= 2:
                        dve.wait_ge(hs["spv"], 4 * ly + h // 2)
                    later = h_a[:, h % 2, 0:640]
                    dve.wait_ge(hs["soft"], k0 + h + 1)
                    V.tensor_copy(later[:, 0:128], sp_[:, 512:640])
                    V.tensor_copy(later[:, 384:512], sp_[:, 1024:1152])
                    own(V.tensor_tensor(later[:, 512:640], sp_[:, 1152:1280], sp_[:, 896:1024], ALU.add))
                    own(V.tensor_tensor(later[:, 128:384], sp_[:, 640:896], later[:, 384:640], ALU.add))
                    later_hi = h_later_hi[:, h % 2, 640:1280]
                    own(V.tensor_copy(later_hi, later))
                    V.tensor_tensor(h_later_lo[:, h % 2, 0:640], later, later_hi.bitcast(F32), ALU.subtract)
                    dve.wait_ge(hs["sphi"], k0 + h + 1)
                    V.tensor_tensor(h_sp_lo[:, h % 2, :], sp_, h_sp_hi[h // 4][:, :].bitcast(F32), ALU.subtract)\
                        .then_inc(hs["sp"], 1)
                    if h == 0:
                        d_out(DIFF_HEADS - 1)
                    evac(25 + 2 * h)

                for k in range(4):
                    dve.wait_ge(hs["odh"], 4 * ly + k + 1)
                    V.tensor_tensor(h_odl[:, k, :], h_od[:, k, :], h_odh[:, k, :].bitcast(F32), ALU.subtract)\
                        .then_inc(hs["odl"], 1)
                for a in range(3):
                    dve.wait_ge(hs["osh"], 4 * ly + a + 1)
                    V.tensor_tensor(h_osl[:, a, :], h_os[:, a, :], h_osh[:, a, :].bitcast(F32), ALU.subtract)\
                        .then_inc(hs["osl"], 1)

                u0 = START[f"merge{ly}"]

                def merged_lo(f):
                    dve.wait_ge(hs["mh"], 8 * ly + f + 1)
                    V.tensor_tensor(h_ml[:, f, :], h_m[:, f % 2, :], h_mh[:, f, :].bitcast(F32), ALU.subtract)\
                        .then_inc(hs["ml"], 1)

                for m in range(2 * KT):
                    f = m % KT
                    if m == 2:
                        dve.wait_ge(hs["osh"], 4 * ly + 4)
                        V.tensor_tensor(h_osl[:, 3, :], bank[2][:, :], h_osh[:, 3, :].bitcast(F32), ALU.subtract)\
                            .then_inc(hs["osl"], 1)
                    if m % 2 == 0:
                        dve.wait_ge(hs["mt"], 8 * ly + m // 2 + 1)
                    else:
                        dve.wait_ge(s_used, u0 + m // 2 + 1)
                    dve.wait_ge(hs["gate"], 16 * ly + m + 1)
                    b = bank[(4, 5, 0, 7)[m % 4]][:, :]
                    if m < KT:
                        V.tensor_tensor(h_mt[:, f, :], b, h_gate[:, f, :], ALU.mult).then_inc(hs["mevac"], 1)
                    else:
                        if f:
                            dve.wait_ge(hs["m"], 8 * ly + f)
                        V.tensor_tensor(h_m2[:, :], b, h_gate[:, m, :], ALU.mult).then_inc(hs["mevac"], 1)
                        dve.wait_ge(hs["mevac"], 16 * ly + m + 1)
                        if f >= 2:
                            dve.wait_ge(hs["ml"], 8 * ly + f - 1)
                        V.tensor_tensor(h_m[:, f % 2, :], h_m2[:, :], h_mt[:, f, :], ALU.add).then_inc(hs["m"], 1)
                        if f:
                            merged_lo(f - 1)
                merged_lo(7)
                projected(n0 + 1, f"out{ly}", (2, 4, 5, 7))

            dve.wait_ge(s_gain, 16)
            for k in range(KT):
                dve.wait_ge(s_xt, k + 1)
                V.tensor_copy(X[:, k, :], bank[k][:, :]).then_inc(s_x, 1)
                if k:
                    lo(0, k - 1)
            lo(0, KT - 1)
            gla()
            ffn(0, 1, "ffn0", 2)
            nsa()
            V.tensor_copy(negtri_r[:, :], negtri)
            V.tensor_copy(negones_r[:, :], negones)
            g4, g5 = (COLS["gain"][0] + GAIN[n] * KT for n in (MID, MID + 1))
            own(V.tensor_tensor(mid_gain[:, :], par_sb[:, g4:g4 + KT], par_sb[:, g5:g5 + KT], ALU.mult))
            ffn(1, 3, "ffn1", MID)
            for k in range(KT):
                dve.wait_ge(s_sq, 8 * 5 + k + 1)
                if k == 0:
                    V.tensor_copy(mid_ss[:, :], sq[:, 0, :]).then_inc(s_ss, 1)
                else:
                    dve.wait_ge(s_ss, 8 * 5 + k)
                    V.tensor_tensor(mid_ss[:, :], mid_ss[:, :], sq[:, k % 2, :], ALU.add).then_inc(s_ss, 1)
            dve.wait_ge(s_rstd, MID + 1)
            for k in range(KT):
                V.scalar_tensor_tensor(X[:, k, :], X[:, k, :], gain(GAIN[MID], k), rstd[:, :], ALU.mult, ALU.mult)\
                    .then_inc(s_x, 1)
                if k == 3:
                    dve.wait_ge(s_stat, 6)
                    own(V.tensor_tensor(mid_r[:, :], bank[5][:, :], rstd[:, :], ALU.mult))
                    V.tensor_tensor(mid_r[:, :], mid_r[:, :], rstd[:, :], ALU.mult).then_inc(s_mid, 1)
            dve.wait_ge(s_rstd, 6)
            own(V.tensor_tensor(rstd[:, :], rstd[:, :], mid_r[:, :], ALU.mult))
            hybrid(0)
            ffn(2, 6, "ffn2", 7)
            hybrid(1)
            ffn(3, 8, "ffn3", 9)
            dve.wait_ge(s_rstd, 10)
            dve.wait_ge(s_ygain, 16)
            for c in range(TT):
                for half in range(2):
                    dve.wait_ge(s_yt, 4 * half + c + 1)
                    cols = slice(half * T, (half + 1) * T)
                    V.scalar_tensor_tensor(y_tok[:, c, cols], bank[4 * half + c][:, :], rstd[:, 2 * c:2 * c + 1], y_gain[:, cols],
                                           ALU.mult, ALU.mult).then_inc(s_y, 1)


def _units(w, cols):
    w = np.ascontiguousarray(w[:, :cols])
    return w.reshape(KT, P, cols // P, P).transpose(2, 1, 0, 3)


def _row_units(w):
    return w.reshape(w.shape[0] // P, P, KT, P)


def _padded(w):
    return np.concatenate([w, np.zeros((w.shape[0], P - w.shape[1]), w.dtype)], axis=1)


def lay_out(a):
    def pairs(w):
        return np.stack([w[..., :FFN].reshape(*w.shape[:-1], FT, P), w[..., FFN:].reshape(*w.shape[:-1], FT, P)], axis=-2)\
            .reshape(*w.shape[:-1], 2 * FFN)

    def ffn(up, down):
        return [_units(pairs(up), 2 * FFN), _row_units(down)]

    def half_units(w):
        return w.reshape(4, P, 4, 2, P).transpose(2, 1, 3, 0, 4).reshape(4, P, KT, P)

    g = a["gla_w_in"][0]
    qk, kv, r0, a0 = 512, 1024, 2048, 3072
    low = np.concatenate([np.zeros((D, P - GLA_RANK), g.dtype), g[:, a0:]], axis=1)
    units = [_units(low, P), _units(g[:, :a0], a0), _units(a["gla_w_o"][0], D)]
    units += ffn(a["ffn_w_up"][0], a["ffn_w_down"][0])
    units += [_units(a["nsa_w_kv"], 1536)]
    for w in (a["cmp_k_w1"], a["cmp_v_w1"]):
        units.append(w.reshape(4, 4, P, CMP_HIDDEN).transpose(0, 2, 1, 3).reshape(4, P, KT, P))
    w = a["nsa_w_in"][0]
    units += [_units(_padded(w[:, D:]), P), _units(w, D), _units(a["nsa_w_o"][0], D)]
    units += ffn(a["ffn_w_up"][1], a["ffn_w_down"][1])
    for ly in range(2):
        units.append(_units(a["w_in_2"][ly], U_HYB * P))
        units += [half_units(a["w_o_diff_2"][ly]), half_units(a["w_o_sb_2"][ly])]
        units.append(_units(a["w_out_2"][ly], D))
        units += ffn(a["w_ffn_in_2"][ly], a["w_ffn_out_2"][ly])
    stream = np.concatenate(units)
    assert stream.shape == (UNITS, P, KT, P), stream.shape

    params = np.zeros((P, N_COLS), np.float32)

    def put(name, x):
        lo, hi = COLS[name]
        params[:, lo:hi] = x.reshape(P, hi - lo)

    def cols(v):
        return np.moveaxis(v.reshape(*v.shape[:-1], -1, P), -1, 0)

    gains = np.stack([a["norm_mix"][0], a["norm_ffn"][0], a["kv_norm"], a["norm_mix"][1], a["norm_ffn"][1], a["norm_final"],
                      a["norm_attn_2"][0], a["norm_ffn_2"][0], a["norm_attn_2"][1], a["norm_ffn_2"][1],
                      a["norm_final_2"]])
    put("gain", cols(gains))
    put("conv_w", cols(pairs(a["ffn_conv_w"])))
    put("conv_b", cols(pairs(a["ffn_conv_b"])))
    put("b_gate", cols(a["b_gate_2"]))
    put("subln", cols(a["diff_subln_2"]))
    put("gla_norm", cols(a["gla_norm"][0]))
    up = np.zeros((P, 512), np.float32)
    up[0] = a["gla_b_alpha"][0]
    up[P - GLA_RANK:] = a["gla_w_alpha_up"][0]
    put("w_alpha", up)
    pe = np.stack([a["cmp_pe_k"], a["cmp_pe_v"]])
    pe = pe.reshape(2, 16, P).transpose(2, 0, 1)
    put("pe", pe)
    w2 = a["cmp_k_w2"].reshape(2, P, DH).transpose(1, 0, 2)
    put("w2k", np.concatenate([w2, w2], axis=-1))
    put("w2v", a["cmp_v_w2"].reshape(2, P, DH).transpose(1, 0, 2))
    lam = np.zeros((P, 8), np.float32)
    lam[:DH] = a["diff_lambda_2"].transpose(2, 0, 1).reshape(DH, 8)
    put("lam", lam)
    return stream, params


def arranged(a):
    stream, params = lay_out(a)
    tables, masks = constants()
    return {"x_dram": np.ascontiguousarray(a["x"]), "weights_dram": stream, "params_dram": params,
              "consts_dram": tables, "masks_dram": masks, "gain_out_dram": a["norm_final_2"].reshape(1, D)}


def kernel(**inputs):
    import concourse.bacc as _bacc
    from concourse.bass_utils import run_bass_kernel_spmd as _run

    arrays = arranged({n: np.asarray(v) for n, v in inputs.items()})
    nc = _bacc.Bacc("TRN2", target_bir_lowering=False, num_devices=1)
    args = [nc.dram_tensor(n, v.shape, mybir.dt.from_np(v.dtype), kind="ExternalInput").ap() for n, v in arrays.items()]
    args.append(nc.dram_tensor("out_dram", (1, T, D), F32, kind="ExternalOutput").ap())
    build(nc, *args)
    r = _run(nc, [arrays], core_ids=[0])
    return r.results[0]["out_dram"]
```
